# Optimizing a Trainium2 kernel written in Bass

```python
import jax, jax.numpy as jnp
from jax import lax
import numpy as np

D_MODEL = 1024
BATCH = 1
SEQ = 256
DEPTH = 1
DEC_BATCH = 8
DEC_SEQ = 4
PAST_LEN = 2048
PAGE_SIZE = 128

D_MIX = D_MODEL
W_RWKV = D_MIX // 2
N_R = 64
H_R = W_RWKV // N_R
LORA_W = D_MODEL // 16
LORA_A = D_MODEL // 16
LORA_G = D_MODEL // 8
R_PROJ = 3 * W_RWKV + LORA_W + LORA_A + LORA_G
GN_EPS = 64e-5
W_GDN = D_MIX - W_RWKV
D_G = 128
H_G = W_GDN // D_G
GDN_CONV_DIM = 3 * W_GDN
CONV_W = 4
G_PROJ = GDN_CONV_DIM + W_GDN + 2 * H_G
P_TOT = R_PROJ + G_PROJ
GDN_CHUNK = 64
N_MEM = 256
H_X = 4
D_X = D_MODEL // H_X
N_EXPERTS = 32
TOP_K = 4
D_FF = D_MODEL
SWIGLU_LIMIT = 7.0
SWIGLU_ALPHA = 1.702
MOE_BLOCK = 128
RMS_EPS = 1e-6

kernel_name = 'hymba_rwkv7_gdn_memx_moe_step'

F32 = jnp.float32

def rmsnorm(x, g, eps=RMS_EPS):
    xf = x.astype(F32)
    y = xf * lax.rsqrt(jnp.mean(xf * xf, axis=-1, keepdims=True) + eps)
    return (y * g.astype(F32)).astype(x.dtype)

def l2norm(x, eps=1e-6):
    xf = x.astype(F32)
    return xf * lax.rsqrt(jnp.sum(xf * xf, axis=-1, keepdims=True) + eps)

def rwkv7_recurrence(r, wl, k, v, kk, a, s0):
    def step(s, inp):
        r_t, wl_t, k_t, v_t, kk_t, a_t = inp
        sa = jnp.einsum('bhvk,bhk->bhv', s, -kk_t)
        s = (s * jnp.exp(wl_t)[:, :, None, :]
             + sa[..., None] * (kk_t * a_t)[:, :, None, :]
             + v_t[..., None] * k_t[:, :, None, :])
        return s, jnp.einsum('bhvk,bhk->bhv', s, r_t)
    xs = tuple(jnp.moveaxis(t, 1, 0) for t in (r, wl, k, v, kk, a))
    s, ys = lax.scan(step, s0, xs)
    return jnp.moveaxis(ys, 0, 1), s

def gated_delta_chunked(q, k, v, g, beta, s0, chunk):
    b, t, h, _ = q.shape
    dv = v.shape[-1]
    pad = (-t) % chunk
    n = (t + pad) // chunk

    def blocks(x):
        x = jnp.pad(x, [(0, 0), (0, pad)] + [(0, 0)] * (x.ndim - 2))
        x = x.reshape((b, n, chunk) + x.shape[2:])
        return jnp.moveaxis(x, 3, 1)

    q, k, v, g, beta = (blocks(x) for x in (q, k, v, g, beta))
    gc = jnp.cumsum(g, axis=-1)
    tril = jnp.tril(jnp.ones((chunk, chunk), bool))
    strict = jnp.tril(jnp.ones((chunk, chunk), bool), -1)
    diff = gc[..., :, None] - gc[..., None, :]
    decay = jnp.where(tril, jnp.exp(jnp.where(tril, diff, 0.0)), 0.0)
    k_beta = k * beta[..., None]
    lmat = jnp.where(strict, jnp.einsum('bhnik,bhnjk->bhnij', k_beta, k) * decay, 0.0)
    eye = jnp.eye(chunk, dtype=q.dtype)
    tmat = lax.linalg.triangular_solve(eye + lmat, jnp.broadcast_to(eye, lmat.shape),
                                       left_side=True, lower=True, unit_diagonal=True)
    u = jnp.einsum('bhnij,bhnjv->bhniv', tmat, v * beta[..., None])
    w = jnp.einsum('bhnij,bhnjk->bhnik', tmat, k_beta * jnp.exp(gc)[..., None])
    attn = jnp.where(tril, jnp.einsum('bhnik,bhnjk->bhnij', q, k) * decay, 0.0)
    g_last = gc[..., -1]
    k_tail = k * jnp.exp(g_last[..., None] - gc)[..., None]
    q_dec = q * jnp.exp(gc)[..., None]

    def step(s, inp):
        u_i, w_i, qd_i, a_i, kt_i, gl_i = inp
        v_new = u_i - jnp.einsum('bhck,bhkv->bhcv', w_i, s)
        o = jnp.einsum('bhck,bhkv->bhcv', qd_i, s) + jnp.einsum('bhcd,bhdv->bhcv', a_i, v_new)
        s = s * jnp.exp(gl_i)[..., None, None] + jnp.einsum('bhck,bhcv->bhkv', kt_i, v_new)
        return s, o

    xs = tuple(jnp.moveaxis(x, 2, 0) for x in (u, w, q_dec, attn, k_tail, g_last))
    s, o = lax.scan(step, s0, xs)
    o = jnp.transpose(o, (1, 0, 3, 2, 4)).reshape(b, n * chunk, h, dv)[:, :t]
    return o, s

def rwkv7_group(pr, shift_prev, s0, lp):
    b, t, _ = pr.shape
    prev = jnp.concatenate([shift_prev[:, None, :].astype(pr.dtype), pr[:, :-1]], axis=1)
    xm = (pr + (prev - pr) * lp['mu_shift']).astype(F32)
    r = xm[..., :W_RWKV]
    k = xm[..., W_RWKV:2 * W_RWKV]
    v = xm[..., 2 * W_RWKV:3 * W_RWKV]
    o = 3 * W_RWKV
    w_lo = xm[..., o:o + LORA_W]
    a_lo = xm[..., o + LORA_W:o + LORA_W + LORA_A]
    g_lo = xm[..., o + LORA_W + LORA_A:]
    logw = -jax.nn.softplus(-(lp['w0'] + jnp.tanh(w_lo) @ lp['w2_decay'])) - 0.5
    wl = -jnp.exp(logw)
    a = jax.nn.sigmoid(lp['a0'] + a_lo @ lp['a2_iclr'])
    g = jax.nn.sigmoid(g_lo) @ lp['g2_gate']
    hs = lambda z: z.reshape(b, t, H_R, N_R)
    kk = l2norm(hs(k * lp['k_k']))
    k = k * (1.0 + (a - 1.0) * lp['k_a'])
    r_h, k_h, v_h = hs(r), hs(k), hs(v)
    y, s = rwkv7_recurrence(r_h, hs(wl), k_h, v_h, kk, hs(a), s0.astype(F32))
    mean = jnp.mean(y, axis=-1, keepdims=True)
    var = jnp.mean(jnp.square(y - mean), axis=-1, keepdims=True)
    yn = ((y - mean) * lax.rsqrt(var + GN_EPS)).reshape(b, t, W_RWKV) * lp['lnx_w'] + lp['lnx_b']
    bonus = jnp.sum(r_h * k_h * lp['r_k'], axis=-1, keepdims=True) * v_h
    out = (yn + bonus.reshape(b, t, W_RWKV)) * g
    return out.astype(pr.dtype), pr[:, -1], s

def gdn_group(pg, conv_buf, s0, lp):
    b, t, _ = pg.shape
    raw = pg[..., :GDN_CONV_DIM]
    z = pg[..., GDN_CONV_DIM:GDN_CONV_DIM + W_GDN].astype(F32)
    bb = pg[..., GDN_CONV_DIM + W_GDN:GDN_CONV_DIM + W_GDN + H_G].astype(F32)
    aa = pg[..., GDN_CONV_DIM + W_GDN + H_G:].astype(F32)
    xp = jnp.concatenate([conv_buf.astype(raw.dtype), raw], axis=1)
    cw = lp['conv_w']
    conv = xp[:, 0:t] * cw[0]
    for j in range(1, CONV_W):
        conv = conv + xp[:, j:j + t] * cw[j]
    qkv = jax.nn.silu(conv.astype(F32))
    hs = lambda zz: zz.reshape(b, t, H_G, D_G)
    q = l2norm(hs(qkv[..., :W_GDN])) * (D_G ** -0.5)
    k = l2norm(hs(qkv[..., W_GDN:2 * W_GDN]))
    v = hs(qkv[..., 2 * W_GDN:])
    beta = jax.nn.sigmoid(bb)
    g = -jnp.exp(lp['a_log'].astype(F32)) * jax.nn.softplus(aa + lp['dt_bias'])
    o, s = gated_delta_chunked(q, k, v, g, beta, s0.astype(F32), min(GDN_CHUNK, t))
    o = o * lax.rsqrt(jnp.mean(o * o, axis=-1, keepdims=True) + RMS_EPS) * lp['gdn_norm_w']
    o = o * jax.nn.silu(hs(z))
    return o.reshape(b, t, W_GDN).astype(pg.dtype), xp[:, -(CONV_W - 1):], s

def parallel_mixer(h, shift_prev, s_r, conv_buf, s_g, lp):
    proj = h @ lp['w_in']
    y_r, shift_new, s_r_new = rwkv7_group(proj[..., :R_PROJ], shift_prev, s_r, lp)
    y_g, conv_new, s_g_new = gdn_group(proj[..., R_PROJ:], conv_buf, s_g, lp)
    y = jnp.concatenate([y_r, y_g], axis=-1) @ lp['w_out']
    return y, shift_new, s_r_new, conv_new, s_g_new

def memory_kv(mem, g, wk, wv):
    b, m, _ = mem.shape
    hm = rmsnorm(mem, g)
    return (hm @ wk).reshape(b, m, H_X, D_X), (hm @ wv).reshape(b, m, H_X, D_X)

def memory_cross_attention(h, mk, mv, wq, wo):
    b, t, _ = h.shape
    q = (h @ wq).reshape(b, t, H_X, D_X)
    s = jnp.einsum('bthd,bmhd->bhtm', q, mk.astype(q.dtype)).astype(F32) * (D_X ** -0.5)
    p = jax.nn.softmax(s, axis=-1).astype(h.dtype)
    o = jnp.einsum('bhtm,bmhd->bthd', p, mv.astype(h.dtype)).reshape(b, t, H_X * D_X)
    return o @ wo

def routed_ffn(h, lp):
    n_tok, d = h.shape
    logits = h.astype(F32) @ lp['router_w'].astype(F32) + lp['router_b'].astype(F32)
    top_v, top_i = lax.top_k(logits, TOP_K)
    gates = jax.nn.softmax(top_v, axis=-1)
    n_assign = n_tok * TOP_K
    flat_e = top_i.reshape(n_assign)
    flat_tok = jnp.arange(n_assign, dtype=jnp.int32) // TOP_K
    order = jnp.argsort(flat_e)
    sorted_e = flat_e[order]
    counts = jnp.bincount(flat_e, length=N_EXPERTS)
    padded = (counts + MOE_BLOCK - 1) // MOE_BLOCK * MOE_BLOCK
    starts = jnp.cumsum(counts) - counts
    pends = jnp.cumsum(padded)
    pstarts = pends - padded
    dest = pstarts[sorted_e] + jnp.arange(n_assign, dtype=jnp.int32) - starts[sorted_e]
    n_blocks = -(-(n_assign + N_EXPERTS * (MOE_BLOCK - 1)) // MOE_BLOCK)
    m_rows = n_blocks * MOE_BLOCK
    tok_sorted = flat_tok[order]
    row_tok = jnp.full((m_rows,), n_tok, jnp.int32).at[dest].set(tok_sorted)
    block_e = jnp.clip(jnp.searchsorted(pends, jnp.arange(n_blocks, dtype=jnp.int32) * MOE_BLOCK,
                                        side='right'), 0, N_EXPERTS - 1)
    h_pad = jnp.concatenate([h, jnp.zeros((1, d), h.dtype)], axis=0)
    xb = h_pad[row_tok].reshape(n_blocks, MOE_BLOCK, d)
    w1, b1, w2, b2 = lp['w1_e'], lp['b1_e'], lp['w2_e'], lp['b2_e']

    def expert_block(args):
        xe, e = args
        hc = xe @ w1[e] + b1[e]
        hg = jnp.minimum(hc[:, :D_FF], SWIGLU_LIMIT)
        hl = jnp.clip(hc[:, D_FF:], -SWIGLU_LIMIT, SWIGLU_LIMIT)
        act = hg * jax.nn.sigmoid(SWIGLU_ALPHA * hg) * (hl + 1.0)
        return act @ w2[e] + b2[e]

    yb = lax.map(expert_block, (xb, block_e)).reshape(m_rows, d)
    contrib = yb[dest] * gates.reshape(n_assign)[order][:, None].astype(yb.dtype)
    return jax.ops.segment_sum(contrib, tok_sorted, num_segments=n_tok).astype(h.dtype)

def decoder_layer(x, mk, mv, shift_prev, s_r, conv_buf, s_g, lp):
    y, shift_new, s_r_new, conv_new, s_g_new = parallel_mixer(
        rmsnorm(x, lp['norm_mix']), shift_prev, s_r, conv_buf, s_g, lp)
    x = x + y
    x = x + memory_cross_attention(rmsnorm(x, lp['norm_cross']), mk, mv, lp['wq_x'], lp['wo_x'])
    b, t, d = x.shape
    x = x + routed_ffn(rmsnorm(x, lp['norm_ffn']).reshape(b * t, d), lp).reshape(b, t, d)
    return x, shift_new, s_r_new, conv_new, s_g_new

def setup_inputs(seed: int = 0) -> dict:
    key = jax.random.key(seed)
    ks = iter(jax.random.split(key, 64))
    nrm = lambda shape, scale: scale * jax.random.normal(next(ks), shape, F32)
    uni = lambda shape, lo, hi: jax.random.uniform(next(ks), shape, F32, lo, hi)
    L = DEPTH
    dt = jnp.exp(uni((L, H_G), float(np.log(1e-3)), float(np.log(1e-1))))
    return {
        'x_prompt': nrm((BATCH, SEQ, D_MODEL), 1.0),
        'x_sample': nrm((DEC_BATCH, DEC_SEQ, D_MODEL), 1.0),
        'mem_prompt': nrm((BATCH, N_MEM, D_MODEL), 1.0),
        'state_rwkv': nrm((L, DEC_BATCH, H_R, N_R, N_R), 0.5),
        'state_rwkv_shift': nrm((L, DEC_BATCH, R_PROJ), 1.0),
        'state_gdn': nrm((L, DEC_BATCH, H_G, D_G, D_G), 0.1),
        'state_gdn_conv': nrm((L, DEC_BATCH, CONV_W - 1, GDN_CONV_DIM), 1.0),
        'cache_mem_k': nrm((L, DEC_BATCH, N_MEM, H_X, D_X), 1.0),
        'cache_mem_v': nrm((L, DEC_BATCH, N_MEM, H_X, D_X), 1.0),
        'norm_mix': 1.0 + nrm((L, D_MODEL), 0.02),
        'w_in': nrm((L, D_MODEL, P_TOT), D_MODEL ** -0.5),
        'mu_shift': uni((L, R_PROJ), 0.0, 1.0),
        'w0': uni((L, W_RWKV), -6.0, -0.5),
        'w2_decay': nrm((L, LORA_W, W_RWKV), 0.1),
        'a0': nrm((L, W_RWKV), 0.5),
        'a2_iclr': nrm((L, LORA_A, W_RWKV), 0.1),
        'g2_gate': nrm((L, LORA_G, W_RWKV), LORA_G ** -0.5),
        'k_k': 0.85 + nrm((L, W_RWKV), 0.05),
        'k_a': 1.0 + nrm((L, W_RWKV), 0.05),
        'r_k': nrm((L, H_R, N_R), 0.1),
        'lnx_w': 1.0 + nrm((L, W_RWKV), 0.02),
        'lnx_b': nrm((L, W_RWKV), 0.02),
        'conv_w': nrm((L, CONV_W, GDN_CONV_DIM), CONV_W ** -0.5),
        'a_log': jnp.log(uni((L, H_G), 1.0, 16.0)),
        'dt_bias': dt + jnp.log(-jnp.expm1(-dt)),
        'gdn_norm_w': 1.0 + nrm((L, D_G), 0.02),
        'w_out': nrm((L, D_MIX, D_MODEL), D_MIX ** -0.5),
        'norm_cross': 1.0 + nrm((L, D_MODEL), 0.02),
        'norm_mem': 1.0 + nrm((L, D_MODEL), 0.02),
        'wq_x': nrm((L, D_MODEL, D_MODEL), D_MODEL ** -0.5),
        'wk_x': nrm((L, D_MODEL, D_MODEL), D_MODEL ** -0.5),
        'wv_x': nrm((L, D_MODEL, D_MODEL), D_MODEL ** -0.5),
        'wo_x': nrm((L, D_MODEL, D_MODEL), D_MODEL ** -0.5),
        'norm_ffn': 1.0 + nrm((L, D_MODEL), 0.02),
        'router_w': nrm((L, D_MODEL, N_EXPERTS), D_MODEL ** -0.5),
        'router_b': nrm((L, N_EXPERTS), 0.01),
        'w1_e': nrm((L, N_EXPERTS, D_MODEL, 2 * D_FF), D_MODEL ** -0.5),
        'b1_e': nrm((L, N_EXPERTS, 2 * D_FF), 0.01),
        'w2_e': nrm((L, N_EXPERTS, D_FF, D_MODEL), D_FF ** -0.5),
        'b2_e': nrm((L, N_EXPERTS, D_MODEL), 0.01),
        'final_norm': 1.0 + nrm((D_MODEL,), 0.02),
    }

def reference(x_prompt, x_sample, mem_prompt, state_rwkv, state_rwkv_shift, state_gdn, state_gdn_conv,
              cache_mem_k, cache_mem_v, norm_mix, w_in, mu_shift, w0, w2_decay, a0, a2_iclr, g2_gate,
              k_k, k_a, r_k, lnx_w, lnx_b, conv_w, a_log, dt_bias, gdn_norm_w, w_out,
              norm_cross, norm_mem, wq_x, wk_x, wv_x, wo_x,
              norm_ffn, router_w, router_b, w1_e, b1_e, w2_e, b2_e, final_norm):
    xp, xs = x_prompt, x_sample
    bp = x_prompt.shape[0]
    dt = x_prompt.dtype
    p_sr, p_sh, p_sg, p_cb, p_mk, p_mv = [], [], [], [], [], []
    s_sr, s_sh, s_sg, s_cb = [], [], [], []
    for l in range(DEPTH):
        lp = {
            'norm_mix': norm_mix[l], 'w_in': w_in[l], 'mu_shift': mu_shift[l], 'w0': w0[l],
            'w2_decay': w2_decay[l], 'a0': a0[l], 'a2_iclr': a2_iclr[l], 'g2_gate': g2_gate[l],
            'k_k': k_k[l], 'k_a': k_a[l], 'r_k': r_k[l], 'lnx_w': lnx_w[l], 'lnx_b': lnx_b[l],
            'conv_w': conv_w[l], 'a_log': a_log[l], 'dt_bias': dt_bias[l], 'gdn_norm_w': gdn_norm_w[l],
            'w_out': w_out[l], 'norm_cross': norm_cross[l], 'wq_x': wq_x[l], 'wo_x': wo_x[l],
            'norm_ffn': norm_ffn[l], 'router_w': router_w[l], 'router_b': router_b[l],
            'w1_e': w1_e[l], 'b1_e': b1_e[l], 'w2_e': w2_e[l], 'b2_e': b2_e[l],
        }
        mk, mv = memory_kv(mem_prompt, norm_mem[l], wk_x[l], wv_x[l])
        xp, sh, sr, cb, sg = decoder_layer(
            xp, mk, mv,
            jnp.zeros((bp, R_PROJ), dt), jnp.zeros((bp, H_R, N_R, N_R), F32),
            jnp.zeros((bp, CONV_W - 1, GDN_CONV_DIM), dt), jnp.zeros((bp, H_G, D_G, D_G), F32), lp)
        p_sr.append(sr.astype(dt)); p_sh.append(sh.astype(dt)); p_sg.append(sg.astype(dt))
        p_cb.append(cb.astype(dt)); p_mk.append(mk.astype(dt)); p_mv.append(mv.astype(dt))
        xs, sh, sr, cb, sg = decoder_layer(
            xs, cache_mem_k[l], cache_mem_v[l], state_rwkv_shift[l], state_rwkv[l],
            state_gdn_conv[l], state_gdn[l], lp)
        s_sr.append(sr.astype(dt)); s_sh.append(sh.astype(dt)); s_sg.append(sg.astype(dt))
        s_cb.append(cb.astype(dt))
    y_prompt = rmsnorm(xp, final_norm)
    y_sample = rmsnorm(xs, final_norm)
    return (y_prompt, y_sample,
            jnp.stack(p_sr), jnp.stack(p_sh), jnp.stack(p_sg), jnp.stack(p_cb), jnp.stack(p_mk), jnp.stack(p_mv),
            jnp.stack(s_sr), jnp.stack(s_sh), jnp.stack(s_sg), jnp.stack(s_cb))


_drawn_inputs = setup_inputs


def setup_inputs(seed=0):
    import zlib

    import numpy as np

    out = dict(_drawn_inputs(seed))
    spreads = {}
    factors = {'lnx_w': 2.687,
     'norm_cross': 3.996,
     'norm_mem': 2.737,
     'b1_e': 8.0,
     'b2_e': 8.0,
     'gdn_norm_w': 2.668,
     'lnx_b': 3.414,
     'router_b': 3.689}
    for name, (base, spread) in spreads.items():
        noise = np.random.default_rng([zlib.crc32(name.encode()), seed]).standard_normal(out[name].shape)
        drawn = base * np.exp(spread * noise) if base else spread * noise
        out[name] = __import__('jax').numpy.asarray(drawn.astype(out[name].dtype))
    for name, factor in factors.items():
        out[name] = (out[name] * factor).astype(out[name].dtype)
    return out
```

```python
from contextlib import ExitStack

import concourse.bass as bass
from concourse import mybir

F32 = mybir.dt.float32
I32 = mybir.dt.int32
ALU = mybir.AluOpType
ACT = mybir.ActivationFunctionType
AXX = mybir.AxisListType.X

P = 128
D = 1024
KC = D // P
TP, NB, TS = 256, 8, 4
NS = NB * TS
T = TP + NS
TILES = [(0, P), (P, P), (TP, NS)]
HR, NR = 8, 64
HG, DG = 4, 128
PAIRS = HR * NR // P
R_PROJ = 3 * HR * NR + 256
R_TILES = R_PROJ // P
C_TILES = 3 * HG
CONV = 3 * HG * DG
CW = 4
Z0 = R_TILES + C_TILES
P_TOT = R_PROJ + CONV + HG * DG + 2 * HG
CR = 64
NCR = TP // CR
RW = 1 + TP + NB * (1 + TS)
GW = CW - 1 + TP + NB * (CW - 1 + TS)
NM = 256
HX, DX = 4, 256
NE, TOPK = 32, 4
RMS_EPS = 1e-6
GN_EPS = 64e-5
LIMIT, ALPHA = 7.0, 1.702
EXP_M05 = 0.6065306597126334

V_MU, V_A0, V_KK, V_KA, V_RK, V_LW, V_LB, V_CW, V_GN = 0, 14, 18, 22, 26, 30, 34, 38, 86
V_ROWS = 87


class Count:

    def __init__(self, sem):
        self.sem, self.n = sem, 0

    def inc(self, ins):
        self.n += 1
        ins.then_inc(self.sem, 1)
        return self.n

    def step(self, eng, ins):
        self.inc(ins)
        eng.wait_ge(self.sem, self.n)


def semaphores(nc, st, prefix):
    made = []

    def make(name):
        made.append(nc.alloc_semaphore(f"{prefix}_{name}"))
        return made[-1]

    def close():
        with nc.Block() as block:
            @block.gpsimd
            def _(pool):
                for s in made:
                    nc.gpsimd.sem_clear(s)
        for s in made:
            nc.release_semaphore(s)
    st.callback(close)
    return make


def build(nc, a, out):
    outer = ExitStack()
    with outer:
        def sb(st, name, shape, dt=F32):
            return st.enter_context(nc.sbuf_tensor(name, shape, dt))

        ps = outer.enter_context(nc.psum_tensor("ps", [P, 8, 512], F32))
        ident = sb(outer, "ident", [P, P])
        ones = sb(outer, "ones", [P, P])
        x = sb(outer, "x", [P, 3, D])
        g8 = sb(outer, "g8", [P, 4, KC])
        stat = sb(outer, "stat", [P, 3, 4])
        eps = sb(outer, "eps", [P, 2])

        def norm_stage(name, src, tiles, gcol, hT, h_tm):
            with ExitStack() as st:
                sem = semaphores(nc, st, name)
                sq_done, root_done, h_done = sem("squares"), sem("root"), sem("h")
                turned, moved = sem("turned"), sem("moved")
                chain = Count(sem("chain"))
                nt = len(tiles)
                width = tiles[-1][0] + tiles[-1][1]
                with nc.Block() as block:
                    @block.scalar
                    def _(act):
                        for i, (_, n) in enumerate(tiles):
                            nc.scalar.activation(h_tm[:n, i, :], src[:n, i, :], ACT.Square,
                                                 accum_out=stat[:n, i, 0:1]).then_inc(sq_done, 1)
                        for i, (_, n) in enumerate(tiles):
                            act.wait_ge(sq_done, i + 1)
                            nc.scalar.activation(stat[:n, i, 1:2], stat[:n, i, 0:1], ACT.Sqrt, bias=eps[:n, 0:1],
                                                 scale=1.0 / D).then_inc(root_done, 1)

                    @block.vector
                    def _(dve):
                        for i, (_, n) in enumerate(tiles):
                            dve.wait_ge(root_done, i + 1)
                            chain.step(dve, nc.vector.reciprocal(stat[:n, i, 2:3], stat[:n, i, 1:2]))
                            nc.vector.tensor_scalar(h_tm[:n, i, :], src[:n, i, :], stat[:n, i, 2:3], None,
                                                    ALU.mult).then_inc(h_done, 1)
                        for c in range(KC):
                            dve.wait_ge(turned, c + 1)
                            nc.vector.tensor_scalar(hT[:, c, 0:width], ps[:, c % 4, 0:width],
                                                    g8[:, gcol, c:c + 1], None, ALU.mult).then_inc(moved, 1)

                    @block.tensor
                    def _(pe):
                        pe.wait_ge(h_done, nt)
                        for c in range(KC):
                            if c >= 4:
                                pe.wait_ge(moved, c - 3)
                            for i, (t0, n) in enumerate(tiles):
                                ins = nc.tensor.transpose(ps[:, c % 4, t0:t0 + n], h_tm[:n, i, c::KC],
                                                          ident[:n, :n])
                            ins.then_inc(turned, 1)

        mixer(nc, a, out, outer, sb, ps, ident, ones, x, g8, stat, eps, norm_stage)
        attention(nc, a, out, outer, sb, ps, ident, ones, x, g8, stat, eps, norm_stage)
        experts(nc, a, out, outer, sb, ps, ident, ones, x, g8, stat, eps, norm_stage)


class Tiles:
    pass


def mixer(nc, a, out, outer, sb, ps, ident, ones, x, g8, stat, eps, norm_stage):
    st = ExitStack()
    with st:
        yT = sb(st, "yT", [P, KC, T])
        lvl = sb(st, "lvl", [P, 7, P])
        tri = sb(st, "tri", [P, P])
        tr64 = sb(st, "tr64", [P, 2, P])
        tr4 = sb(st, "tr4", [P, 2, P])
        stri = sb(st, "stri", [P, P])
        head64 = sb(st, "head64", [P, P])
        blk4 = sb(st, "blk4", [P, P])
        bm4 = sb(st, "bm4", [P, 4, NB])
        bmask = sb(st, "bmask", [P, NB])
        vrow = sb(st, "vrow", [V_ROWS, P])
        vec = sb(st, "vec", [P, V_ROWS])
        ba = sb(st, "ba", [2 * HG, T])
        w2x = sb(st, "w2x", [65, HR * NR])
        a2 = sb(st, "a2", [P, HR * NR])
        g2 = sb(st, "g2", [P, HR * NR])
        dtb = sb(st, "dtb", [P, 2, HG])
        zt = sb(st, "zt", [P, HG, T])
        pr = sb(st, "pr", [P, R_TILES, RW])
        pg = sb(st, "pg", [P, C_TILES, GW])

        ld = ExitStack()
        with ld:
            sem = semaphores(nc, ld, "in")
            h_tm = sb(ld, "h_tm", [P, 3, D])
            hT = sb(ld, "hT", [P, KC, T])
            NG = 3
            wide = 512
            wst = sb(ld, "wst", [P, NG, KC, wide])
            shr = sb(ld, "shr", [NB, R_PROJ])
            cvr = sb(ld, "cvr", [NB * (CW - 1), CONV])
            x_in = [sem(f"x_in{i}") for i in range(3)]
            vec_in, small_in, tail_in = sem("vec_in"), sem("small_in"), sem("tail_in")
            w_in = [sem(f"w_in{i}") for i in range(NG)]
            masks = Count(sem("masks"))
            ngroups = -(-P_TOT // wide)
            w_view = a["w_in"][0].rearrange("(p c) n -> p c n", c=KC)

            def load_w(eng, g):
                n = min(wide, P_TOT - g * wide)
                eng.dma_start(wst[:, g % NG, :, 0:n], w_view[:, :, g * wide:g * wide + n]).then_inc(w_in[g % NG], 16)

            def first(block):
                @block.sync
                def _(sp):
                    xp = a["x_prompt"][0].rearrange("(i p) d -> i p d", p=P)
                    for i in range(2):
                        sp.dma_start(x[:, i, :], xp[i]).then_inc(x_in[i], 16)
                    sp.dma_start(x[:NS, 2, :], a["x_sample"].rearrange("b t d -> (b t) d")).then_inc(x_in[2], 16)
                    for i, n in enumerate(("norm_mix", "norm_cross", "norm_mem", "norm_ffn")):
                        sp.dma_start(g8[:, i, :], a[n][0].rearrange("(p c) -> p c", c=KC)).then_inc(small_in, 16)
                    for g in range(NG):
                        load_w(sp, g)
                    sp.wait_ge(small_in, 64)
                    for i in range(3):
                        sp.wait_ge(x_in[i], 16)

                @block.gpsimd
                def _(pool):
                    masks.step(pool, nc.gpsimd.memset(eps[:, 0:1], RMS_EPS))
                    masks.step(pool, nc.gpsimd.memset(eps[:, 1:2], GN_EPS))
                    masks.step(pool, nc.gpsimd.memset(ident[:], 1.0))
                    masks.step(pool, nc.gpsimd.affine_select(ident[:], ident[:], [[-1, P]], ALU.is_equal, 0.0, 0, 1))

                    def keep(ap, pattern, base, cm):
                        masks.step(pool, nc.gpsimd.affine_select(ap, ap, pattern, ALU.is_ge, 0.0, base, cm))
                    for ap in (ones[:], blk4[:], tri[:], stri[:], tr64[:, :, :], tr4[:, :, :], bm4[:, :, :]):
                        masks.step(pool, nc.gpsimd.memset(ap, 1.0))
                    for ap in (lvl[:, :, :], head64[:], pr[:, :, 0:1], pg[:, :, 0:CW - 1]):
                        masks.step(pool, nc.gpsimd.memset(ap, 0.0))
                    keep(tri[:], [[1, P]], 0, -1)
                    keep(stri[:], [[1, P]], -1, -1)
                    for m in (tr64, tr4):
                        keep(m[:, 0, :], [[1, P]], -1, -1)
                        keep(m[:, 1, :], [[1, P]], 0, -1)
                    keep(tr64[:, :, 64:], [[0, 2], [0, 64]], -64, 1)
                    for j in range(2):
                        v = tr4[:, j, :].rearrange("p (b t) -> p b t", t=TS)
                        keep(v, [[-TS, P // TS], [0, TS]], 0, 1)
                    v = blk4[:].rearrange("p (b t) -> p b t", t=TS)
                    keep(v, [[-TS, P // TS], [0, TS]], 0, 1)
                    keep(v, [[TS, P // TS], [0, TS]], TS - 1, -1)
                    keep(bm4[:, :, :], [[-32, 4], [-4, NB]], 0, 1)
                    keep(bm4[:, :, :], [[32, 4], [4, NB]], 3, -1)
                    for j in range(2):
                        masks.step(pool, nc.gpsimd.memset(head64[64 * j:64 * j + 64, 64 * j:64 * j + 64], 1.0))
                    for lv in range(7):
                        B = 1 << lv
                        v = lvl[:, lv, :].rearrange("p (j h b) -> p j h b", h=2, b=B)[:, :, 1, :]
                        masks.step(pool, nc.gpsimd.memset(v, 1.0))
                        keep(v, [[-2 * B, P // (2 * B)], [0, B]], 0, 1)
                        keep(v, [[2 * B, P // (2 * B)], [0, B]], B - 1, -1)

            with nc.Block() as block:
                first(block)
            norm_stage("mix", x, TILES, 0, hT, h_tm)

            prj, evac_v, evac_a = sem("prj"), sem("evac_v"), sem("evac_a")
            turned, turned_ok = sem("turned"), sem("turned_ok")
            bm_done = sem("bm_done")
            ntile = -(-P_TOT // P)

            def dest(i):
                if i < R_TILES:
                    v = pr[:, i, 1 + TP:].rearrange("p (b u) -> p b u", u=1 + TS)
                    return pr[:, i, 1:1 + TP], v[:, :, 1:]
                if i < Z0:
                    v = pg[:, i - R_TILES, CW - 1 + TP:].rearrange("p (b u) -> p b u", u=CW - 1 + TS)
                    return pg[:, i - R_TILES, CW - 1:CW - 1 + TP], v[:, :, CW - 1:]
                if i < Z0 + HG:
                    return zt[:, i - Z0, 0:TP], zt[:, i - Z0, TP:].rearrange("p (b u) -> p b u", u=TS)
                return ba[:, 0:TP], ba[:, TP:].rearrange("p (b u) -> p b u", u=TS)

            with nc.Block() as block:
                @block.sync
                def _(sp):
                    for g in range(NG, ngroups):
                        sp.wait_ge(prj, (g - NG + 1) * wide // P)
                        load_w(sp, g)

                def move(eng, copy, i, done):
                    eng.wait_ge(prj, i + 1)
                    n = min(P, P_TOT - i * P)
                    big, small = dest(i)
                    copy(big, ps[:n, i % 4, 0:TP])
                    copy(small, ps[:n, i % 4, TP:T].rearrange("p (b u) -> p b u", u=TS)).then_inc(done, 1)

                @block.vector
                def _(dve):
                    nc.vector.tensor_reduce(bmask[:], bm4[:, :, :].rearrange("p m b -> p b m"), AXX,
                                            ALU.add).then_inc(bm_done, 1)
                    dve.wait_ge(turned, 1)
                    nc.vector.tensor_copy(vec[:, :], ps[:, 4, 0:V_ROWS]).then_inc(turned_ok, 1)
                    dve.wait_ge(turned, 2)
                    nc.vector.tensor_copy(
                        pr[:, :, 1 + TP:].rearrange("p i (b u) -> p i b u", u=1 + TS)[:, :, :, 0],
                        ps[:, 5, 0:R_TILES * NB].rearrange("p (i b) -> p i b", b=NB)).then_inc(turned_ok, 1)
                    dve.wait_ge(turned, 3)
                    for j in range(CW - 1):
                        nc.vector.tensor_copy(
                            pg[:, :, CW - 1 + TP:].rearrange("p i (b u) -> p i b u", u=CW - 1 + TS)[:, :, :, j],
                            ps[:, 6, 0:C_TILES * NB * 3].rearrange("p (i b j) -> p i b j", b=NB, j=3)[:, :, :, j])
                    for i in range(0, ntile, 2):
                        move(dve, nc.vector.tensor_copy, i, evac_v)

                @block.scalar
                def _(act):
                    rows = [("mu_shift", V_MU, 14), ("a0", V_A0, 4), ("k_k", V_KK, 4), ("k_a", V_KA, 4),
                            ("r_k", V_RK, 4), ("lnx_w", V_LW, 4), ("lnx_b", V_LB, 4), ("conv_w", V_CW, 48),
                            ("gdn_norm_w", V_GN, 1)]
                    for name, r0, n in rows:
                        src = a[name][0]
                        src = (src.rearrange("h n -> (h n)") if name == "r_k" else
                               src.rearrange("w n -> (w n)") if name == "conv_w" else src)
                        act.dma_start(vrow[r0:r0 + n, :], src.rearrange("(r p) -> r p", p=P)).then_inc(vec_in, 16)
                    act.dma_start(shr[:, :], a["state_rwkv_shift"][0]).then_inc(vec_in, 16)
                    act.dma_start(cvr[:, :], a["state_gdn_conv"][0].rearrange("b j n -> (b j) n")).then_inc(vec_in, 16)
                    act.dma_start(w2x[0:64, :], a["w2_decay"][0]).then_inc(tail_in, 16)
                    act.dma_start(w2x[64:65, :], a["w0"]).then_inc(tail_in, 16)
                    act.dma_start(a2[64:P, :], a["a2_iclr"][0]).then_inc(tail_in, 16)
                    act.dma_start(g2[:, :], a["g2_gate"][0]).then_inc(tail_in, 16)
                    act.dma_start(dtb[:, 0, :], a["dt_bias"][0].partition_broadcast(P)).then_inc(tail_in, 16)
                    act.dma_start(dtb[:, 1, :], a["a_log"][0].partition_broadcast(P)).then_inc(tail_in, 16)
                    for i in range(1, ntile, 2):
                        move(act, nc.scalar.copy, i, evac_a)
                    act.wait_ge(tail_in, 96)

                @block.tensor
                def _(pe):
                    pe.wait_ge(vec_in, 16 * 11)
                    nc.tensor.transpose(ps[:, 4, 0:V_ROWS], vrow[:, :], ident[:V_ROWS, :V_ROWS]).then_inc(turned, 1)
                    for i in range(R_TILES):
                        ins = nc.tensor.transpose(ps[:, 5, i * NB:(i + 1) * NB], shr[:, i * P:(i + 1) * P],
                                                  ident[:NB, :NB])
                    ins.then_inc(turned, 1)
                    for i in range(C_TILES):
                        ins = nc.tensor.transpose(ps[:, 6, i * 24:(i + 1) * 24], cvr[:, i * P:(i + 1) * P],
                                                  ident[:24, :24])
                    ins.then_inc(turned, 1)
                    for i in range(ntile):
                        g, n = i * P // wide, min(P, P_TOT - i * P)
                        if i * P % wide == 0:
                            pe.wait_ge(w_in[g % NG], 16 * (g // NG + 1))
                        if i >= 4:
                            pe.wait_ge(evac_a if i % 2 else evac_v, (i - 4) // 2 + 1)
                        o = i * P % wide
                        for c in range(KC):
                            ins = nc.tensor.matmul(ps[:n, i % 4, 0:T], wst[:, g % NG, c, o:o + n], hT[:, c, :],
                                                   start=(c == 0), stop=(c == KC - 1))
                        ins.then_inc(prj, 1)


        rk = ExitStack()
        with rk:
            def sb_(n, shape):
                return sb(rk, n, shape)
            gate = sb_("gate", [P, PAIRS, T])
            bv = sb_("bv", [P, PAIRS, T])
            plast = sb_("plast", [P, PAIRS, NCR + NB])
            be_e = sb_("be_e", [P, NCR * PAIRS, P])
            ka_e = sb_("ka_e", [P, NCR * PAIRS, P])
            ar_e = sb_("ar_e", [P, NCR * PAIRS, 2, P])
            be_s = sb_("be_s", [P, 2, 2, 2 * NS])
            ka_s = sb_("ka_s", [P, 2, 2, 2 * NS])
            ar_s = sb_("ar_s", [P, 2, 2, 2, 2 * NS])
            v_c = sb_("v_c", [P, 18, NR])
            qk = sb_("qk", [P, 2, HG, T])
            gv = sb_("gv", [P, HG, T])
            sc = sb_("sc", [P, 12, 9])
            glb = sb_("glb", [P, HG * NB])
            m = Tiles()
            m.pr, m.vec, m.w2x, m.a2, m.g2, m.tr64, m.tr4, m.head64 = pr, vec, w2x, a2, g2, tr64, tr4, head64
            m.gate, m.bv, m.plast, m.be_e, m.ka_e, m.ar_e, m.be_s, m.ka_s = gate, bv, plast, be_e, ka_e, ar_e, be_s, ka_s
            m.ar_s, m.v_c, m.pg, m.zt, m.ba, m.dtb, m.tri, m.stri = ar_s, v_c, pg, zt, ba, dtb, tri, stri
            m.lvl, m.blk4, m.bm4, m.bmask, m.qk, m.gv, m.sc, m.glb = lvl, blk4, bm4, bmask, qk, gv, sc, glb
            m.yT = yT
            rwkv_elementwise(nc, a, out, sb, ps, ident, eps, m)
            carry_out(nc, out, sb, ps, ident, m)
            gdn_elementwise(nc, a, sb, ps, ident, ones, eps, m)
            recurrences(nc, a, out, sb, ps, ident, ones, eps, m)
        project_add(nc, sb, ps, x, yT, a["w_out"], "out")


S_BE, S_G, S_GC, S_NEG, S_EG, S_KT, S_GL, S_X, S_Y, S_U, S_DT, S_AL = range(12)


def rwkv_elementwise(nc, a, out, sb, ps, ident, eps, m):
    with ExitStack() as st:
        sem = semaphores(nc, st, "rw")
        xm = sb(st, "xm", [P, R_TILES, T])
        thx = sb(st, "thx", [65, T])
        sg = sb(st, "sg", [P, T])
        wl = sb(st, "wl", [P, 3, HR * NR])
        pc = sb(st, "pc", [P, PAIRS, T])
        px = sb(st, "px", [P, PAIRS, T])
        pi = sb(st, "pi", [P, PAIRS, T])
        av = sb(st, "av", [P, PAIRS, T])
        kk = sb(st, "kk", [P, PAIRS, T])
        tmp = sb(st, "tmp", [P, PAIRS, T])
        rkc = sb(st, "rkc", [P, PAIRS])
        v_e = sb(st, "v_e", [P, 4, P])
        pr, vec = m.pr, m.vec
        xr, xk, xv = (xm[:, 4 * j:4 * j + 4, :] for j in range(3))
        d, z = Count(sem("dve_chain")), Count(sem("zeroed"))
        lo_ready, th_ready, z_done, wl_ready, cs_done = (sem(n) for n in ("lo", "th", "z", "wl", "cs"))
        a_done, g_done, gate_ok, sq_ready, ss_done, root = (sem(n) for n in ("a", "g", "gate", "sq", "ss", "root"))
        a_ready, rkk, bonus, p_ready, ones_row, z_t = (sem(n) for n in ("a_ready", "rkk", "bonus", "p", "ones", "z_t"))
        kk_done = sem("kk")
        a_t, sg_t, bonus_used = (sem(n) for n in ("a_t", "sg_t", "bonus_used"))
        pairs = range(PAIRS)
        with nc.Block() as block:
            @block.gpsimd
            def _(pool):
                nc.gpsimd.memset(thx[64:65, :], 1.0).then_inc(ones_row, 1)
                pool.wait_ge(ones_row, 1)
                for ap in (m.be_e[:, :, :], m.ka_e[:, :, :], m.ar_e[:, :, :, :], m.be_s[:, :, :, :],
                           m.ka_s[:, :, :, :], m.ar_s[:, :, :, :, :]):
                    z.step(pool, nc.gpsimd.memset(ap, 0.0))

            @block.vector
            def _(dve):
                prs = pr[:, :, 1 + TP:].rearrange("p i (b u) -> p i b u", u=1 + TS)
                xms = xm[:, :, TP:].rearrange("p i (b u) -> p i b u", u=TS)
                for i0, i1 in ((12, 14), (0, 12)):
                    nc.vector.tensor_tensor(xm[:, i0:i1, 0:TP], pr[:, i0:i1, 0:TP], pr[:, i0:i1, 1:1 + TP], ALU.subtract)
                    d.step(dve, nc.vector.tensor_tensor(xms[:, i0:i1], prs[:, i0:i1, :, 0:TS], prs[:, i0:i1, :, 1:],
                                                        ALU.subtract))
                    for i in range(i0, i1):
                        mu = vec[:, V_MU + i:V_MU + i + 1]
                        nc.vector.scalar_tensor_tensor(xm[:, i, 0:TP], xm[:, i, 0:TP], mu, pr[:, i, 1:1 + TP],
                                                       ALU.mult, ALU.add)
                        ins = nc.vector.scalar_tensor_tensor(xms[:, i], xms[:, i], mu, prs[:, i, :, 1:],
                                                             ALU.mult, ALU.add)
                        if i == 13:
                            ins.then_inc(lo_ready, 1)
                d.step(dve, nc.vector.tensor_scalar(rkc[:, :], vec[:, V_A0:V_A0 + 4], 0.5, None, ALU.mult))
                for p in pairs:
                    ins = nc.vector.tensor_scalar(kk[:, p, :], xk[:, p, :], vec[:, V_KK + p:V_KK + p + 1], None,
                                                  ALU.mult)
                d.step(dve, ins)
                nc.vector.tensor_tensor(tmp[:, :, :], kk[:, :, :], kk[:, :, :], ALU.mult).then_inc(sq_ready, 1)
                dve.wait_ge(th_ready, 2)
                nc.vector.tensor_scalar(sg[:, :], sg[:, :], 0.5, 0.5, ALU.mult, ALU.add).then_inc(sg_t, 1)
                for i, (t0, n) in enumerate(TILES):
                    dve.wait_ge(z_t, i + 1)
                    nc.vector.tensor_scalar(wl[:n, i, :], wl[:n, i, :], -EXP_M05 / 2, -EXP_M05 / 2,
                                            ALU.mult, ALU.add).then_inc(wl_ready, 1)
                dve.wait_ge(a_t, 4)
                d.step(dve, nc.vector.tensor_scalar(av[:, :, :], av[:, :, :], 0.5, 0.5, ALU.mult, ALU.add))
                dve.wait_ge(root, 4)
                d.step(dve, nc.vector.reciprocal(pi[:, :, :], pi[:, :, :]))
                nc.vector.tensor_tensor(kk[:, :, :], kk[:, :, :], pi[:, :, :], ALU.mult).then_inc(kk_done, 1)
                dve.wait_ge(kk_done, 1)
                for p in pairs:
                    ins = nc.vector.tensor_scalar(tmp[:, p, :], av[:, p, :], 1.0, vec[:, V_KA + p:V_KA + p + 1],
                                                  ALU.subtract, ALU.mult)
                d.step(dve, ins)
                d.step(dve, nc.vector.scalar_tensor_tensor(xk, tmp[:, :, :], 1.0, xk, ALU.add, ALU.mult))
                for p in pairs:
                    nc.vector.scalar_tensor_tensor(tmp[:, p, :], xr[:, p, :], vec[:, V_RK + p:V_RK + p + 1],
                                                   xk[:, p, :], ALU.mult, ALU.mult).then_inc(rkk, 1)
                d.step(dve, nc.vector.tensor_tensor(av[:, :, :], kk[:, :, :], av[:, :, :], ALU.mult))
                for p in pairs:
                    dve.wait_ge(bonus, p + 1)
                    nc.vector.tensor_tensor(m.bv[:, p, :], ps[:, 4 + p, 0:T], xv[:, p, :], ALU.mult).then_inc(
                        bonus_used, 1)
                dve.wait_ge(p_ready, 3 * 4 + 3)
                dve.wait_ge(z.sem, 6)
                for h in range(2):
                    r = slice(64 * h, 64 * h + 64)
                    for p in pairs:
                        def ch(ap):
                            return ap[r, p, 0:TP].rearrange("p (c t) -> p c t", t=CR)
                        o = slice(64 * h, 64 * h + 64)
                        es = slice(NS * h, NS * h + NS)
                        p2, pp = p // 2, p % 2
                        for dst, dsm, f0, f1 in (
                                (m.ar_e[r, p::PAIRS, 0, o], m.ar_s[r, p2, 0, pp, es], px, kk),
                                (m.be_e[r, p::PAIRS, o], m.be_s[r, p2, pp, es], av, pi),
                                (m.ka_e[r, p::PAIRS, o], m.ka_s[r, p2, pp, es], xk, pi),
                                (m.ar_e[r, p::PAIRS, 1, o], m.ar_s[r, p2, 1, pp, es], pc, xr)):
                            nc.vector.tensor_tensor(dst, ch(f0), ch(f1), ALU.mult)
                            nc.vector.tensor_tensor(dsm, f0[r, p, TP:], f1[r, p, TP:], ALU.mult)
                nc.vector.tensor_copy(m.plast[:, :, 0:NCR], pc[:, :, CR - 1:TP:CR])
                nc.vector.tensor_copy(m.plast[:, :, NCR:], pc[:, :, TP + TS - 1::TS])

            @block.scalar
            def _(act):
                act.wait_ge(lo_ready, 1)
                nc.scalar.activation(thx[0:64, :], xm[0:64, 12, :], ACT.Tanh).then_inc(th_ready, 1)
                nc.scalar.activation(sg[:, :], xm[:, 13, :], ACT.Tanh, scale=0.5).then_inc(th_ready, 1)
                for i, (t0, n) in enumerate(TILES):
                    act.wait_ge(z_done, i + 1)
                    nc.scalar.activation(wl[:n, i, :], ps[:n, i, :], ACT.Tanh, scale=0.5).then_inc(z_t, 1)
                act.wait_ge(sq_ready, 1)
                for p in pairs:
                    act.wait_ge(a_done, p + 1)
                    nc.scalar.activation(av[:, p, :], ps[:, 4 + p, 0:T], ACT.Tanh, bias=rkc[:, p:p + 1],
                                         scale=0.5).then_inc(a_t, 1)
                for p in pairs:
                    act.wait_ge(g_done, p + 1)
                    nc.scalar.copy(m.gate[:, p, :], ps[:, p, 0:T]).then_inc(gate_ok, 1)
                for p in pairs:
                    act.wait_ge(ss_done, p + 1)
                    nc.scalar.activation(pi[:, p, :], ps[:, 4 + p, 0:T], ACT.Sqrt, bias=eps[:, 0:1]).then_inc(root, 1)
                act.wait_ge(kk_done, 1)
                for p in pairs:
                    act.wait_ge(cs_done, p + 1)
                    v = ps[:, p, :].rearrange("p (i j t) -> p i j t", i=2, j=2)
                    for dst, j, s in ((px, 0, 1.0), (pc, 1, 1.0), (pi, 1, -1.0)):
                        nc.scalar.activation(dst[:, p, 0:TP].rearrange("p (i t) -> p i t", i=2), v[:, :, j, :],
                                             ACT.Exp, scale=s).then_inc(p_ready, 1)
                act.wait_ge(cs_done, 5)
                v = ps[:, 4, 0:256].rearrange("p (q j t) -> p q j t", q=4, j=2)
                for dst, j, s in ((px, 0, 1.0), (pc, 1, 1.0), (pi, 1, -1.0)):
                    nc.scalar.activation(dst[:, :, TP:], v[:, :, j, :], ACT.Exp, scale=s).then_inc(p_ready, 1)

            @block.tensor
            def _(pe):
                pe.wait_ge(ones_row, 1)
                pe.wait_ge(th_ready, 1)
                for i, (t0, n) in enumerate(TILES):
                    nc.tensor.matmul(ps[:n, i, :], thx[:, t0:t0 + n], m.w2x[:, :], start=True,
                                     stop=True).then_inc(z_done, 1)
                for p in pairs:
                    nc.tensor.matmul(ps[:, 4 + p, 0:T], m.a2[64:P, p * P:(p + 1) * P], xm[64:P, 12, :], start=True,
                                     stop=True).then_inc(a_done, 1)
                pe.wait_ge(sg_t, 1)
                pe.wait_ge(z_t, 3)
                for p in pairs:
                    nc.tensor.matmul(ps[:, p, 0:T], m.g2[:, p * P:(p + 1) * P], sg[:, :], start=True,
                                     stop=True).then_inc(g_done, 1)
                pe.wait_ge(sq_ready, 1)
                pe.wait_ge(a_t, 4)
                for p in pairs:
                    nc.tensor.matmul(ps[:, 4 + p, 0:T], m.head64[:], tmp[:, p, :], start=True,
                                     stop=True).then_inc(ss_done, 1)
                pe.wait_ge(wl_ready, 3)
                pe.wait_ge(gate_ok, 4)
                for p in pairs:
                    for i in range(2):
                        ins = nc.tensor.matmul(ps[:, p, 256 * i:256 * i + 256], wl[:, i, p * P:(p + 1) * P],
                                               m.tr64[:, :, :], start=True, stop=True)
                    ins.then_inc(cs_done, 1)
                for p in pairs:
                    pe.wait_ge(rkk, p + 1)
                    pe.wait_ge(root, 4)
                    nc.tensor.matmul(ps[:, 4 + p, 0:T], m.head64[:], tmp[:, p, :], start=True,
                                     stop=True).then_inc(bonus, 1)
                pe.wait_ge(bonus_used, 1)
                for p in pairs:
                    ins = nc.tensor.matmul(ps[:, 4, 64 * p:64 * p + 64], wl[:NS, 2, p * P:(p + 1) * P],
                                           m.tr4[:NS, :, 0:NS], start=True, stop=True)
                ins.then_inc(cs_done, 1)

        v_s = sb(st, "v_s", [P, 2, 2, 2 * NS])
        turned, kept, spread, zeroed = sem("turned"), sem("kept"), sem("spread"), sem("zeroed2")
        with nc.Block() as block:
            @block.gpsimd
            def _(pool):
                nc.gpsimd.memset(v_e[:, :, :], 0.0).then_inc(zeroed, 1)
                pool.wait_ge(zeroed, 1)
                nc.gpsimd.memset(v_s[:, :, :, :], 0.0).then_inc(zeroed, 1)

            @block.scalar
            def _(act):
                act.wait_ge(zeroed, 2)
                for h in range(2):
                    r = slice(64 * h, 64 * h + 64)
                    ins = nc.scalar.copy(v_s[r, :, :, NS * h:NS * h + NS],
                                         xv[r, :, TP:].rearrange("p (i j) t -> p i j t", i=2))
                ins.then_inc(spread, 1)
                for c in range(NCR):
                    if c:
                        act.wait_ge(turned, c + 1)
                    for h in range(2):
                        r = slice(64 * h, 64 * h + 64)
                        ins = nc.scalar.copy(v_e[r, :, CR * h:CR * h + CR], xv[r, :, c * CR:c * CR + CR])
                    ins.then_inc(spread, 1)

            @block.tensor
            def _(pe):
                pe.wait_ge(spread, 1)
                for p in pairs:
                    r = slice(64 * (p % 2), 64 * (p % 2) + 64)
                    ins = nc.tensor.matmul(ps[r, 2, (p // 2) * P:(p // 2) * P + P], v_s[:, p // 2, p % 2, :], ident[:],
                                           start=True, stop=True)
                ins.then_inc(turned, 1)
                for c in range(NCR):
                    pe.wait_ge(spread, c + 2)
                    if c >= 2:
                        pe.wait_ge(kept, c)
                    for p in pairs:
                        ins = nc.tensor.transpose(ps[:, c % 2, p * P:(p + 1) * P], v_e[:, p, :], ident[:])
                    ins.then_inc(turned, 1)

            @block.vector
            def _(dve):
                dve.wait_ge(turned, 1)
                for q in range(4):
                    r, h = slice(NS * q, NS * q + NS), q % 2
                    ins = nc.vector.tensor_copy(m.v_c[r, 16:18, :], ps[r, 2, 0:256].rearrange(
                        "p (i v) -> p i v", i=2)[:, :, NR * h:NR * h + NR])
                ins.then_inc(kept, 1)
                for c in range(NCR):
                    dve.wait_ge(turned, c + 2)
                    for h in range(2):
                        r = slice(64 * h, 64 * h + 64)
                        ins = nc.vector.tensor_copy(
                            m.v_c[r, 4 * c:4 * c + 4, :],
                            ps[r, c % 2, :].rearrange("p (q v) -> p q v", q=4)[:, :, NR * h:NR * h + NR])
                    ins.then_inc(kept, 1)


def carry_out(nc, out, sb, ps, ident, m):
    with ExitStack() as st:
        sem = semaphores(nc, st, "co")
        NJ = CW - 1
        last = sb(st, "last", [P, R_TILES, 1 + NB])
        lastc = sb(st, "lastc", [P, C_TILES, (1 + NB) * NJ])
        row = sb(st, "row", [1 + NB, R_PROJ])
        rowc = sb(st, "rowc", [(1 + NB) * NJ, CONV])
        picked, turned, moved, stored = sem("picked"), sem("turned"), sem("moved"), sem("stored")
        with nc.Block() as block:
            @block.vector
            def _(dve):
                nc.vector.tensor_copy(last[:, :, 0:1], m.pr[:, :, TP:TP + 1])
                nc.vector.tensor_copy(last[:, :, 1:], m.pr[:, :, 1 + TP + TS::1 + TS]).then_inc(picked, 1)
                nc.vector.tensor_copy(lastc[:, :, 0:NJ], m.pg[:, :, TP:TP + NJ])
                nc.vector.tensor_copy(lastc[:, :, NJ:].rearrange("p i (b j) -> p i b j", j=NJ),
                                      m.pg[:, :, NJ + TP:].rearrange("p i (b u) -> p i b u", u=NJ + TS)[:, :, :, TS:]
                                      ).then_inc(picked, 1)
                dve.wait_ge(turned, 1)
                for i in range(4):
                    n = min(512, R_PROJ - 512 * i)
                    ins = nc.vector.tensor_copy(row[:, 512 * i:512 * i + n], ps[:1 + NB, i, 0:n])
                ins.then_inc(moved, 1)

            @block.scalar
            def _(act):
                act.wait_ge(turned, 2)
                for i in range(3):
                    ins = nc.scalar.copy(rowc[:, 512 * i:512 * i + 512], ps[:(1 + NB) * NJ, 4 + i, :])
                ins.then_inc(moved, 1)

            @block.tensor
            def _(pe):
                pe.wait_ge(picked, 1)
                for i in range(R_TILES):
                    ins = nc.tensor.transpose(ps[:1 + NB, i // 4, P * (i % 4):P * (i % 4) + P], last[:, i, :], ident[:])
                ins.then_inc(turned, 1)
                pe.wait_ge(picked, 2)
                for i in range(C_TILES):
                    ins = nc.tensor.transpose(ps[:(1 + NB) * NJ, 4 + i // 4, P * (i % 4):P * (i % 4) + P],
                                              lastc[:, i, :], ident[:])
                ins.then_inc(turned, 1)

            @block.sync
            def _(sp):
                sp.wait_ge(moved, 2)
                sp.dma_start(out[3][0], row[0:1, :]).then_inc(stored, 16)
                sp.dma_start(out[9][0], row[1:1 + NB, :]).then_inc(stored, 16)
                sp.dma_start(out[5][0, 0], rowc[0:NJ, :]).then_inc(stored, 16)
                sp.dma_start(out[11][0].rearrange("b j n -> (b j) n"), rowc[NJ:, :]).then_inc(stored, 16)
                sp.wait_ge(stored, 64)


def gdn_elementwise(nc, a, sb, ps, ident, ones, eps, m):
    with ExitStack() as st:
        sem = semaphores(nc, st, "gd")
        cv = sb(st, "cv", [P, C_TILES, T])
        th = sb(st, "th", [P, C_TILES, T])
        cwh = sb(st, "cwh", [P, 48])
        gm = sb(st, "gm", [P, HG * NB])
        d, g = Count(sem("dve")), Count(sem("pool"))
        conv_v, conv_p, cw_ok, th_v, sq, ss, root, zh, zth = (
            sem(n) for n in ("conv_v", "conv_p", "cw", "th", "sq", "ss", "root", "zh", "zth"))
        bt, bt_ok, x_ok, ex, ln, gs, gc, sc_t, gm_ok, egc = (
            sem(n) for n in ("bt", "bt_ok", "x", "ex", "ln", "g", "gc", "sc_t", "gm", "egc"))
        sc, vec = m.sc, m.vec
        gv_ok = sem("gv_ok")
        NV = 8

        pgs = m.pg[:, :, CW - 1 + TP:].rearrange("p i (b u) -> p i b u", u=CW - 1 + TS)

        def convolve(eng, ops, i0, i1, chain, done, fused):
            for j in range(CW):
                for i in range(i0, i1):
                    w = cwh[:, 12 * j + i:12 * j + i + 1]
                    to = cv if fused or j == 0 else th
                    ts = to[:, i, TP:].rearrange("p (b u) -> p b u", u=TS)
                    for dst, src in ((to[:, i, 0:TP], m.pg[:, i, j:j + TP]), (ts, pgs[:, i, :, j:j + TS])):
                        if j == 0 or not fused:
                            ins = ops.tensor_scalar(dst, src, w, None, ALU.mult)
                        else:
                            ins = ops.scalar_tensor_tensor(dst, src, w, dst, ALU.mult, ALU.add)
                if j and not fused:
                    chain.step(eng, ins)
                    ins = ops.tensor_tensor(cv[:, i0:i1, :], cv[:, i0:i1, :], th[:, i0:i1, :], ALU.add)
                if j < CW - 1:
                    chain.step(eng, ins)
                else:
                    ins.then_inc(done, 1)

        with nc.Block() as block:
            @block.vector
            def _(dve):
                nc.vector.tensor_scalar(cwh[:, :], vec[:, V_CW:V_CW + 48], 0.5, None, ALU.mult).then_inc(cw_ok, 1)
                d.step(dve, nc.vector.memset(sc[:, :, :], 0.0))
                for j, row in ((0, S_DT), (1, S_AL)):
                    for i in range(2):
                        nc.vector.tensor_copy(sc[:, row, 4 * i:4 * i + 4], m.dtb[:, j, :])
                    for h in range(HG):
                        r = slice(NS * h, NS * h + NS)
                        ins = nc.vector.tensor_copy(sc[r, row, 8:9], m.dtb[r, j, h:h + 1])
                dve.wait_ge(bt, 1)
                for j, row in ((0, S_BE), (1, S_X)):
                    nc.vector.tensor_copy(sc[:, row, 0:8].rearrange("p (i h) -> p i h", i=2),
                                          ps[:, 0, 0:16].rearrange("p (i j h) -> p i j h", i=2, j=2)[:, :, j, :])
                    for h in range(HG):
                        r = slice(NS * h, NS * h + NS)
                        ins = nc.vector.tensor_copy(sc[r, row, 8:9], ps[r, 0, 16 + 4 * j + h:17 + 4 * j + h])
                d.step(dve, ins)
                d.step(dve, nc.vector.tensor_tensor(sc[:, S_X, :], sc[:, S_X, :], sc[:, S_DT, :], ALU.add))
                d.step(dve, nc.vector.tensor_scalar(sc[:, S_Y, :], sc[:, S_X, :], -1.0, None, ALU.mult))
                nc.vector.tensor_tensor(sc[:, S_Y, :], sc[:, S_X, :], sc[:, S_Y, :], ALU.max).then_inc(x_ok, 1)
                dve.wait_ge(cw_ok, 1)
                convolve(dve, nc.vector, 0, NV, d, conv_v, True)
                dve.wait_ge(ln, 1)
                d.step(dve, nc.vector.tensor_scalar(sc[:, S_X, :], sc[:, S_X, :], 0.0, None, ALU.max))
                d.step(dve, nc.vector.tensor_tensor(sc[:, S_X, :], sc[:, S_X, :], sc[:, S_U, :], ALU.add))
                nc.vector.tensor_scalar(sc[:, S_BE, :], sc[:, S_BE, :], 0.5, 0.5, ALU.mult, ALU.add)
                d.step(dve, nc.vector.scalar_tensor_tensor(sc[:, S_G, :], sc[:, S_X, :], -1.0, sc[:, S_AL, :],
                                                           ALU.mult, ALU.mult))
                nc.vector.tensor_scalar(gm[:, :], m.bm4[:, :, :].rearrange("p m b -> p (m b)"), sc[:, S_G, 8:9], None,
                                        ALU.mult).then_inc(gs, 1)
                dve.wait_ge(gc, 1)
                nc.vector.tensor_copy(sc[:, S_GC, :], ps[:, 1, 0:9])
                nc.vector.tensor_copy(m.glb[:, :], ps[:, 1, 32:64])
                d.step(dve, nc.vector.tensor_copy(sc[:, S_GL, :], ps[:, 1, 16:25]))
                nc.vector.tensor_tensor(sc[:, S_KT, :], sc[:, S_GL, :], sc[:, S_GC, :], ALU.subtract).then_inc(gm_ok, 1)
                dve.wait_ge(egc, 2)
                nc.vector.tensor_scalar(sc[:, S_NEG, :], sc[:, S_EG, :], -1.0, None, ALU.mult)
                dve.wait_ge(th_v, 2)
                nc.vector.scalar_tensor_tensor(cv[:, 0:8, :], th[:, 0:8, :], 1.0, cv[:, 0:8, :], ALU.add,
                                               ALU.mult).then_inc(sq, 1)
                nc.vector.scalar_tensor_tensor(m.gv[:, :, :], th[:, 8:12, :], 1.0, cv[:, 8:12, :], ALU.add,
                                               ALU.mult).then_inc(gv_ok, 1)
                for i in range(8):
                    dve.wait_ge(root, i + 1)
                    ins = nc.vector.reciprocal(th[:, i, :], th[:, i, :])
                d.step(dve, ins)
                nc.vector.scalar_tensor_tensor(m.qk[:, 1, :, :], cv[:, 0:4, :], DG ** -0.5, th[:, 0:4, :], ALU.mult,
                                               ALU.mult)
                nc.vector.tensor_tensor(m.qk[:, 0, :, :], cv[:, 4:8, :], th[:, 4:8, :], ALU.mult)
                dve.wait_ge(zth, 1)
                nc.vector.scalar_tensor_tensor(m.zt[:, :, :], cv[:, 8:12, :], 1.0, m.zt[:, :, :], ALU.add, ALU.mult)

            @block.gpsimd
            def _(pool):
                pool.wait_ge(cw_ok, 1)
                convolve(pool, nc.gpsimd, NV, C_TILES, g, conv_p, False)
                nc.gpsimd.tensor_scalar(m.zt[:, :, :], m.zt[:, :, :], 0.5, None, ALU.mult).then_inc(zh, 1)

            @block.scalar
            def _(act):
                act.wait_ge(x_ok, 1)
                nc.scalar.activation(sc[:, S_BE, :], sc[:, S_BE, :], ACT.Tanh, scale=0.5)
                nc.scalar.activation(sc[:, S_AL, :], sc[:, S_AL, :], ACT.Exp)
                nc.scalar.activation(sc[:, S_U, :], sc[:, S_Y, :], ACT.Exp, scale=-1.0).then_inc(ex, 1)
                act.wait_ge(ex, 1)
                nc.scalar.activation(sc[:, S_U, :], sc[:, S_U, :], ACT.Ln, bias=1.0).then_inc(ln, 1)
                act.wait_ge(gm_ok, 1)
                nc.scalar.activation(sc[:, S_EG, :], sc[:, S_GC, :], ACT.Exp).then_inc(egc, 1)
                nc.scalar.activation(sc[:, S_KT, :], sc[:, S_KT, :], ACT.Exp)
                nc.scalar.activation(sc[:, S_GL, :], sc[:, S_GL, :], ACT.Exp)
                nc.scalar.activation(m.glb[:, :], m.glb[:, :], ACT.Exp).then_inc(egc, 1)
                act.wait_ge(conv_v, 1)
                nc.scalar.activation(th[:, 0:8, :], cv[:, 0:8, :], ACT.Tanh).then_inc(th_v, 1)
                act.wait_ge(conv_p, 1)
                nc.scalar.activation(th[:, 8:12, :], cv[:, 8:12, :], ACT.Tanh).then_inc(th_v, 1)
                act.wait_ge(sq, 1)
                nc.scalar.activation(th[:, 0:8, :], cv[:, 0:8, :], ACT.Square).then_inc(sq, 1)
                act.wait_ge(zh, 1)
                for i in range(8):
                    act.wait_ge(ss, i + 1)
                    nc.scalar.activation(th[:, i, :], ps[:, i % 8, 0:T], ACT.Sqrt, bias=eps[:, 0:1]).then_inc(root, 1)
                act.wait_ge(gv_ok, 1)
                nc.scalar.activation(cv[:, 8:12, :], m.zt[:, :, :], ACT.Tanh).then_inc(zth, 1)

            @block.tensor
            def _(pe):
                for i in range(2):
                    nc.tensor.transpose(ps[:, 0, 8 * i:8 * i + 8], m.ba[:, P * i:P * i + P], ident[:8, :8])
                for h in range(HG):
                    ins = nc.tensor.matmul(ps[NS * h:NS * h + NS, 0, 16:24], m.ba[:, TP:T], ident[:8, :8],
                                           start=True, stop=True, tile_position=(0, NS * h))
                ins.then_inc(bt, 1)
                pe.wait_ge(gs, 1)
                nc.tensor.matmul(ps[:, 1, 0:8], m.tri[:], sc[:, S_G, 0:8], start=True, stop=True)
                nc.tensor.matmul(ps[:, 1, 8:9], m.tr4[:, 1, :], sc[:, S_G, 8:9], start=True, stop=True)
                nc.tensor.matmul(ps[:, 1, 16:24], ones[:], sc[:, S_G, 0:8], start=True, stop=True)
                nc.tensor.matmul(ps[:, 1, 24:25], m.blk4[:], sc[:, S_G, 8:9], start=True, stop=True)
                nc.tensor.matmul(ps[:, 1, 32:64], ones[:], gm[:, :], start=True, stop=True).then_inc(gc, 1)
                pe.wait_ge(sq, 2)
                pe.wait_ge(egc, 2)
                for i in range(8):
                    nc.tensor.matmul(ps[:, i, 0:T], ones[:], th[:, i, :], start=True, stop=True).then_inc(ss, 1)


def over(ap, n, at=1):
    v = ap.unsqueeze(at)
    shape = list(v.shape)
    shape[at] = n
    return v.broadcast_to(shape)


def invert(nc, sb, ps, ident, m, name, groups):
    with ExitStack() as st:
        sem = semaphores(nc, st, name)
        ng = len(groups)
        ct = [sb(st, f"{name}_ct{g}", [P, n, P]) for g, (_, _, n, _) in enumerate(groups)]
        tt = [sb(st, f"{name}_t{g}", [P, n, P]) for g, (_, _, n, _) in enumerate(groups)]
        xt = [sb(st, f"{name}_x{g}", [P, n, P]) for g, (_, _, n, _) in enumerate(groups)]
        init, c_ok = Count(sem("init")), sem("c_ok")
        t_done, t_ok = [sem(f"t_done{g}") for g in range(ng)], [sem(f"t_ok{g}") for g in range(ng)]
        x_done, x_ok = [sem(f"x_done{g}") for g in range(ng)], [sem(f"x_ok{g}") for g in range(ng)]
        z_done, z_ok = [sem(f"z_done{g}") for g in range(ng)], [sem(f"z_ok{g}") for g in range(ng)]
        steps = [(lv, g) for lv in range(1, max(q[3] for q in groups)) for g in range(ng) if lv < groups[g][3]]
        levels = sorted({lv for lv, _ in steps})
        order = [(kind, lv, g) for lv in levels for kind in "TXZ" for l2, g in steps if l2 == lv]
        emptied = {"T": t_ok, "X": x_ok, "Z": z_ok}
        bank = {q: i % 8 for i, q in enumerate(order)}

        def out_of(q):
            n = groups[q[2]][2]
            return ps[:, bank[q], 0:n * P].rearrange("p (u t) -> p u t", u=n)

        with nc.Block() as block:
            @block.gpsimd
            def _(pool):
                done = 0
                for lv, g in steps:
                    at, _, n, _ = groups[g]
                    if lv > 1:
                        pool.wait_ge(x_done[g], lv - 1)
                    if done:
                        pool.wait_ge(c_ok, done)
                    nc.gpsimd.tensor_tensor(ct[g][:, :, :], at, over(m.lvl[:, lv, :], n), ALU.mult).then_inc(c_ok, 1)
                    done += 1

            @block.vector
            def _(dve):
                for at, ttr, n, _ in groups:
                    ins = nc.vector.tensor_tensor(ttr, at, over(m.lvl[:, 0, :], n), ALU.mult)
                init.step(dve, ins)
                for at, ttr, n, _ in groups:
                    init.inc(nc.vector.tensor_tensor(ttr, over(ident[:], n), ttr, ALU.subtract))
                dve.wait_ge(init.sem, 1 + ng)
                for lv, g in steps:
                    dve.wait_ge(z_done[g], lv)
                    ttr = groups[g][1]
                    nc.vector.tensor_tensor(ttr, ttr, out_of(("Z", lv, g)), ALU.subtract).then_inc(z_ok[g], 1)

            @block.scalar
            def _(act):
                for kind, lv, g in order:
                    if kind == "T":
                        act.wait_ge(t_done[g], lv)
                        nc.scalar.copy(tt[g][:, :, :], out_of((kind, lv, g))).then_inc(t_ok[g], 1)
                    if kind == "X":
                        act.wait_ge(x_done[g], lv)
                        nc.scalar.copy(xt[g][:, :, :], out_of((kind, lv, g))).then_inc(x_ok[g], 1)

            @block.tensor
            def _(pe):
                for i, (kind, lv, g) in enumerate(order):
                    if i >= 8:
                        k8, l8, g8 = order[i - 8]
                        pe.wait_ge(emptied[k8][g8], l8)
                    _, ttr, n, _ = groups[g]
                    if kind == "T":
                        pe.wait_ge(init.sem, 2 + g)
                        if lv > 1:
                            pe.wait_ge(z_ok[g], lv - 1)
                    elif kind == "X":
                        pe.wait_ge(t_ok[g], lv)
                        pe.wait_ge(c_ok, steps.index((lv, g)) + 1)
                    else:
                        pe.wait_ge(x_ok[g], lv)
                    dst = out_of((kind, lv, g))
                    for u in range(n):
                        if kind == "T":
                            ins = nc.tensor.transpose(dst[:, u, :], ttr[:, u, :], ident[:])
                        elif kind == "X":
                            ins = nc.tensor.matmul(dst[:, u, :], ct[g][:, u, :], tt[g][:, u, :], start=True, stop=True)
                        else:
                            ins = nc.tensor.matmul(dst[:, u, :], xt[g][:, u, :], ttr[:, u, :], start=True, stop=True)
                    ins.then_inc({"T": t_done, "X": x_done, "Z": z_done}[kind][g], 1)


def recurrences(nc, a, out, sb, ps, ident, ones, eps, m):
    with ExitStack() as st:
        m.y_r = sb(st, "y_r", [P, 18, NR])
        m.y_g = sb(st, "y_g", [P, 9, DG])
        sample_step(nc, a, out, sb, ps, ident, ones, m)
        prompt_chunks(nc, out, sb, ps, ident, ones, m)
        read_out(nc, sb, ps, ident, eps, m)


def sample_step(nc, a, out, sb, ps, ident, ones, m):
    with ExitStack() as st:
        sem = semaphores(nc, st, "sa")
        stage_t = m.pr[:, :, :].rearrange("p i w -> p (i w)")[:, 0:PAIRS * NB * P].rearrange(
            "p (q b k) -> p q b k", q=PAIRS, b=NB)
        mst = sb(st, "mst", [P, PAIRS, NB, NR])
        sst = sb(st, "sst", [P, HG, NB, DG])
        mb = sb(st, "s_mb", [P, 2, 2, P])
        mk = sb(st, "s_mk", [P, 2, 2, P])
        gmx = sb(st, "s_gm", [P, 2, P])
        dt = sb(st, "s_dt", [P, P])
        dtm = sb(st, "s_dtm", [P, 2, P])
        gb = sb(st, "s_gb", [P, P])
        tmt = sb(st, "s_tmt", [P, 2, 2, P])
        kv = sb(st, "s_kv", [P, 2, P])
        tinv = sb(st, "s_tinv", [P, 3, P])
        ati = sb(st, "s_ati", [P, 3, P])
        qs_, ks_ = m.qk[:, 1, :, TP:], m.qk[:, 0, :, TP:]
        loaded, zeroed, gb_ok, mm, ev, dd, de = (sem(n) for n in ("loaded", "zeroed", "gb", "mm", "ev", "dd", "de"))
        dch = Count(sem("dve"))
        ks_c = sb(st, "s_ksc", [P, 2, P])
        gvs = sb(st, "s_gvs", [P, P])
        with nc.Block() as block:
            @block.gpsimd
            def _(pool):
                nc.gpsimd.memset(stage_t, 0.0).then_inc(zeroed, 1)
                pool.wait_ge(zeroed, 1)
                nc.gpsimd.tensor_scalar(gb[:, :], ones[:], m.sc[:, S_G, 8:9], None, ALU.mult).then_inc(gb_ok, 1)

            @block.sync
            def _(sp):
                for h in range(HG):
                    sp.dma_start(sst[:, h], a["state_gdn"][0, :, h].rearrange("b k v -> k b v")).then_inc(loaded, 16)
                sp.wait_ge(zeroed, 1)
                for p in range(PAIRS):
                    for h in range(2):
                        r = slice(64 * h, 64 * h + 64)
                        sp.dma_start(stage_t[r, p, :, r],
                                     a["state_rwkv"][0, :, 2 * p + h].rearrange("b v k -> v b k")).then_inc(loaded, 16)
                sp.wait_ge(loaded, 16 * 12)

            @block.tensor
            def _(pe):
                for q, w in ((0, m.be_s), (1, m.ka_s)):
                    for p2 in range(2):
                        for pp in range(2):
                            r = slice(64 * pp, 64 * pp + 64)
                            ins = nc.tensor.matmul(ps[r, 2 * q + p2, 0:256], w[:, p2, pp, :],
                                                   m.ar_s[:, p2].rearrange("p j q t -> p (j q t)"), start=True, stop=True)
                            nc.tensor.matmul(ps[r, 6, 256 * q + P * p2:256 * q + P * p2 + P], w[:, p2, pp, :],
                                             ident[:], start=True, stop=True)
                        ins.then_inc(mm, 1)
                pe.wait_ge(gb_ok, 1)
                nc.tensor.matmul(ps[:, 4, 0:P], gb[:, :], m.tr4[:, 1, :], start=True, stop=True).then_inc(mm, 1)
                pe.wait_ge(ev, 1)
                nc.tensor.matmul(ps[:, 5, 0:256], ks_c[:, 0, :], ks_c[:, :, :].rearrange("p j t -> p (j t)"),
                                 start=True, stop=True).then_inc(mm, 1)
                nc.tensor.transpose(ps[:, 7, 0:P], ks_c[:, 0, :], ident[:])
                nc.tensor.transpose(ps[:, 7, P:2 * P], gvs[:, :], ident[:]).then_inc(mm, 1)

            @block.vector
            def _(dve):
                nc.vector.tensor_copy(gvs[:, :].rearrange("p (h t) -> p h t", h=HG), m.gv[:, :, TP:])
                nc.vector.tensor_copy(ks_c[:, :, :].rearrange("p j (h t) -> p j h t", h=HG),
                                      m.qk[:, :, :, TP:]).then_inc(ev, 1)
                for i in range(4):
                    dve.wait_ge(mm, i + 1)
                    dst = (mb, mk)[i // 2]
                    nc.vector.tensor_tensor(dst[:, i % 2, :, :].rearrange("p j t -> p (j t)"), ps[:, i, 0:256],
                                            m.tr4[:, :, :].rearrange("p j t -> p (j t)"), ALU.mult)
                dve.wait_ge(mm, 5)
                nc.vector.tensor_scalar(dt[:, :], ps[:, 4, 0:P], m.sc[:, S_GC, 8:9], 0.0, ALU.subtract,
                                        ALU.min).then_inc(dd, 1)
                dve.wait_ge(de, 1)
                nc.vector.scalar_tensor_tensor(dtm[:, 0, :], dt[:, :], m.sc[:, S_BE, 8:9], m.tr4[:, 0, :], ALU.mult,
                                               ALU.mult)
                dch.step(dve, nc.vector.tensor_tensor(dtm[:, 1, :], dt[:, :], m.tr4[:, 1, :], ALU.mult))
                dve.wait_ge(mm, 7)
                dch.step(dve, nc.vector.tensor_tensor(gmx[:, :, :].rearrange("p j t -> p (j t)"), ps[:, 5, 0:256],
                                                      dtm[:, :, :].rearrange("p j t -> p (j t)"), ALU.mult))
                nc.vector.tensor_copy(ati[:, 0, :], gmx[:, 0, :])
                nc.vector.tensor_copy(ati[:, 1:3, :], mb[:, :, 0, :])
                nc.vector.tensor_scalar(kv[:, 0, :], ps[:, 7, 0:P], m.sc[:, S_KT, 8:9], None, ALU.mult)
                nc.vector.tensor_copy(kv[:, 1, :], ps[:, 7, P:2 * P])
                nc.vector.tensor_copy(tmt[:, :, :, :].rearrange("p q i k -> p (q i k)"), ps[:, 6, :])

            @block.scalar
            def _(act):
                act.wait_ge(dd, 1)
                nc.scalar.activation(dt[:, :], dt[:, :], ACT.Exp).then_inc(de, 1)

        turned = sem("turned")

        def turn_states(block):
            def gather(eng, copy, odd):
                for q in range(8):
                    if q % 2 == odd:
                        eng.wait_ge(turned, q + 1)
                        for h in range(2):
                            r = slice(64 * h, 64 * h + 64)
                            ins = copy(mst[r, q // 2, 4 * odd:4 * odd + 4, :],
                                       ps[r, q, :].rearrange("p (b k) -> p b k", b=4)[:, :, r])

            @block.tensor
            def _(pe):
                for q in range(8):
                    for b in range(4):
                        ins = nc.tensor.transpose(ps[:, q, P * b:P * b + P], stage_t[:, q // 2, 4 * (q % 2) + b, :],
                                                  ident[:])
                    ins.then_inc(turned, 1)

            @block.vector
            def _(dve):
                gather(dve, nc.vector.tensor_copy, 0)

            @block.scalar
            def _(act):
                gather(act, nc.scalar.copy, 1)

        with nc.Block() as block:
            turn_states(block)
        invert(nc, sb, ps, ident, m, "si", [(ati[:, :, :], tinv[:, :, :], 3, 2)])

        zt = sb(st, "s_z", [P, 2, NB, NR])
        zg = sb(st, "s_zg", [P, NB, DG])
        zs = sb(st, "s_zs", [P, 2, 2, NR])
        zgs = sb(st, "s_zgs", [P, 2, DG])
        rr = sb(st, "s_r", [P, 2, NR])
        un = sb(st, "s_un", [P, 2, NR])
        vm = sb(st, "s_vm", [P, 2, NB, NR])
        um, ugm = zt, zg
        r0 = sb(st, "s_r0", [P, DG])
        ug = sb(st, "s_ug", [P, DG])
        mm, ev = sem("mm2"), Count(sem("ev2"))
        vc = m.v_c[:, 16:18, :]
        with nc.Block() as block:
            @block.tensor
            def _(pe):
                for j in range(2):
                    for p2 in range(2):
                        for pp in range(2):
                            r = slice(64 * pp, 64 * pp + 64)
                            ins = nc.tensor.matmul(ps[r, 2 * j + p2, :], m.ar_s[:, p2, j, pp, :],
                                                   mst[:, 2 * p2 + pp].rearrange("p b v -> p (b v)"),
                                                   start=True, stop=True)
                        ins.then_inc(mm, 1)
                for j in range(2):
                    for half in range(2):
                        for h in range(HG):
                            r = slice(NS * h, NS * h + NS)
                            ins = nc.tensor.matmul(ps[r, 4 + 2 * j + half, :], ks_c[:, j, r],
                                                   sst[:, h, 4 * half:4 * half + 4, :].rearrange("p b v -> p (b v)"),
                                                   start=True, stop=True, tile_position=(0, NS * h))
                        ins.then_inc(mm, 1)

            @block.vector
            def _(dve):
                bm = over(m.bmask[:, :], NR, 2)
                for j in range(2):
                    for p2 in range(2):
                        dve.wait_ge(mm, 2 * j + p2 + 1)
                        ins = nc.vector.tensor_tensor(zt[:, p2], ps[:, 2 * j + p2, :].rearrange("p (b v) -> p b v", b=NB),
                                                      bm, ALU.mult)
                    ev.step(dve, ins)
                    ev.step(dve, nc.vector.tensor_reduce(zs[:, j], zt[:, :, :, :].rearrange("p q b v -> p q v b"), AXX,
                                                         ALU.add))
                bm = over(m.bmask[:, :], DG, 2)
                for j in range(2):
                    dve.wait_ge(mm, 4 + 2 * j + 2)
                    for half in range(2):
                        b4 = slice(4 * half, 4 * half + 4)
                        ins = nc.vector.tensor_tensor(zg[:, b4], ps[:, 4 + 2 * j + half, :].rearrange(
                            "p (b v) -> p b v", b=4), over(m.bmask[:, b4], DG, 2), ALU.mult)
                    ev.step(dve, ins)
                    ev.step(dve, nc.vector.tensor_reduce(zgs[:, j], zg[:, :, :].rearrange("p b v -> p v b"), AXX,
                                                         ALU.add))
                nc.vector.tensor_tensor(vm[:, :, :, :], over(vc, NB, 2), over(over(m.bmask[:, :], NR, 2), 2), ALU.mult)
                nc.vector.scalar_tensor_tensor(r0[:, :], zgs[:, 0, :], m.sc[:, S_NEG, 8:9], kv[:, 1, :], ALU.mult,
                                               ALU.add)

        mm, ev = sem("mm3"), sem("ev3")
        with nc.Block() as block:
            @block.tensor
            def _(pe):
                for p2 in range(2):
                    ins = nc.tensor.matmul(ps[:, 0, 64 * p2:64 * p2 + 64], mk[:, p2, 0, :], vc[:, p2, :], start=True,
                                           stop=True)
                ins.then_inc(mm, 1)
                nc.tensor.matmul(ps[:, 1, 0:DG], tinv[:, 0, :], r0[:, :], start=True, stop=True).then_inc(mm, 1)
                pe.wait_ge(ev, 1)
                for p2 in range(2):
                    ins = nc.tensor.matmul(ps[:, 2, 64 * p2:64 * p2 + 64], tinv[:, 1 + p2, :], rr[:, p2, :], start=True,
                                           stop=True)
                ins.then_inc(mm, 1)
                pe.wait_ge(ev, 2)
                nc.tensor.matmul(ps[:, 3, 0:DG], gmx[:, 1, :], ug[:, :], start=True, stop=True).then_inc(mm, 1)
                pe.wait_ge(ev, 3)
                for p2 in range(2):
                    nc.tensor.matmul(ps[:, 4, 64 * p2:64 * p2 + 64], mk[:, p2, 1, :], vc[:, p2, :], start=True,
                                     stop=False)
                    ins = nc.tensor.matmul(ps[:, 4, 64 * p2:64 * p2 + 64], mb[:, p2, 1, :], un[:, p2, :], start=False,
                                           stop=True)
                ins.then_inc(mm, 1)

            @block.vector
            def _(dve):
                dve.wait_ge(mm, 1)
                nc.vector.tensor_tensor(rr[:, :, :].rearrange("p q v -> p (q v)"), ps[:, 0, 0:P],
                                        zs[:, 0].rearrange("p q v -> p (q v)"), ALU.add).then_inc(ev, 1)
                dve.wait_ge(mm, 2)
                nc.vector.tensor_scalar(ug[:, :], ps[:, 1, 0:DG], m.sc[:, S_BE, 8:9], None, ALU.mult).then_inc(ev, 1)
                dve.wait_ge(mm, 3)
                nc.vector.tensor_scalar(un[:, :, :].rearrange("p q v -> p (q v)"), ps[:, 2, 0:P], -1.0, None,
                                        ALU.mult).then_inc(ev, 1)
                dve.wait_ge(mm, 4)
                nc.vector.scalar_tensor_tensor(m.y_g[:, 8, :], zgs[:, 1, :], m.sc[:, S_EG, 8:9], ps[:, 3, 0:DG],
                                               ALU.mult, ALU.add)
                nc.vector.tensor_tensor(ugm[:, :, :], over(ug[:, :], NB), over(m.bmask[:, :], DG, 2), ALU.mult)
                dve.wait_ge(ev, 3)
                nc.vector.tensor_tensor(um[:, :, :, :], over(un[:, :, :], NB, 2), over(over(m.bmask[:, :], NR, 2), 2),
                                        ALU.mult)
                dve.wait_ge(mm, 5)
                nc.vector.tensor_tensor(m.y_r[:, 16:18, :].rearrange("p q v -> p (q v)"), ps[:, 4, 0:P],
                                        zs[:, 1].rearrange("p q v -> p (q v)"), ALU.add)

        mm, ev, ev2 = sem("mm4"), Count(sem("ev4")), sem("ev5")
        with nc.Block() as block:
            @block.tensor
            def _(pe):
                for p in range(PAIRS):
                    p2, r = p // 2, slice(64 * (p % 2), 64 * (p % 2) + 64)
                    nc.tensor.matmul(ps[:, p, :], tmt[r, 1, p2, :], vm[r, p2].rearrange("p b v -> p (b v)"), start=True,
                                     stop=False)
                    nc.tensor.matmul(ps[:, p, :], tmt[r, 0, p2, :], um[r, p2].rearrange("p b v -> p (b v)"),
                                     start=False, stop=True).then_inc(mm, 1)
                for h in range(HG):
                    r = slice(NS * h, NS * h + NS)
                    if h >= 2:
                        pe.wait_ge(ev2, h - 1)
                    for half in range(2):
                        ins = nc.tensor.matmul(ps[:, 4 + 2 * (h % 2) + half, :], kv[r, 0, :],
                                               ugm[r, 4 * half:4 * half + 4, :].rearrange("p b v -> p (b v)"),
                                               start=True, stop=True, tile_position=(NS * h, 0))
                    ins.then_inc(mm, 1)

            @block.vector
            def _(dve):
                for h in range(HG):
                    ins = nc.vector.tensor_tensor(sst[:, h], sst[:, h], over(m.glb[:, NB * h:NB * h + NB], DG, 2),
                                                  ALU.mult)
                for p in range(PAIRS):
                    dve.wait_ge(mm, p + 1)
                    ins = nc.vector.tensor_tensor(mst[:, p].rearrange("p b v -> p (b v)"), ps[:, p, :],
                                                  mst[:, p].rearrange("p b v -> p (b v)"), ALU.add)
                ev.step(dve, ins)
                ev.step(dve, nc.vector.tensor_tensor(mst[:, :, :, :], mst[:, :, :, :],
                                                     over(m.plast[:, :, NCR:], NR, 3), ALU.mult))
                for h in range(2):
                    r = slice(64 * h, 64 * h + 64)
                    ins = nc.vector.tensor_copy(stage_t[r, :, :, r], mst[r, :, :, :])
                for h in range(HG):
                    dve.wait_ge(mm, 5 + h)
                    for half in range(2):
                        v = sst[:, h, 4 * half:4 * half + 4, :].rearrange("p b v -> p (b v)")
                        ins = nc.vector.tensor_tensor(v, ps[:, 4 + 2 * (h % 2) + half, :], v, ALU.add)
                    ins.then_inc(ev2, 1)
        turned, stored = sem("turned2"), sem("stored")
        with nc.Block() as block:
            turn_states(block)
        with nc.Block() as block:
            @block.sync
            def _(sp):
                for p in range(PAIRS):
                    sp.dma_start(out[8][0].rearrange("b h v k -> (h v) b k")[P * p:P * p + P], mst[:, p]).then_inc(
                        stored, 16)
                for h in range(HG):
                    sp.dma_start(out[10][0, :, h].rearrange("b k v -> k b v"), sst[:, h]).then_inc(stored, 16)
                sp.wait_ge(stored, 16 * 8)


def prompt_chunks(nc, out, sb, ps, ident, ones, m):
    with ExitStack() as st:
        sem = semaphores(nc, st, "pc")
        NU, NG = NCR * PAIRS, 2 * HG
        mb = m.pr[:, :, :].rearrange("p i w -> p (i w)")[:, 0:NU * 2 * P].rearrange(
            "p (u j t) -> p u j t", u=NU, j=2)
        tinv = m.pg[:, :, :].rearrange("p i w -> p (i w)")[:, 0:(NU + NG) * P].rearrange(
            "p (u t) -> p u t", u=NU + NG)
        mk = sb(st, "mk", [P, NU, 2, P])
        gmx = sb(st, "gmx", [P, NG, 2, P])
        kt = sb(st, "kt", [P, NG, P])
        vt = sb(st, "vt", [P, NG, P])
        be_tm = mb[:, :, 0, :]

        with ExitStack() as s1:
            gb = sb(s1, "gb", [P, NG, P])
            dt = sb(s1, "dt", [P, NG, P])
            dtm = sb(s1, "dtm", [P, NG, 2, P])
            gb_ok, pe_done, dd, de, dch = sem("gb"), sem("pe"), sem("dd"), sem("de"), Count(sem("dch"))
            v_done, a_done = sem("v_done"), sem("a_done")
            order = ([("row", 0), ("row", 1), ("kt", 0), ("kt", 1), ("vt", 0), ("vt", 1)]
                     + [("mb", c, h) for c in range(2) for h in range(2)] + [("gm", i, h) for i in range(2)
                                                                             for h in range(2)]
                     + [("mk", c, h) for c in range(2) for h in range(2)]
                     + [(w, c, h) for w in ("mb", "mk") for c in range(2, NCR) for h in range(2)])
            by_act = [q for q in order if q[0] in ("kt", "vt")]
            by_dve = [q for q in order if q not in by_act]
            bank = {q: i % 8 for i, q in enumerate(order)}
            with nc.Block() as block:
                @block.gpsimd
                def _(pool):
                    for u in range(NG):
                        if u:
                            pool.wait_ge(gb_ok, u)
                        nc.gpsimd.tensor_scalar(gb[:, u, :], ones[:], m.sc[:, S_G, u:u + 1], None,
                                                ALU.mult).then_inc(gb_ok, 1)

                @block.tensor
                def _(pe):
                    for i, q in enumerate(order):
                        if i >= 8:
                            old = order[i - 8]
                            if old in by_act:
                                pe.wait_ge(a_done, by_act.index(old) + 1)
                            else:
                                pe.wait_ge(v_done, by_dve.index(old) + 1)
                        b = bank[q]
                        if q[0] == "row":
                            for h in range(HG):
                                pe.wait_ge(gb_ok, 4 * q[1] + h + 1)
                                ins = nc.tensor.matmul(ps[:, b, P * h:P * h + P], gb[:, 4 * q[1] + h, :], m.tri[:],
                                                       start=True, stop=True)
                        elif q[0] in ("kt", "vt"):
                            src = m.qk[:, 0] if q[0] == "kt" else m.gv
                            for h in range(HG):
                                ins = nc.tensor.transpose(ps[:, b, P * h:P * h + P], src[:, h, P * q[1]:P * q[1] + P],
                                                          ident[:])
                        elif q[0] == "gm":
                            t = slice(P * q[1], P * q[1] + P)
                            for j in range(2):
                                h = 2 * q[2] + j
                                ins = nc.tensor.matmul(ps[:, b, 256 * j:256 * j + 256].rearrange(
                                    "p (j t) -> p j t", j=2), m.qk[:, 0, h, t], m.qk[:, :, h, t], start=True, stop=True)
                        else:
                            w = m.be_e if q[0] == "mb" else m.ka_e
                            for j in range(2):
                                u = PAIRS * q[1] + 2 * q[2] + j
                                ins = nc.tensor.matmul(ps[:, b, 256 * j:256 * j + 256], w[:, u, :],
                                                       m.ar_e[:, u].rearrange("p j t -> p (j t)"), start=True, stop=True)
                        ins.then_inc(pe_done, 1)

                @block.vector
                def _(dve):
                    for q in by_dve:
                        dve.wait_ge(pe_done, order.index(q) + 1)
                        b = ps[:, bank[q], :]
                        if q[0] == "row":
                            for h in range(HG):
                                u = 4 * q[1] + h
                                ins = nc.vector.tensor_scalar(dt[:, u, :], b[:, P * h:P * h + P],
                                                              m.sc[:, S_GC, u:u + 1], 0.0, ALU.subtract, ALU.min)
                            ins.then_inc(v_done, 1)
                        elif q[0] == "gm":
                            if q[1:] == (0, 0):
                                dve.wait_ge(de, 2)
                                for u in range(NG):
                                    nc.vector.scalar_tensor_tensor(dtm[:, u, 0, :], dt[:, u, :],
                                                                   m.sc[:, S_BE, u:u + 1], m.stri[:], ALU.mult, ALU.mult)
                                dch.step(dve, nc.vector.tensor_tensor(dtm[:, :, 1, :], dt[:, :, :],
                                                                      over(m.tri[:], NG), ALU.mult))
                            u = 4 * q[1] + 2 * q[2]
                            nc.vector.tensor_tensor(gmx[:, u:u + 2].rearrange("p u j t -> p (u j t)"), b,
                                                    dtm[:, u:u + 2].rearrange("p u j t -> p (u j t)"),
                                                    ALU.mult).then_inc(v_done, 1)
                        else:
                            u = PAIRS * q[1] + 2 * q[2]
                            dst = mb if q[0] == "mb" else mk
                            nc.vector.tensor_tensor(dst[:, u:u + 2], b.rearrange("p (u j t) -> p u j t", u=2, j=2),
                                                    over(m.tr64[:, :, :], 2), ALU.mult).then_inc(v_done, 1)

                @block.scalar
                def _(act):
                    for q in by_act:
                        act.wait_ge(pe_done, order.index(q) + 1)
                        b = ps[:, bank[q], :]
                        for h in range(HG):
                            u = 4 * q[1] + h
                            if q[0] == "kt":
                                ins = nc.scalar.activation(kt[:, u, :], b[:, P * h:P * h + P], ACT.Copy,
                                                           scale=m.sc[:, S_KT, u:u + 1])
                            else:
                                ins = nc.scalar.copy(vt[:, u, :], b[:, P * h:P * h + P])
                        ins.then_inc(a_done, 1)
                    act.wait_ge(v_done, 2)
                    for i in range(2):
                        nc.scalar.activation(dt[:, 4 * i:4 * i + 4], dt[:, 4 * i:4 * i + 4], ACT.Exp).then_inc(de, 1)

        for i in range(2):
            invert(nc, sb, ps, ident, m, f"pi{i}",
                   [(mb[:, 8 * i + 4 * c:8 * i + 4 * c + 4, 0, :], tinv[:, 8 * i + 4 * c:8 * i + 4 * c + 4, :], 4, 6)
                    for c in range(2)]
                   + [(gmx[:, 4 * i:4 * i + 4, 0, :], tinv[:, NU + 4 * i:NU + 4 * i + 4, :], 4, 7)])

        ka_tm = sb(st, "ka_tm", [P, NU, P])
        turned = sem("turned")
        with nc.Block() as block:
            @block.tensor
            def _(pe):
                for q in range(8):
                    for j in range(4):
                        src = (m.be_e, m.ka_e)[q % 2]
                        ins = nc.tensor.transpose(ps[:, q, P * j:P * j + P], src[:, 4 * (q // 2) + j, :], ident[:])
                    ins.then_inc(turned, 1)

            def gather(eng, copy, odd, dst):
                for q in range(odd, 8, 2):
                    eng.wait_ge(turned, q + 1)
                    u = 4 * (q // 2)
                    copy(dst[:, u:u + 4, :], ps[:, q, :].rearrange("p (u k) -> p u k", u=4))

            @block.vector
            def _(dve):
                gather(dve, nc.vector.tensor_copy, 0, be_tm)

            @block.scalar
            def _(act):
                gather(act, nc.scalar.copy, 1, ka_tm)

        ms = sb(st, "ms", [P, 2, PAIRS, NR])
        ss = sb(st, "ss", [P, HG, DG])
        rr = sb(st, "rr", [P, PAIRS, NR])
        un = sb(st, "un", [P, PAIRS, NR])
        r0 = sb(st, "r0", [P, HG, DG])
        ug = sb(st, "ug", [P, HG, DG])
        qs = sb(st, "qs", [P, HG, DG])
        r_done, u_done, y_done, m_done = (sem(n) for n in ("r_done", "u_done", "y_done", "m_done"))
        r_ok, u_ok, y_ok, m_ok = (sem(n) for n in ("r_ok", "u_ok", "y_ok", "m_ok"))
        ks_done, w_done, o_done, s_done = (sem(n) for n in ("ks_done", "w_done", "o_done", "s_done"))
        r0_ok, qs_ok, ug_ok, o_ok, s_ok = (sem(n) for n in ("r0_ok", "qs_ok", "ug_ok", "o_ok", "s_ok"))
        mch = Count(sem("mch"))

        with nc.Block() as block:
            @block.tensor
            def _(pe):
                def each(w, sem_):
                    for j in range(HG):
                        prods = w(j)
                        for k, (dst, lhs, rhs) in enumerate(prods):
                            ins = nc.tensor.matmul(dst, lhs, rhs, start=(k == 0), stop=(k == len(prods) - 1))
                    ins.then_inc(sem_, 1)

                for c in range(NCR):
                    i, u0 = c // 2, PAIRS * c
                    cols = [slice(NR * p, NR * p + NR) for p in range(PAIRS)]
                    if c:
                        pe.wait_ge(m_ok, c)
                    each(lambda p: ([(ps[:, 0, cols[p]], m.ar_e[:, u0 + p, 0, :], ms[:, c % 2, p, :])] if c else []) + [
                        (ps[:, 0, cols[p]], mk[:, u0 + p, 0, :], m.v_c[:, u0 + p, :])], r_done)
                    if c == 2:
                        pe.wait_ge(s_ok, 1)
                        for j, b in ((0, 4), (1, 5)):
                            for h in range(HG):
                                ins = nc.tensor.matmul(ps[:, b, P * h:P * h + P], m.qk[:, j, h, P:2 * P], ss[:, h, :],
                                                       start=True, stop=True)
                            ins.then_inc(ks_done, 1)
                    if c % 2:
                        pe.wait_ge(ug_ok, i + 1)
                        if i:
                            pe.wait_ge(o_ok, 1)
                        each(lambda h: [(ps[:, 7, P * h:P * h + P], gmx[:, 4 * i + h, 1, :], ug[:, h, :])], o_done)
                    pe.wait_ge(r_ok, c + 1)
                    each(lambda p: [(ps[:, 1, cols[p]], tinv[:, u0 + p, :], rr[:, p, :])], u_done)
                    if c % 2 == 0:
                        if i:
                            pe.wait_ge(r0_ok, 1)
                        src = r0 if i else vt
                        each(lambda h: [(ps[:, 6, P * h:P * h + P], tinv[:, NU + 4 * i + h, :], src[:, h, :])],
                             w_done)
                    else:
                        if i:
                            pe.wait_ge(r0_ok, 1)
                        each(lambda h: [(ps[:, 4, P * h:P * h + P], kt[:, 4 * i + h, :], ug[:, h, :])], s_done)
                    pe.wait_ge(u_ok, c + 1)
                    if c:
                        pe.wait_ge(y_ok, c)
                    each(lambda p: [(ps[:, 3, cols[p]], ka_tm[:, u0 + p, :], m.v_c[:, u0 + p, :]),
                                       (ps[:, 3, cols[p]], be_tm[:, u0 + p, :], un[:, p, :])], m_done)
                    each(lambda p: ([(ps[:, 2, cols[p]], m.ar_e[:, u0 + p, 1, :], ms[:, c % 2, p, :])] if c else []) + [
                        (ps[:, 2, cols[p]], mk[:, u0 + p, 1, :], m.v_c[:, u0 + p, :]),
                        (ps[:, 2, cols[p]], mb[:, u0 + p, 1, :], un[:, p, :])], y_done)

            def flat(ap):
                return ap.rearrange("p q v -> p (q v)")

            @block.scalar
            def _(act):
                for c in range(NCR):
                    i = c // 2
                    act.wait_ge(r_done, c + 1)
                    nc.scalar.copy(flat(rr[:, :, :]), ps[:, 0, 0:256]).then_inc(r_ok, 1)
                    if c == 2:
                        act.wait_ge(ks_done, 2)
                        for h in range(HG):
                            ins = nc.scalar.activation(qs[:, h, :], ps[:, 5, P * h:P * h + P], ACT.Copy,
                                                       scale=m.sc[:, S_EG, 4 + h:5 + h])
                        ins.then_inc(qs_ok, 1)
                    if c == 1:
                        act.wait_ge(o_done, 1)
                        nc.scalar.copy(flat(m.y_g[:, 0:4, :]), ps[:, 7, :]).then_inc(o_ok, 1)
                    act.wait_ge(y_done, c + 1)
                    nc.scalar.copy(flat(m.y_r[:, PAIRS * c:PAIRS * c + PAIRS, :]), ps[:, 2, 0:256]).then_inc(y_ok, 1)

            @block.vector
            def _(dve):
                for c in range(NCR):
                    i = c // 2
                    if c == 2:
                        dve.wait_ge(ks_done, 1)
                        for h in range(HG):
                            ins = nc.vector.scalar_tensor_tensor(r0[:, h, :], ps[:, 4, P * h:P * h + P],
                                                                 m.sc[:, S_NEG, 4 + h:5 + h], vt[:, 4 + h, :], ALU.mult,
                                                                 ALU.add)
                        ins.then_inc(r0_ok, 1)
                    dve.wait_ge(u_done, c + 1)
                    nc.vector.tensor_scalar(flat(un[:, :, :]), ps[:, 1, 0:256], -1.0, None, ALU.mult).then_inc(u_ok, 1)
                    if c % 2 == 0:
                        dve.wait_ge(w_done, i + 1)
                        for h in range(HG):
                            ins = nc.vector.tensor_scalar(ug[:, h, :], ps[:, 6, P * h:P * h + P],
                                                          m.sc[:, S_BE, 4 * i + h:4 * i + h + 1], None, ALU.mult)
                        ins.then_inc(ug_ok, 1)
                    dve.wait_ge(m_done, c + 1)
                    new = ms[:, (c + 1) % 2]
                    if c == 0:
                        mch.step(dve, nc.vector.tensor_copy(flat(new), ps[:, 3, 0:256]))
                    else:
                        mch.step(dve, nc.vector.tensor_tensor(flat(new), ps[:, 3, 0:256], flat(ms[:, c % 2]), ALU.add))
                    nc.vector.tensor_tensor(new, new, over(m.plast[:, :, c], NR, 2),
                                            ALU.mult).then_inc(m_ok, 1)
                    if c % 2:
                        dve.wait_ge(s_done, i + 1)
                        if i == 0:
                            nc.vector.tensor_copy(flat(ss[:, :, :]), ps[:, 4, :]).then_inc(s_ok, 1)
                        else:
                            for h in range(HG):
                                nc.vector.scalar_tensor_tensor(ss[:, h, :], ss[:, h, :], m.sc[:, S_GL, 4 + h:5 + h],
                                                               ps[:, 4, P * h:P * h + P], ALU.mult, ALU.add)
                            dve.wait_ge(o_done, 2)
                            dve.wait_ge(qs_ok, 1)
                            nc.vector.tensor_tensor(flat(m.y_g[:, 4:8, :]), ps[:, 7, :], flat(qs[:, :, :]), ALU.add)

        spread, turned, kept, stored, zeroed = (sem(n) for n in ("spread", "turned2", "kept", "stored", "zeroed"))
        with nc.Block() as block:
            @block.vector
            def _(dve):
                dve.wait_ge(zeroed, 1)
                for h in range(2):
                    r = slice(64 * h, 64 * h + 64)
                    ins = nc.vector.tensor_copy(r0[r, :, r], ms[r, NCR % 2, :, :])
                ins.then_inc(spread, 1)
                dve.wait_ge(turned, 1)
                for h in range(2):
                    r = slice(64 * h, 64 * h + 64)
                    ins = nc.vector.tensor_copy(rr[r, :, :], ps[r, 0, :].rearrange("p (q k) -> p q k", q=4)[:, :, r])
                ins.then_inc(kept, 1)

            @block.gpsimd
            def _(pool):
                nc.gpsimd.memset(r0[:, :, :], 0.0).then_inc(zeroed, 1)

            @block.tensor
            def _(pe):
                pe.wait_ge(spread, 1)
                for p in range(PAIRS):
                    ins = nc.tensor.transpose(ps[:, 0, P * p:P * p + P], r0[:, p, :], ident[:])
                ins.then_inc(turned, 1)

            @block.sync
            def _(sp):
                sp.dma_start(out[4][0, 0].rearrange("h k v -> k h v"), ss[:, :, :]).then_inc(stored, 16)
                sp.wait_ge(kept, 1)
                sp.dma_start(out[2][0, 0].rearrange("(q h) v k -> (h v) q k", h=2), rr[:, :, :]).then_inc(stored, 16)
                sp.wait_ge(stored, 32)


def read_out(nc, sb, ps, ident, eps, m):
    with ExitStack() as st:
        sem = semaphores(nc, st, "ro")
        y, g = m.y_r, m.y_g
        ye = sb(st, "ye", [P, 18, P])
        sq = sb(st, "sq", [P, 18 * NR])
        mom = sb(st, "mom", [P, 4, 18])
        zeroed, v_ok, root, spread, turned, kept = (sem(n) for n in ("zeroed", "var", "root", "spread", "turned", "kept"))
        d = Count(sem("dve"))
        gok = sem("g_ready")
        sqr = sq[:, :].rearrange("p (u v) -> p u v", v=NR)
        sqg = sq[:, :].rearrange("p (u v) -> p u v", v=DG)
        with nc.Block() as block:
            @block.gpsimd
            def _(pool):
                nc.gpsimd.memset(ye[:, :, :], 0.0).then_inc(zeroed, 1)

            @block.scalar
            def _(act):
                act.wait_ge(v_ok, 1)
                nc.scalar.activation(mom[:, 2, :], mom[:, 1, :], ACT.Sqrt, bias=eps[:, 1:2], scale=1.0 / NR).then_inc(
                    root, 1)
                act.wait_ge(v_ok, 2)
                nc.scalar.activation(mom[:, 3, 0:9], mom[:, 3, 0:9], ACT.Sqrt, bias=eps[:, 0:1],
                                     scale=1.0 / DG).then_inc(root, 1)

            @block.vector
            def _(dve):
                d.step(dve, nc.vector.tensor_reduce(mom[:, 0, :], y[:, :, :], AXX, ALU.add))
                d.step(dve, nc.vector.tensor_scalar(mom[:, 0, :], mom[:, 0, :], 1.0 / NR, None, ALU.mult))
                d.step(dve, nc.vector.tensor_tensor(y[:, :, :], y[:, :, :], over(mom[:, 0, :], NR, 2), ALU.subtract))
                d.step(dve, nc.vector.tensor_tensor(sqr, y[:, :, :], y[:, :, :], ALU.mult))
                nc.vector.tensor_reduce(mom[:, 1, :], sqr, AXX, ALU.add).then_inc(v_ok, 1)
                dve.wait_ge(v_ok, 1)
                d.step(dve, nc.vector.tensor_tensor(sqg, g[:, :, :], g[:, :, :], ALU.mult))
                nc.vector.tensor_reduce(mom[:, 3, 0:9], sqg, AXX, ALU.add).then_inc(v_ok, 1)
                dve.wait_ge(root, 1)
                d.step(dve, nc.vector.reciprocal(mom[:, 2, :], mom[:, 2, :]))
                dve.wait_ge(zeroed, 1)
                for h in range(2):
                    r = slice(64 * h, 64 * h + 64)
                    nc.vector.tensor_tensor(ye[r, 0:16, r], y[r, 0:16, :], over(mom[r, 2, 0:16], NR, 2), ALU.mult)
                for q in range(4):
                    r, h = slice(NS * q, NS * q + NS), q % 2
                    ins = nc.vector.tensor_tensor(ye[r, 16:18, 64 * h:64 * h + 64], y[r, 16:18, :],
                                                  over(mom[r, 2, 16:18], NR, 2), ALU.mult)
                ins.then_inc(spread, 1)
                dve.wait_ge(root, 2)
                d.step(dve, nc.vector.reciprocal(mom[:, 3, 0:9], mom[:, 3, 0:9]))
                nc.vector.tensor_tensor(g[:, :, :], g[:, :, :], over(mom[:, 3, 0:9], DG, 2), ALU.mult).then_inc(gok, 1)
                yT = m.yT
                for c in range(NCR):
                    dve.wait_ge(turned, c + 1)
                    for h in range(2):
                        r = slice(64 * h, 64 * h + 64)
                        nc.vector.tensor_copy(yT[r, 0:4, CR * c:CR * c + CR],
                                              ps[r, c, :].rearrange("p (q t) -> p q t", q=4)[:, :, r])
                dve.wait_ge(turned, 5)
                for h in range(2):
                    r = slice(64 * h, 64 * h + 64)
                    ins = nc.vector.tensor_copy(yT[r, 0:4, TP:],
                                                ps[r, 4, 0:256].rearrange("p (q t) -> p q t", q=4)[
                                                    :, :, NS * h:NS * h + NS])
                d.step(dve, ins)
                for p in range(PAIRS):
                    ins = nc.vector.tensor_scalar(yT[:, p, :], yT[:, p, :], m.vec[:, V_LW + p:V_LW + p + 1],
                                                  m.vec[:, V_LB + p:V_LB + p + 1], ALU.mult, ALU.add)
                d.step(dve, ins)
                d.step(dve, nc.vector.tensor_tensor(yT[:, 0:4, :], yT[:, 0:4, :], m.bv[:, :, :], ALU.add))
                nc.vector.tensor_tensor(yT[:, 0:4, :], yT[:, 0:4, :], m.gate[:, :, :], ALU.mult)
                gw = m.vec[:, V_GN:V_GN + 1]
                for i in range(2):
                    dve.wait_ge(turned, 6 + i)
                    nc.vector.tensor_scalar(yT[:, 4:8, P * i:P * i + P], ps[:, 5 + i, :].rearrange(
                        "p (h t) -> p h t", h=HG), gw, None, ALU.mult)
                dve.wait_ge(turned, 8)
                d.step(dve, nc.vector.tensor_scalar(yT[:, 4:8, TP:], ps[:, 7, 0:P].rearrange("p (h t) -> p h t", h=HG),
                                                    gw, None, ALU.mult))
                nc.vector.tensor_tensor(yT[:, 4:8, :], yT[:, 4:8, :], m.zt[:, :, :], ALU.mult)

            @block.tensor
            def _(pe):
                pe.wait_ge(spread, 1)
                for c in range(NCR):
                    for p in range(PAIRS):
                        ins = nc.tensor.transpose(ps[:, c, P * p:P * p + P], ye[:, PAIRS * c + p, :], ident[:])
                    ins.then_inc(turned, 1)
                for p2 in range(2):
                    ins = nc.tensor.transpose(ps[:, 4, P * p2:P * p2 + P], ye[:, 16 + p2, :], ident[:])
                ins.then_inc(turned, 1)
                pe.wait_ge(gok, 1)
                for i in range(2):
                    for h in range(HG):
                        ins = nc.tensor.transpose(ps[:, 5 + i, P * h:P * h + P], g[:, 4 * i + h, :], ident[:])
                    ins.then_inc(turned, 1)
                nc.tensor.transpose(ps[:, 7, 0:P], g[:, 8, :], ident[:]).then_inc(turned, 1)


def project_add(nc, sb, ps, x, yT, w, name):
    with ExitStack() as st:
        sem = semaphores(nc, st, name)
        wt = sb(st, f"{name}_w", [P, KC, D])
        w_in = [sem(f"w_in{j}") for j in range(2)]
        summed, added = sem("summed"), sem("added")
        parts = [(i, half) for half in range(2) for i in range(3)]
        with nc.Block() as block:
            @block.sync
            def _(sp):
                v = w[0].rearrange("(c p) n -> p c n", c=KC)
                for j in range(2):
                    cols = slice(512 * j, 512 * j + 512)
                    sp.dma_start(wt[:, :, cols], v[:, :, cols]).then_inc(w_in[j], 16)

            @block.tensor
            def _(pe):
                for k, (i, half) in enumerate(parts):
                    pe.wait_ge(w_in[half], 16)
                    t0, n = TILES[i]
                    for c in range(KC):
                        ins = nc.tensor.matmul(ps[:n, k, :], yT[:, c, t0:t0 + n], wt[:, c, 512 * half:512 * half + 512],
                                               start=(c == 0), stop=(c == KC - 1))
                    ins.then_inc(summed, 1)

            @block.vector
            def _(dve):
                for k, (i, half) in enumerate(parts):
                    dve.wait_ge(summed, k + 1)
                    v = x[:TILES[i][1], i, 512 * half:512 * half + 512]
                    nc.vector.tensor_tensor(v, v, ps[:TILES[i][1], k, :], ALU.add)


def attention(nc, a, out, outer, sb, ps, ident, ones, x, g8, stat, eps, norm_stage):
    with ExitStack() as st:
        sem = semaphores(nc, st, "at")
        h_tm = sb(st, "ah_tm", [P, 3, D])
        hT = sb(st, "ahT", [P, KC, T])
        memx = sb(st, "memx", [P, 2, D])
        kT = sb(st, "kT", [P, KC, NM])
        qT = sb(st, "qT", [P, KC, T])
        oT = sb(st, "oT", [P, KC, T])
        k_tm = h_tm
        loaded = sem("mem_in")
        with nc.Block() as block:
            @block.sync
            def _(sp):
                sp.dma_start(memx[:, :, :], a["mem_prompt"][0].rearrange("(i p) d -> p i d", p=P)).then_inc(loaded, 16)
                sp.wait_ge(loaded, 16)
        norm_stage("mem", memx, TILES[:2], 2, hT, h_tm)

        with ExitStack() as s1:
            wk = sb(s1, "wk", [P, KC, D])
            wv = sb(s1, "wv", [P, KC, D])
            w_in, summed, v_ok, a_ok, turned, stored = (
                sem(n) for n in ("kv_in", "kv_sum", "v_ok", "a_ok", "k_turned", "kv_stored"))
            parts = [(w, i, half) for w in range(2) for i in range(2) for half in range(2)]
            with nc.Block() as block:
                @block.sync
                def _(sp):
                    for w, n in ((wk, "wk_x"), (wv, "wv_x")):
                        sp.dma_start(w[:, :, :], a[n][0].rearrange("(p c) n -> p c n", c=KC)).then_inc(w_in, 16)
                    sp.wait_ge(v_ok, 4)
                    sp.dma_start(out[6][0, 0].rearrange("(i p) h d -> p i (h d)", p=P), k_tm[:, 0:2, :]).then_inc(
                        stored, 16)
                    sp.wait_ge(a_ok, 4)
                    sp.dma_start(out[7][0, 0].rearrange("(i p) h d -> p i (h d)", p=P), memx[:, :, :]).then_inc(
                        stored, 16)
                    sp.wait_ge(stored, 32)

                @block.tensor
                def _(pe):
                    pe.wait_ge(w_in, 32)
                    for k, (w, i, half) in enumerate(parts):
                        for c in range(KC):
                            ins = nc.tensor.matmul(ps[:, k, :], hT[:, c, P * i:P * i + P],
                                                   (wk, wv)[w][:, c, 512 * half:512 * half + 512], start=(c == 0),
                                                   stop=(c == KC - 1))
                        ins.then_inc(summed, 1)
                    for q in range(4):
                        pe.wait_ge(v_ok, 4)
                        for j in range(2):
                            for i in range(2):
                                n = 2 * q + j
                                ins = nc.tensor.transpose(ps[:, q, 256 * j + P * i:256 * j + P * i + P],
                                                          k_tm[:, i, P * n:P * n + P], ident[:])
                        ins.then_inc(turned, 1)

                @block.vector
                def _(dve):
                    for k in range(4):
                        _, i, half = parts[k]
                        dve.wait_ge(summed, k + 1)
                        nc.vector.tensor_copy(k_tm[:, i, 512 * half:512 * half + 512], ps[:, k, :]).then_inc(v_ok, 1)
                    for q in range(4):
                        dve.wait_ge(turned, q + 1)
                        nc.vector.tensor_copy(kT[:, 2 * q:2 * q + 2, :].rearrange("p n m -> p (n m)"), ps[:, q, :])

                @block.scalar
                def _(act):
                    for k in range(4, 8):
                        _, i, half = parts[k]
                        act.wait_ge(summed, k + 1)
                        nc.scalar.copy(memx[:, i, 512 * half:512 * half + 512], ps[:, k, :]).then_inc(a_ok, 1)

        norm_stage("cross", x, TILES, 1, hT, h_tm)

        with ExitStack() as s1:
            wq = sb(s1, "wq", [P, KC, D])
            w_in, summed, q_ok = sem("q_in"), sem("q_sum"), sem("q_ok")
            with nc.Block() as block:
                @block.sync
                def _(sp):
                    sp.dma_start(wq[:, :, :], a["wq_x"][0].rearrange("(p c) n -> p c n", c=KC)).then_inc(w_in, 16)

                @block.tensor
                def _(pe):
                    pe.wait_ge(w_in, 16)
                    for n in range(KC):
                        for c in range(KC):
                            ins = nc.tensor.matmul(ps[:, n, 0:T], wq[:, c, P * n:P * n + P], hT[:, c, :],
                                                   start=(c == 0), stop=(c == KC - 1))
                        ins.then_inc(summed, 1)

                @block.scalar
                def _(act):
                    for n in range(KC):
                        act.wait_ge(summed, n + 1)
                        nc.scalar.mul(qT[:, n, :], ps[:, n, 0:T], DX ** -0.5)
        prompt_attention(nc, sb, ps, ident, qT, kT, memx, oT)
        sample_attention(nc, a, sb, ps, ident, qT, oT)
        project_add(nc, sb, ps, x, oT, a["wo_x"], "wo")


def prompt_attention(nc, sb, ps, ident, qT, kT, v, oT):
    with ExitStack() as st:
        sem = semaphores(nc, st, "pa")
        pr = sb(st, "probs", [P, 8, NM])
        pT = sb(st, "probsT", [P, HX, 2, TP])
        mx = sb(st, "pa_mx", [P, 3, 8])
        s_done, mx_ok, e_ok, n_ok, turned, t_ok, o_done, d = (
            sem(n) for n in ("scores", "max", "exp", "norm", "turned", "t_ok", "o_done", "chain"))
        ch = Count(d)
        with nc.Block() as block:
            @block.tensor
            def _(pe):
                for u in range(8):
                    h, i = u // 2, u % 2
                    for dc in range(2):
                        ins = nc.tensor.matmul(ps[:, h, NM * i:NM * i + NM], qT[:, 2 * h + dc, P * i:P * i + P],
                                               kT[:, 2 * h + dc, :], start=(dc == 0), stop=(dc == 1))
                    if i:
                        ins.then_inc(s_done, 1)
                for h in range(HX):
                    pe.wait_ge(n_ok, h + 1)
                    for mt in range(2):
                        for i in range(2):
                            ins = nc.tensor.transpose(ps[:, 4 + h, NM * mt + P * i:NM * mt + P * i + P],
                                                      pr[:, 2 * h + i, P * mt:P * mt + P], ident[:])
                    ins.then_inc(turned, 1)
                for h in range(HX):
                    pe.wait_ge(t_ok, h + 1)
                    for dc in range(2):
                        for mt in range(2):
                            c0 = DX * h + P * dc
                            ins = nc.tensor.matmul(ps[:, h, TP * dc:TP * dc + TP], v[:, mt, c0:c0 + P], pT[:, h, mt, :],
                                                   start=(mt == 0), stop=(mt == 1))
                    ins.then_inc(o_done, 1)

            @block.vector
            def _(dve):
                for h in range(HX):
                    dve.wait_ge(s_done, h + 1)
                    nc.vector.tensor_reduce(mx[:, 0, 2 * h:2 * h + 2], ps[:, h, :].rearrange("p (i m) -> p i m", i=2),
                                            AXX, ALU.max, negate=True).then_inc(mx_ok, 1)
                for h in range(HX):
                    dve.wait_ge(e_ok, 2 * h + 2)
                    ch.step(dve, nc.vector.reciprocal(mx[:, 2, 2 * h:2 * h + 2], mx[:, 1, 2 * h:2 * h + 2]))
                    nc.vector.tensor_tensor(pr[:, 2 * h:2 * h + 2, :], pr[:, 2 * h:2 * h + 2, :],
                                            over(mx[:, 2, 2 * h:2 * h + 2], NM, 2), ALU.mult).then_inc(n_ok, 1)
                for h in range(HX):
                    dve.wait_ge(turned, h + 1)
                    nc.vector.tensor_copy(pT[:, h].rearrange("p m t -> p (m t)"), ps[:, 4 + h, :]).then_inc(t_ok, 1)

            @block.scalar
            def _(act):
                for u in range(8):
                    act.wait_ge(mx_ok, u // 2 + 1)
                    nc.scalar.activation(pr[:, u, :], ps[:, u // 2, NM * (u % 2):NM * (u % 2) + NM], ACT.Exp,
                                         bias=mx[:, 0, u:u + 1], accum_out=mx[:, 1, u:u + 1]).then_inc(e_ok, 1)
                for h in range(HX):
                    act.wait_ge(o_done, h + 1)
                    nc.scalar.copy(oT[:, 2 * h:2 * h + 2, 0:TP], ps[:, h, :].rearrange("p (c t) -> p c t", c=2))


def sample_attention(nc, a, sb, ps, ident, qT, oT):
    with ExitStack() as st:
        sem = semaphores(nc, st, "sx")
        NK, NV = 2, 3
        kb = sb(st, "kb", [P, NK, 2, D])
        vb = sb(st, "vb", [P, NV, 2, D])
        kbT = sb(st, "kbT", [P, 2, KC, NM])
        qm = sb(st, "qm", [P, KC, NB, NS])
        pm = sb(st, "pm", [P, 2, NB, P])
        pr = sb(st, "s_probs", [P, NM])
        os_ = sb(st, "s_o", [P, NM])
        mx = sb(st, "sx_mx", [P, 3])
        k_in, v_in = [sem(f"k_in{j}") for j in range(NK)], [sem(f"v_in{j}") for j in range(NV)]
        zeroed, q_ok, turned, kt_v, kt_a, s_done, mx_ok, e_ok, p_ok, pt_done, pm_ok, o_done, o_ok, ot_done = (
            sem(n) for n in ("zeroed", "q_ok", "turned", "kt_v", "kt_a", "s_done", "mx_ok", "e_ok", "p_ok", "pt_done",
                             "pm_ok", "o_done", "o_ok", "ot_done"))
        ch = Count(sem("chain"))
        with nc.Block() as block:
            @block.gpsimd
            def _(pool):
                nc.gpsimd.memset(qm[:, :, :, :], 0.0).then_inc(zeroed, 1)
                pool.wait_ge(zeroed, 1)
                nc.gpsimd.memset(pm[:, :, :, :], 0.0).then_inc(zeroed, 1)

            @block.sync
            def _(sp):
                kd = a["cache_mem_k"][0].rearrange("b (i p) h d -> b p i (h d)", p=P)
                vd = a["cache_mem_v"][0].rearrange("b (i p) h d -> b p i (h d)", p=P)
                for b in range(NB):
                    if b >= NK:
                        sp.wait_ge(turned, 4 * (b - NK + 1))
                    sp.dma_start(kb[:, b % NK], kd[b]).then_inc(k_in[b % NK], 16)
                for b in range(NB):
                    if b >= NV:
                        sp.wait_ge(o_done, b - NV + 1)
                    sp.dma_start(vb[:, b % NV], vd[b]).then_inc(v_in[b % NV], 16)

            @block.tensor
            def _(pe):
                def scores(b):
                    pe.wait_ge(kt_v, 2 * b + 2)
                    pe.wait_ge(kt_a, 2 * b + 2)
                    for dc in range(2):
                        for h in range(HX):
                            n, r = 2 * h + dc, slice(NS * h, NS * h + NS)
                            ins = nc.tensor.matmul(ps[r, 0, 0:NM], qm[:, n, b, :], kbT[:, b % 2, n, :],
                                                   start=(b == 0 and dc == 0), stop=(b == NB - 1 and dc == 1),
                                                   tile_position=(0, NS * h))
                    ins.then_inc(s_done, 1)

                for b in range(NB):
                    pe.wait_ge(k_in[b % NK], 16 * (b // NK + 1))
                    for q in range(4):
                        if b:
                            pe.wait_ge((kt_v, kt_a)[q % 2], 2 * (b - 1) + q // 2 + 1)
                        for j in range(2):
                            for i in range(2):
                                n = 2 * q + j
                                ins = nc.tensor.transpose(ps[:, 4 + q, NM * j + P * i:NM * j + P * i + P],
                                                          kb[:, b % NK, i, P * n:P * n + P], ident[:])
                        ins.then_inc(turned, 1)
                    if b:
                        if b == 1:
                            pe.wait_ge(q_ok, 1)
                        scores(b - 1)
                scores(NB - 1)
                pe.wait_ge(p_ok, 1)
                for mt in range(2):
                    ins = nc.tensor.transpose(ps[:, 1, P * mt:P * mt + P], pr[:, P * mt:P * mt + P], ident[:])
                ins.then_inc(pt_done, 1)
                pe.wait_ge(pm_ok, 1)
                for b in range(NB):
                    pe.wait_ge(v_in[b % NV], 16 * (b // NV + 1))
                    for mt in range(2):
                        for h in range(HX):
                            r = slice(NS * h, NS * h + NS)
                            ins = nc.tensor.matmul(ps[r, 2, 0:DX], pm[:, mt, b, r], vb[:, b % NV, mt, DX * h:DX * h + DX],
                                                   start=(b == 0 and mt == 0), stop=(b == NB - 1 and mt == 1),
                                                   tile_position=(0, NS * h))
                    ins.then_inc(o_done, 1)
                pe.wait_ge(o_ok, 1)
                for dc in range(2):
                    ins = nc.tensor.transpose(ps[:, 3, P * dc:P * dc + P], os_[:, P * dc:P * dc + P], ident[:])
                ins.then_inc(ot_done, 1)

            def take(eng, copy, b, odd, done):
                for q in range(odd, 4, 2):
                    eng.wait_ge(turned, 4 * b + q + 1)
                    if b >= 2:
                        eng.wait_ge(s_done, b - 1)
                    copy(kbT[:, b % 2, 2 * q:2 * q + 2, :].rearrange("p n m -> p (n m)"), ps[:, 4 + q, :]).then_inc(
                        done, 1)

            @block.vector
            def _(dve):
                dve.wait_ge(zeroed, 2)
                for b in range(NB):
                    ins = nc.vector.tensor_copy(qm[:, :, b, TS * b:TS * b + TS], qT[:, :, TP + TS * b:TP + TS * b + TS])
                ins.then_inc(q_ok, 1)
                for b in range(NB):
                    take(dve, nc.vector.tensor_copy, b, 0, kt_v)
                dve.wait_ge(s_done, NB)
                nc.vector.tensor_reduce(mx[:, 0:1], ps[:, 0, 0:NM], AXX, ALU.max, negate=True).then_inc(mx_ok, 1)
                dve.wait_ge(e_ok, 1)
                ch.step(dve, nc.vector.reciprocal(mx[:, 2:3], mx[:, 1:2]))
                nc.vector.tensor_scalar(pr[:, :], pr[:, :], mx[:, 2:3], None, ALU.mult).then_inc(p_ok, 1)
                dve.wait_ge(pt_done, 1)
                for b in range(NB):
                    ins = nc.vector.tensor_copy(
                        pm[:, :, b, :].rearrange("p m (h t) -> p m h t", h=HX)[:, :, :, TS * b:TS * b + TS],
                        ps[:, 1, 0:256].rearrange("p (m h t) -> p m h t", m=2, h=HX)[:, :, :, TS * b:TS * b + TS])
                ins.then_inc(pm_ok, 1)
                dve.wait_ge(ot_done, 1)
                for dc in range(2):
                    nc.vector.tensor_copy(oT[:, dc::2, TP:], ps[:, 3, P * dc:P * dc + P].rearrange(
                        "p (h t) -> p h t", h=HX))

            @block.scalar
            def _(act):
                for b in range(NB):
                    take(act, nc.scalar.copy, b, 1, kt_a)
                act.wait_ge(mx_ok, 1)
                nc.scalar.activation(pr[:, :], ps[:, 0, 0:NM], ACT.Exp, bias=mx[:, 0:1], accum_out=mx[:, 1:2]).then_inc(
                    e_ok, 1)
                act.wait_ge(o_done, NB)
                nc.scalar.copy(os_[:, :], ps[:, 2, 0:DX]).then_inc(o_ok, 1)


CAP = 64
HK = 4
NQ = P
LIST = 2 * NE


def experts(nc, a, out, outer, sb, ps, ident, ones, x, g8, stat, eps, norm_stage):
    with ExitStack() as st:
        sem = semaphores(nc, st, "mo")
        h_tm = sb(st, "eh_tm", [P, 3, D])
        code = sb(st, "code", [P, 3, NE])
        gate = sb(st, "gate_e", [P, 3, NE])
        tab = sb(st, "tab", [1, 2 * LIST + 1], I32)
        base = sb(st, "base", [P, LIST])
        iota = sb(st, "iota", [P, CAP])
        gfx = sb(st, "gfx", [P, 2, HK])
        pick = sb(st, "pick", [4, 4, CAP])
        route(nc, a, st, sb, ps, ident, ones, x, g8, stat, eps, norm_stage, h_tm, code, gate, tab, base, iota, gfx,
              pick)

        w1 = sb(st, "w1", [P, 2, 2, HK, 2 * D])
        w2 = sb(st, "w2", [P, 2, HK, D])
        b1 = sb(st, "b1", [4, 2, 512])
        sel = sb(st, "sel", [P, 3, CAP])
        gsel = sb(st, "gsel", [P, 3, 2, CAP])
        gT = sb(st, "gT", [P, 3, P])
        off = sb(st, "off", [P, 2, 3])
        xe = sb(st, "xe", [P, 512])
        xeT = sb(st, "xeT", [P, 2, HK, CAP])
        hg = sb(st, "hg", [P, 512])
        hl = sb(st, "hl", [P, 512])
        th = sb(st, "e_th", [P, 512])
        y = sb(st, "y", [P, 512])
        w1_in = [[sem(f"w1_in{s}{h}") for h in range(2)] for s in range(2)]
        b1_in = [sem(f"b1_in{s}") for s in range(2)]
        w2_in = sem("w2_in")
        w1_done, cmb_done, gath_done, xt_done, gt_done, at_done, w2_done = (
            sem(n) for n in ("w1_done", "cmb_done", "gath_done", "xt_done", "gt_done", "at_done", "w2_done"))
        th_ok, xe_ok, at_ok, y_ok = (sem(n) for n in ("th_ok", "xe_ok", "at_ok", "y_ok"))
        hg_ok, act_ok, add_ok, sel_ok, xT_ok, g_ok, gt_ok, chain = (
            sem(n) for n in ("hg_ok", "act_ok", "add_ok", "sel_ok", "xT_ok", "g_ok", "gt_ok", "chain"))
        w1_d = a["w1_e"][0].rearrange("e (h p c) n -> h p e c n", h=2, c=HK)
        w2_d = a["w2_e"][0].rearrange("e (h p c) n -> p e h c n", h=2, c=HK)
        b1_d = a["b1_e"][0].rearrange("e (r n) -> r e n", n=512)
    
        def count_of(eng):
            return eng.value_load(tab[0:1, 2 * LIST:2 * LIST + 1], min_val=NE // 2, max_val=LIST // 2 - 1)

        with nc.Block() as block:
            @block.sync
            def _(sp):
                def load(e, s, i):
                    if i is not None:
                        sp.wait_ge(w1_done, 2 * i + s - 1)
                    for h in range(2):
                        sp.dma_start(w1[:, s, h].unsqueeze(1), w1_d[h][:, e]).then_inc(w1_in[s][h], 16)
                        if h == 0:
                            sp.dma_start(b1[:, s].unsqueeze(1), b1_d[:, e]).then_inc(b1_in[s], 16)
                    if i is not None or s:
                        sp.wait_ge(w2_done, 1 if i is None else 2 * i + s)
                    sp.dma_start(w2[:, :, :, :].unsqueeze(1), w2_d[:, e]).then_inc(w2_in, 16)

                pairs = count_of(sp)
                for s in range(2):
                    load(slice(s, s + 1), s, None)
                with sp.Fori(1, pairs) as i:
                    for s in range(2):
                        e = sp.value_load(tab[0:1, bass.ds(2 * i + s, 1)], min_val=0, max_val=NE - 1)
                        load(bass.ds(e, 1), s, i)

            @block.gpsimd
            def _(pool):
                nc.gpsimd.memset(y[:, :], 0.0).then_inc(y_ok, 1)
                nc.gpsimd.memset(gT[:, 0:2, :], 0.0).then_inc(gt_ok, 1)

            @block.tensor
            def _(pe):
                def gather():
                    for half in range(2):
                        for i, (t0, n) in enumerate(TILES):
                            ins = nc.tensor.matmul(ps[CAP * half:CAP * half + CAP, 3, :], sel[:n, i, :],
                                                   h_tm[:n, i, 512 * half:512 * half + 512], start=(i == 0),
                                                   stop=(i == 2))
                    ins.then_inc(gath_done, 1)

                def turn_x():
                    for c in range(HK):
                        ins = nc.tensor.transpose(ps[:, 4, P * c:P * c + P], xe[:, c::HK], ident[:])
                    ins.then_inc(xt_done, 1)

                def combine(i):
                    for half in range(2):
                        r = slice(CAP * half, CAP * half + CAP)
                        ins = nc.tensor.matmul(ps[:, 6 + half, :], gT[r, i, :], y[r, :], start=True, stop=True)
                    ins.then_inc(cmb_done, 1)

                pairs = count_of(pe)
                pe.wait_ge(sel_ok, 1)
                gather()
                pe.wait_ge(xe_ok, 1)
                turn_x()
                with pe.Fori(0, pairs) as j:
                    for s in range(2):
                        k = 2 * j + s
                        pe.wait_ge(xT_ok, k + 1)
                        pe.wait_ge(b1_in[s], 16 * j + 16)
                        for half in range(2):
                            for g in range(2):
                                ins = nc.tensor.matmul(ps[CAP * half:CAP * half + CAP, g, :], pick[:, 2 * g + half, :],
                                                       b1[:, s, :], start=True, stop=False)
                        for h in range(2):
                            pe.wait_ge(w1_in[s][h], 16 * j + 16)
                            for c in range(HK):
                                for g in range(2):
                                    for half in range(2):
                                        c0 = D * g + 512 * half
                                        ins = nc.tensor.matmul(ps[CAP * half:CAP * half + CAP, g, :], xeT[:, h, c, :],
                                                               w1[:, s, h, c, c0:c0 + 512], start=False,
                                                               stop=(h == 1 and c == HK - 1))
                        ins.then_inc(w1_done, 1)
                        pe.wait_ge(y_ok, k + 1)
                        pe.wait_ge(gt_ok, k + 1)
                        pe.wait_ge(add_ok, 3 * k + 1)
                        combine(0)
                        pe.wait_ge(sel_ok, k + 2)
                        gather()
                        pe.wait_ge(add_ok, 3 * k + 2)
                        combine(1)
                        pe.wait_ge(xe_ok, k + 2)
                        turn_x()
                        pe.wait_ge(add_ok, 3 * k + 3)
                        combine(2)
                        pe.wait_ge(g_ok, k + 1)
                        for i, (t0, n) in enumerate(TILES):
                            ins = nc.tensor.transpose(ps[:, 3, t0:t0 + n], gsel[:n, i].rearrange("p r t -> p (r t)"),
                                                      ident[:n, :n])
                        ins.then_inc(gt_done, 1)
                        pe.wait_ge(act_ok, k + 1)
                        for c in range(HK):
                            ins = nc.tensor.transpose(ps[:, 5, P * c:P * c + P], hl[:, c::HK], ident[:])
                        ins.then_inc(at_done, 1)
                        pe.wait_ge(at_ok, k + 1)
                        pe.wait_ge(w2_in, 16 * k + 16)
                        actT = th[:, :].rearrange("p (c h t) -> p c h t", c=HK, h=2)
                        for h in range(2):
                            for c in range(HK):
                                for half in range(2):
                                    ins = nc.tensor.matmul(ps[CAP * half:CAP * half + CAP, 2, :], actT[:, c, h, :],
                                                           w2[:, h, c, 512 * half:512 * half + 512],
                                                           start=(h == 0 and c == 0), stop=(h == 1 and c == HK - 1))
                        ins.then_inc(w2_done, 1)
                pe.wait_ge(y_ok, 2 * pairs + 1)
                pe.wait_ge(gt_ok, 2 * pairs + 1)
                for i in range(3):
                    pe.wait_ge(add_ok, 6 * pairs + i + 1)
                    combine(i)

            @block.scalar
            def _(act):
                def take_x():
                    nc.scalar.copy(xe[:, :], ps[:, 3, :]).then_inc(xe_ok, 1)

                pairs = count_of(act)
                act.wait_ge(gath_done, 1)
                take_x()
                with act.Fori(0, pairs) as j:
                    for s in range(2):
                        k = 2 * j + s
                        act.wait_ge(hg_ok, k + 1)
                        nc.scalar.activation(th[:, :], hg[:, :], ACT.Tanh, scale=ALPHA / 2).then_inc(th_ok, 1)
                        act.wait_ge(gath_done, k + 2)
                        take_x()
                        act.wait_ge(at_done, k + 1)
                        nc.scalar.copy(th[:, :], ps[:, 5, :]).then_inc(at_ok, 1)
                        act.wait_ge(w2_done, k + 1)
                        nc.scalar.activation(y[:, :], ps[:, 2, :], ACT.Copy, scale=0.5).then_inc(y_ok, 1)

            @block.vector
            def _(dve):
                ch = Count(chain)

                def add(i):
                    n = TILES[i][1]
                    v = x[:n, i, :].rearrange("p (h d) -> p h d", h=2)
                    nc.vector.tensor_tensor(v, v, ps[:n, 6:8, :], ALU.add).then_inc(add_ok, 1)

                def turned_x():
                    nc.vector.tensor_tensor(xeT[:, :, :, :].rearrange("p h c t -> p c h t"),
                                            ps[:, 4, :].rearrange("p (c h t) -> p c h t", c=HK, h=2),
                                            over(gfx[:, :, :].rearrange("p h c -> p c h"), CAP, 3),
                                            ALU.mult).then_inc(xT_ok, 1)

                def offset(w, e, k, steps):
                    nc.vector.tensor_scalar(off[:, w, :], code[:, :, e].rearrange("p i o -> p (i o)"), base[:, k], None,
                                            ALU.subtract).then_inc(chain, 1)
                    dve.wait_ge(chain, steps)

                def select(w=1):
                    for i, (_, n) in enumerate(TILES):
                        ins = nc.vector.tensor_scalar(sel[:n, i, :], iota[:n, :], off[:n, w, i:i + 1], None, ALU.is_equal)
                    ins.then_inc(sel_ok, 1)

                def weigh(e):
                    for i, (_, n) in enumerate(TILES):
                        ins = nc.vector.tensor_scalar(gsel[:n, i], over(iota[:n, :], 2), off[:n, 0, i:i + 1],
                                                      gate[:n, i, e], ALU.is_equal, ALU.mult)
                    ins.then_inc(g_ok, 1)

                pairs = count_of(dve)
                nc.vector.memset(gT[:, 2, :], 0.0).then_inc(add_ok, 1)
                offset(0, slice(0, 1), slice(0, 1), 1)
                select(0)
                weigh(slice(0, 1))
                dve.wait_ge(gath_done, 1)
                offset(1, slice(1, 2), slice(1, 2), 2)
                select()
                dve.wait_ge(xt_done, 1)
                turned_x()
                with dve.Fori(0, pairs) as j:
                    for s in range(2):
                        k = 2 * j + s
                        dve.wait_ge(w1_done, k + 1)
                        nc.vector.tensor_scalar(hg[:, :], ps[:, 0, :], LIMIT, None, ALU.min).then_inc(hg_ok, 1)
                        nc.vector.tensor_scalar(hl[:, :], ps[:, 1, :], LIMIT, -LIMIT, ALU.min, ALU.max)
                        dve.wait_ge(cmb_done, 3 * k + 1)
                        add(0)
                        dve.wait_ge(th_ok, k + 1)
                        nc.vector.scalar_tensor_tensor(hg[:, :], th[:, :], 1.0, hg[:, :], ALU.add, ALU.mult).then_inc(
                            chain, 1)
                        dve.wait_ge(chain, 3 * k + 3)
                        nc.vector.scalar_tensor_tensor(hl[:, :], hl[:, :], 1.0, hg[:, :], ALU.add, ALU.mult).then_inc(
                            act_ok, 1)
                        dve.wait_ge(cmb_done, 3 * k + 2)
                        add(1)
                        dve.wait_ge(xt_done, k + 2)
                        turned_x()
                        dve.wait_ge(cmb_done, 3 * k + 3)
                        add(2)
                        dve.wait_ge(gt_done, k + 1)
                        nc.vector.tensor_copy(gT[:, :, :].rearrange("p i t -> p (i t)")[:, 0:T], ps[:, 3, 0:T]).then_inc(gt_ok, 1)
                        e1 = bass.ds(dve.value_load(tab[0:1, bass.ds(k + 1, 1)], min_val=0, max_val=NE - 1), 1)
                        offset(0, e1, bass.ds(k + 1, 1), 3 * k + 4)
                        weigh(e1)
                        e2 = bass.ds(dve.value_load(tab[0:1, bass.ds(k + 2, 1)], min_val=0, max_val=NE - 1), 1)
                        offset(1, e2, bass.ds(k + 2, 1), 3 * k + 5)
                        select()
                for i in range(3):
                    dve.wait_ge(cmb_done, 6 * pairs + i + 1)
                    add(i)
    final_norm(nc, a, out, sb, ps, x, stat, eps)


def route(nc, a, outer, sb, ps, ident, ones, x, g8, stat, eps, norm_stage, h_tm, code, gate, tab, base, iota, gfx,
          pick):
    with ExitStack() as st:
        sem = semaphores(nc, st, "rt")
        hT = sb(st, "ehT", [P, KC, T])
        rw = sb(st, "rw", [P, KC, NE])
        rb = sb(st, "rb", [P, NE])
        b2 = sb(st, "b2", [NE, D])
        lg = sb(st, "lg", [P, 3, NE])
        mask = sb(st, "mask", [P, 3, NE])
        onei = sb(st, "onei", [P, NE])
        top = sb(st, "top", [P, 3, 8])
        idx = sb(st, "idx", [P, 3, 8], mybir.dt.uint32)
        idf = sb(st, "idf", [P, 3, 8])
        sm = sb(st, "sm", [P, 3, 2])
        stri = sb(st, "estri", [P, P])
        gateT = sb(st, "gateT", [NE, T])
        mrep = sb(st, "mrep", [P, 3, 4, NE])
        q = sb(st, "q", [P, 8])
        hit = sb(st, "hit", [P, 3, NE])
        tabf = sb(st, "tabf", [P, 2, LIST])
        Q_E, Q_OFF, Q_OVER, Q_POS = range(4)
        loaded, made, summed, moved, ex, turned = (sem(n) for n in ("in", "made", "sum", "moved", "exp", "turned"))
        pool_c, d = Count(sem("pool")), Count(sem("dve"))
        with nc.Block() as block:
            @block.sync
            def _(sp):
                sp.dma_start(rw[:, :, :], a["router_w"][0].rearrange("(p c) e -> p c e", c=KC)).then_inc(loaded, 16)
                sp.dma_start(rb[:, :], a["router_b"][0].partition_broadcast(P)).then_inc(loaded, 16)
                sp.dma_start(b2[:, :], a["b2_e"][0]).then_inc(loaded, 16)
                sp.dma_start(gfx[:, :, :], a["norm_ffn"][0].rearrange("(h p c) -> p h c", h=2, c=HK)).then_inc(loaded, 16)
                sp.wait_ge(loaded, 64)

            @block.gpsimd
            def _(pool):
                def step(ins):
                    pool_c.step(pool, ins)
                step(nc.gpsimd.iota(iota[:, :], [[1, CAP]], 0, 0, allow_small_or_imprecise_dtypes=True))
                step(nc.gpsimd.memset(stri[:, :], 1.0))
                step(nc.gpsimd.affine_select(stri[:], stri[:], [[1, P]], ALU.is_ge, 0.0, -1, -1))
                step(nc.gpsimd.memset(pick[:, :, :], 1.0))
                step(nc.gpsimd.affine_select(pick[:, :, :], pick[:, :, :], [[-1, 4], [0, CAP]], ALU.is_equal, 0.0, 0, 1))
                step(nc.gpsimd.iota(hit[:, 0, 0:4], [[-NE, 4]], 0, 1, allow_small_or_imprecise_dtypes=True))

        norm_stage("ffn", x, TILES, 3, hT, h_tm)
        with nc.Block() as block:
            @block.tensor
            def _(pe):
                for i, (t0, n) in enumerate(TILES):
                    for c in range(KC):
                        ins = nc.tensor.matmul(ps[:n, i, 0:NE], hT[:, c, t0:t0 + n], rw[:, c, :], start=(c == 0),
                                               stop=(c == KC - 1))
                    ins.then_inc(summed, 1)
                pe.wait_ge(made, 1)
                for i, (t0, n) in enumerate(TILES):
                    for j in range(i + 1):
                        m = TILES[j][1]
                        lhs = ones[:m, :n] if j < i else stri[:n, :n]
                        ins = nc.tensor.matmul(ps[:n, 3 + i, 0:NE], lhs, mask[:m, j, :], start=(j == 0), stop=(j == i))
                for j in range(3):
                    m = TILES[j][1]
                    ins = nc.tensor.matmul(ps[:, 6, 0:1], mrep[:m, j].rearrange("p b e -> p (b e)"), ones[:m, 0:1],
                                           start=(j == 0), stop=(j == 2))
                for j, (t0, n) in enumerate(TILES):
                    ins = nc.tensor.transpose(ps[:NE, 7, t0:t0 + n], gate[:n, j, :], ident[:n, :n])
                ins.then_inc(turned, 1)
                pe.wait_ge(made, 2)
                nc.tensor.matmul(ps[:, 0, 0:1], stri[:], q[:, Q_OVER:Q_OVER + 1], start=True, stop=True)
                nc.tensor.matmul(ps[:, 0, 1:2], ones[:], q[:, Q_OVER:Q_OVER + 1], start=True, stop=True).then_inc(
                    turned, 1)
                pe.wait_ge(made, 3)
                nc.tensor.matmul(ps[:, 1, 0:2 * NE], ones[:], hit[:, 1:3, :].rearrange("p j m -> p (j m)"), start=True,
                                 stop=True).then_inc(turned, 1)
                for i, (t0, n) in enumerate(TILES):
                    for half in range(2):
                        ins = nc.tensor.matmul(ps[:n, 2 + 2 * i + half, :], gateT[:, t0:t0 + n],
                                               b2[:, 512 * half:512 * half + 512], start=True, stop=True)
                    ins.then_inc(turned, 1)

            @block.scalar
            def _(act):
                for i, (_, n) in enumerate(TILES):
                    act.wait_ge(moved, i + 1)
                    nc.scalar.activation(top[:n, i, 4:8], top[:n, i, 0:4], ACT.Exp, bias=sm[:n, i, 0:1],
                                         accum_out=sm[:n, i, 1:2]).then_inc(ex, 1)

            @block.vector
            def _(dve):
                d.step(dve, nc.vector.tensor_scalar(hit[:, 1, 0:4], hit[:, 0, 0:4], 0.0, None, ALU.is_ge))
                d.step(dve, nc.vector.tensor_reduce(q[:, Q_OFF:Q_OFF + 1], hit[:, 1, 0:4], AXX, ALU.add))
                d.step(dve, nc.vector.scalar_tensor_tensor(q[:, Q_E:Q_E + 1], q[:, Q_OFF:Q_OFF + 1], -float(NE),
                                                           hit[:, 0, 0:1], ALU.mult, ALU.add))
                d.step(dve, nc.vector.tensor_scalar(q[:, Q_E:Q_E + 1], q[:, Q_E:Q_E + 1], float(NE), None, ALU.add))
                nc.vector.tensor_scalar(q[:, Q_OFF:Q_OFF + 1], q[:, Q_OFF:Q_OFF + 1], float(CAP), None, ALU.mult)
                for i, (_, n) in enumerate(TILES):
                    dve.wait_ge(summed, i + 1)
                    d.step(dve, nc.vector.tensor_tensor(lg[:n, i, :], ps[:n, i, 0:NE], rb[:n, :], ALU.add))
                    d.step(dve, nc.vector.max(top[:n, i, :], lg[:n, i, :]))
                    d.step(dve, nc.vector.max_index(idx[:n, i, :], top[:n, i, :], lg[:n, i, :]))
                    nc.vector.tensor_copy(idf[:n, i, :], idx[:n, i, :])
                    nc.vector.tensor_scalar(sm[:n, i, 0:1], top[:n, i, 0:1], -1.0, None, ALU.mult).then_inc(moved, 1)
                dve.wait_ge(moved, 3)
                for i, (_, n) in enumerate(TILES):
                    dve.wait_ge(ex, i + 1)
                    d.step(dve, nc.vector.reciprocal(sm[:n, i, 1:2], sm[:n, i, 1:2]))
                    d.step(dve, nc.vector.tensor_scalar(top[:n, i, 4:8], top[:n, i, 4:8], sm[:n, i, 1:2], None,
                                                        ALU.mult))
                    for j in range(TOPK):
                        one = mask[:n, i, :] if j == 0 else onei[:n, :]
                        d.step(dve, nc.vector.tensor_scalar(one, iota[:n, 0:NE], idf[:n, i, j:j + 1], None,
                                                            ALU.is_equal))
                        g = top[:n, i, 4 + j:5 + j]
                        if j == 0:
                            ins = nc.vector.tensor_scalar(gate[:n, i, :], one, g, None, ALU.mult)
                        else:
                            nc.vector.tensor_tensor(mask[:n, i, :], mask[:n, i, :], one, ALU.add)
                            ins = nc.vector.scalar_tensor_tensor(gate[:n, i, :], one, g, gate[:n, i, :], ALU.mult,
                                                                 ALU.add)
                        d.step(dve, ins)
                    ins = nc.vector.tensor_copy(mrep[:n, i], over(mask[:n, i, :], 4))
                ins.then_inc(made, 1)
                dve.wait_ge(turned, 1)
                d.step(dve, nc.vector.memset(code[:, :, :], -1.0))
                for i, (_, n) in enumerate(TILES):
                    ins = nc.vector.scalar_tensor_tensor(code[:n, i, :], ps[:n, 3 + i, 0:NE], 1.0, mask[:n, i, :],
                                                         ALU.add, ALU.mult)
                d.step(dve, ins)
                for i, (_, n) in enumerate(TILES):
                    nc.vector.tensor_scalar(code[:n, i, :], code[:n, i, :], 1.0, None, ALU.subtract)
                nc.vector.tensor_copy(gateT[:, :], ps[:NE, 7, 0:T])
                nc.vector.tensor_tensor(q[:, Q_OVER:Q_OVER + 1], ps[:, 6, 0:1], q[:, Q_OFF:Q_OFF + 1],
                                        ALU.is_gt).then_inc(made, 1)
                dve.wait_ge(turned, 2)
                nc.vector.tensor_copy(q[:, Q_POS:Q_POS + 2], ps[:, 0, 0:2])
                d.step(dve, nc.vector.tensor_scalar(q[:, 6:7], q[:, Q_OVER:Q_OVER + 1], -1.0, -1000.0, ALU.add,
                                                    ALU.mult))
                d.step(dve, nc.vector.tensor_tensor(q[:, Q_POS:Q_POS + 1], q[:, Q_POS:Q_POS + 1], q[:, 6:7], ALU.add))
                d.step(dve, nc.vector.tensor_scalar(hit[:, 0, :], iota[:, 0:NE], q[:, Q_POS:Q_POS + 1], None,
                                                    ALU.is_equal))
                nc.vector.tensor_scalar(q[:, 5:6], q[:, Q_OFF:Q_OFF + 1], 5.0 * CAP, None, ALU.subtract)
                nc.vector.tensor_scalar(hit[:, 1, :], hit[:, 0, :], q[:, Q_E:Q_E + 1], None, ALU.mult)
                d.step(dve, nc.vector.memset(base[:, 0:NE], 0.0))
                nc.vector.tensor_scalar(hit[:, 2, :], hit[:, 0, :], q[:, 5:6], None, ALU.mult).then_inc(made, 1)
                d.step(dve, nc.vector.tensor_scalar(q[:, 7:8], q[:, Q_POS + 1:Q_POS + 2], 0.5, NE / 2 + 0.25, ALU.mult,
                                                    ALU.add))
                nc.vector.tensor_copy(tab[0:1, 2 * LIST:2 * LIST + 1], q[0:1, 7:8])
                dve.wait_ge(turned, 3)
                nc.vector.tensor_copy(tab[0:1, 0:NE], iota[0:1, 0:NE])
                nc.vector.tensor_copy(tab[0:1, NE:LIST], ps[0:1, 1, 0:NE])
                nc.vector.tensor_scalar(base[:, NE:LIST], ps[:, 1, NE:2 * NE], 5.0 * CAP, None, ALU.add)
                for i, (_, n) in enumerate(TILES):
                    dve.wait_ge(turned, 4 + i)
                    v = x[:n, i, :].rearrange("p (h d) -> p h d", h=2)
                    nc.vector.tensor_tensor(v, v, ps[:n, 2 + 2 * i:4 + 2 * i, :], ALU.add)


def final_norm(nc, a, out, sb, ps, x, stat, eps):
    with ExitStack() as st:
        sem = semaphores(nc, st, "fn")
        gf = sb(st, "gf", [P, D])
        y = sb(st, "fy", [P, 3, D])
        loaded, sq, root, done, stored = (sem(n) for n in ("in", "sq", "root", "done", "stored"))
        d = Count(sem("dve"))
        with nc.Block() as block:
            @block.sync
            def _(sp):
                sp.dma_start(gf[:, :], a["final_norm"].partition_broadcast(P)).then_inc(loaded, 16)
                for i in range(2):
                    sp.wait_ge(done, i + 1)
                    sp.dma_start(out[0][0].rearrange("(i p) d -> i p d", p=P)[i], y[:, i, :]).then_inc(stored, 16)
                sp.wait_ge(done, 3)
                sp.dma_start(out[1].rearrange("b t d -> (b t) d"), y[:NS, 2, :]).then_inc(stored, 16)
                sp.wait_ge(stored, 48)

            @block.scalar
            def _(act):
                for i, (_, n) in enumerate(TILES):
                    nc.scalar.activation(y[:n, i, :], x[:n, i, :], ACT.Square, accum_out=stat[:n, i, 0:1]).then_inc(
                        sq, 1)
                for i, (_, n) in enumerate(TILES):
                    act.wait_ge(sq, i + 1)
                    nc.scalar.activation(stat[:n, i, 1:2], stat[:n, i, 0:1], ACT.Sqrt, bias=eps[:n, 0:1],
                                         scale=1.0 / D).then_inc(root, 1)

            @block.vector
            def _(dve):
                dve.wait_ge(loaded, 16)
                for i, (_, n) in enumerate(TILES):
                    dve.wait_ge(root, i + 1)
                    d.step(dve, nc.vector.reciprocal(stat[:n, i, 2:3], stat[:n, i, 1:2]))
                    nc.vector.scalar_tensor_tensor(y[:n, i, :], x[:n, i, :], stat[:n, i, 2:3], gf[:n, :], ALU.mult,
                                                   ALU.mult).then_inc(done, 1)


_INS = ['x_prompt', 'x_sample', 'mem_prompt', 'state_rwkv', 'state_rwkv_shift', 'state_gdn', 'state_gdn_conv',
        'cache_mem_k', 'cache_mem_v', 'norm_mix', 'w_in', 'mu_shift', 'w0', 'w2_decay', 'a0', 'a2_iclr', 'g2_gate',
        'k_k', 'k_a', 'r_k', 'lnx_w', 'lnx_b', 'conv_w', 'a_log', 'dt_bias', 'gdn_norm_w', 'w_out',
        'norm_cross', 'norm_mem', 'wq_x', 'wk_x', 'wv_x', 'wo_x',
        'norm_ffn', 'router_w', 'router_b', 'w1_e', 'b1_e', 'w2_e', 'b2_e', 'final_norm']
_OUTS = [(1, TP, D), (NB, TS, D),
         (1, 1, HR, NR, NR), (1, 1, R_PROJ), (1, 1, HG, DG, DG), (1, 1, CW - 1, CONV),
         (1, 1, NM, HX, DX), (1, 1, NM, HX, DX),
         (1, NB, HR, NR, NR), (1, NB, R_PROJ), (1, NB, HG, DG, DG), (1, NB, CW - 1, CONV)]


def kernel(**inputs):
    import numpy as _np
    import concourse.bacc as _bacc
    from concourse import mybir as _mybir
    from concourse.bass_utils import run_bass_kernel_spmd as _run

    nc = _bacc.Bacc("TRN2", target_bir_lowering=False, num_devices=1)
    arrays, ins, outs = {}, {}, []
    for name in _INS:
        arr = _np.ascontiguousarray(inputs[name])
        arrays[f"in_{name}_dram"] = arr
        ins[name] = nc.dram_tensor(f"in_{name}_dram", arr.shape, _mybir.dt.from_np(arr.dtype),
                                   kind="ExternalInput").ap()
    for i, shape in enumerate(_OUTS):
        outs.append(nc.dram_tensor(f"out_{i}_dram", shape, _mybir.dt.float32, kind="ExternalOutput").ap())
    build(nc, ins, outs)
    r = _run(nc, [arrays], core_ids=[0])
    return tuple(r.results[0][f"out_{i}_dram"] for i in range(len(_OUTS)))
```

```python
from contextlib import ExitStack

import concourse.bass as bass
from concourse import mybir

F32 = mybir.dt.float32
I32 = mybir.dt.int32
ALU = mybir.AluOpType
ACT = mybir.ActivationFunctionType
AXX = mybir.AxisListType.X

P = 128
D = 1024
KC = D // P
TP, NB, TS = 256, 8, 4
NS = NB * TS
T = TP + NS
TILES = [(0, P), (P, P), (TP, NS)]
HR, NR = 8, 64
HG, DG = 4, 128
PAIRS = HR * NR // P
R_PROJ = 3 * HR * NR + 256
R_TILES = R_PROJ // P
C_TILES = 3 * HG
CONV = 3 * HG * DG
CW = 4
Z0 = R_TILES + C_TILES
P_TOT = R_PROJ + CONV + HG * DG + 2 * HG
CR = 64
NCR = TP // CR
RW = 1 + TP + NB * (1 + TS)
GW = CW - 1 + TP + NB * (CW - 1 + TS)
NM = 256
HX, DX = 4, 256
NE, TOPK = 32, 4
RMS_EPS = 1e-6
GN_EPS = 64e-5
LIMIT, ALPHA = 7.0, 1.702
EXP_M05 = 0.6065306597126334

V_MU, V_A0, V_KK, V_KA, V_RK, V_LW, V_LB, V_CW, V_GN = 0, 14, 18, 22, 26, 30, 34, 38, 86
V_ROWS = 87


class Count:

    def __init__(self, sem):
        self.sem, self.n = sem, 0

    def inc(self, ins):
        self.n += 1
        ins.then_inc(self.sem, 1)
        return self.n

    def step(self, eng, ins):
        self.inc(ins)
        eng.wait_ge(self.sem, self.n)


DEAD = []


def zero_dead(nc, st):
    for s in DEAD:
        nc.gpsimd.sem_clear(s)
        st.callback(nc.release_semaphore, s)
    DEAD.clear()


def semaphores(nc, st, prefix):
    made = []

    def make(name):
        made.append(nc.alloc_semaphore(f"{prefix}_{name}"))
        return made[-1]

    st.callback(DEAD.extend, made)
    return make


def build(nc, a, out):
    DEAD.clear()
    outer = ExitStack()
    with outer:
        def sb(st, name, shape, dt=F32, side="left"):
            return st.enter_context(nc.sbuf_tensor(name, shape, dt, side=side))

        ps = outer.enter_context(nc.psum_tensor("ps", [P, 8, 512], F32))
        ident = sb(outer, "ident", [P, P])
        ones = sb(outer, "ones", [P, P])
        x = sb(outer, "x", [P, 3, D])
        g8 = sb(outer, "g8", [P, 4, KC])
        stat = sb(outer, "stat", [P, 3, 4])
        eps = sb(outer, "eps", [P, 2])

        def norm_stage(name, src, tiles, gcol, hT, h_tm):
            with ExitStack() as st:
                sem = semaphores(nc, st, name)
                sq_done, root_done, h_done = sem("squares"), sem("root"), sem("h")
                turned = sem("turned")
                chain = Count(sem("chain"))
                nt = len(tiles)
                width = tiles[-1][0] + tiles[-1][1]
                with nc.Block() as block:
                    @block.scalar
                    def _(act):
                        for i, (_, n) in enumerate(tiles):
                            nc.scalar.activation(h_tm[:n, i, :], src[:n, i, :], ACT.Square,
                                                 accum_out=stat[:n, i, 0:1]).then_inc(sq_done, 1)
                        for i, (_, n) in enumerate(tiles):
                            act.wait_ge(sq_done, i + 1)
                            nc.scalar.activation(stat[:n, i, 1:2], stat[:n, i, 0:1], ACT.Sqrt, bias=eps[:n, 0:1],
                                                 scale=1.0 / D).then_inc(root_done, 1)
                        for c in range(1, KC, 2):
                            act.wait_ge(turned, c + 1)
                            nc.scalar.activation(hT[:, c, 0:width], ps[:, c, 0:width], ACT.Copy,
                                                 scale=g8[:, gcol, c:c + 1])

                    @block.vector
                    def _(dve):
                        for i, (_, n) in enumerate(tiles):
                            dve.wait_ge(root_done, i + 1)
                            chain.step(dve, nc.vector.reciprocal(stat[:n, i, 2:3], stat[:n, i, 1:2]))
                            nc.vector.tensor_scalar(h_tm[:n, i, :], src[:n, i, :], stat[:n, i, 2:3], None,
                                                    ALU.mult).then_inc(h_done, 1)
                        for c in range(0, KC, 2):
                            dve.wait_ge(turned, c + 1)
                            nc.vector.tensor_scalar(hT[:, c, 0:width], ps[:, c, 0:width],
                                                    g8[:, gcol, c:c + 1], None, ALU.mult)

                    @block.tensor
                    def _(pe):
                        for i, (t0, n) in enumerate(tiles):
                            pe.wait_ge(h_done, i + 1)
                            for c in range(KC):
                                ins = nc.tensor.transpose(ps[:, c, t0:t0 + n], h_tm[:n, i, c::KC], ident[:n, :n])
                                if i == nt - 1:
                                    ins.then_inc(turned, 1)

        ahead = Ahead(nc, a, outer, sb)
        mixer(nc, a, out, ahead, sb, ps, ident, ones, x, g8, stat, eps, norm_stage)
        attention(nc, a, out, ahead, sb, ps, ident, ones, x, g8, stat, eps, norm_stage)
        experts(nc, a, out, ahead, sb, ps, ident, ones, x, g8, stat, eps, norm_stage)


class Tiles:
    pass


class Ahead:

    def __init__(self, nc, a, outer, sb):
        self.nc, self.a, self.outer, self.sb = nc, a, outer, sb
        self.temp = ExitStack()

    def start(self):
        sem = semaphores(self.nc, self.outer, "ah")
        self.out_in, self.wo_in, self.w1_in = ([sem(f"{n}_in{j}") for j in range(2)] for n in ("out", "wo", "w1"))
        self.mem_in, self.wk_in, self.wv_in, self.wq_in = (sem(f"{n}_in") for n in ("mem", "wk", "wv", "wq"))
        self.wa = self.sb(self.outer, "wa", [P, KC, D], side="right")

    def halves(self, sp, dst, name, done):
        v = self.a[name][0].rearrange("(c p) n -> p c n", c=KC)
        for j in range(2):
            cols = slice(512 * j, 512 * j + 512)
            sp.dma_start(dst[:, :, cols], v[:, :, cols]).then_inc(done[j], 16)

    def whole(self, sp, dst, name, done):
        sp.dma_start(dst[:, :, :], self.a[name][0].rearrange("(p c) n -> p c n", c=KC)).then_inc(done, 16)

    def memory(self):
        self.wb = self.sb(self.outer, "wb", [P, KC, D], side="right")
        self.memx = self.sb(self.temp, "memx", [P, 2, D], side="right")
        self.wv = ExitStack()
        self.wc = self.sb(self.wv, "wc", [P, KC, D], side="right")

    def load_memory(self, sp):
        sp.dma_start(self.memx[:, :, :], self.a["mem_prompt"][0].rearrange("(i p) d -> p i d", p=P)).then_inc(
            self.mem_in, 16)
        self.whole(sp, self.wb, "wk_x", self.wk_in)
        self.whole(sp, self.wc, "wv_x", self.wv_in)


def mixer(nc, a, out, ahead, sb, ps, ident, ones, x, g8, stat, eps, norm_stage):
    st = ExitStack()
    with st:
        yT = sb(st, "yT", [P, KC, T])
        lvl = sb(st, "lvl", [P, 7, P])
        tri = sb(st, "tri", [P, P])
        tr64 = sb(st, "tr64", [P, 2, P])
        tr4 = sb(st, "tr4", [P, 2, P])
        stri = sb(st, "stri", [P, P])
        head64 = sb(st, "head64", [P, P])
        blk4 = sb(st, "blk4", [P, P])
        bm4 = sb(st, "bm4", [P, 4, NB])
        bmask = sb(st, "bmask", [P, NB])
        vrow = sb(st, "vrow", [V_ROWS, P])
        vec = sb(st, "vec", [P, V_ROWS])
        ba = sb(st, "ba", [2 * HG, T])
        w2x = sb(st, "w2x", [65, HR * NR])
        a2 = sb(st, "a2", [P, HR * NR])
        g2 = sb(st, "g2", [P, HR * NR])
        dtb = sb(st, "dtb", [P, 2, HG])
        zt = sb(st, "zt", [P, HG, T])
        pr = sb(st, "pr", [P, R_TILES, RW])
        pg = sb(st, "pg", [P, C_TILES, GW])

        ld = ExitStack()
        with ld:
            sem = semaphores(nc, ld, "in")
            h_tm = sb(ld, "h_tm", [P, 3, D])
            hT = sb(ld, "hT", [P, KC, T])
            NG = 3
            wide = 512
            wst = sb(ld, "wst", [P, NG, KC, wide])
            shr = sb(ld, "shr", [NB, R_PROJ])
            cvr = sb(ld, "cvr", [NB * (CW - 1), CONV])
            x_in = [sem(f"x_in{i}") for i in range(3)]
            vec_in, small_in, tail_in = sem("vec_in"), sem("small_in"), sem("tail_in")
            w_in = [sem(f"w_in{i}") for i in range(NG)]
            masks = Count(sem("masks"))
            ngroups = -(-P_TOT // wide)
            w_view = a["w_in"][0].rearrange("(p c) n -> p c n", c=KC)

            def load_w(eng, g):
                n = min(wide, P_TOT - g * wide)
                eng.dma_start(wst[:, g % NG, :, 0:n], w_view[:, :, g * wide:g * wide + n]).then_inc(w_in[g % NG], 16)

            def first(block):
                @block.sync
                def _(sp):
                    xp = a["x_prompt"][0].rearrange("(i p) d -> i p d", p=P)
                    for i in range(2):
                        sp.dma_start(x[:, i, :], xp[i]).then_inc(x_in[i], 16)
                    sp.dma_start(x[:NS, 2, :], a["x_sample"].rearrange("b t d -> (b t) d")).then_inc(x_in[2], 16)
                    for i, n in enumerate(("norm_mix", "norm_cross", "norm_mem", "norm_ffn")):
                        sp.dma_start(g8[:, i, :], a[n][0].rearrange("(p c) -> p c", c=KC)).then_inc(small_in, 16)
                    for g in range(NG):
                        load_w(sp, g)
                    sp.wait_ge(small_in, 64)
                    for i in range(3):
                        sp.wait_ge(x_in[i], 16)

                @block.gpsimd
                def _(pool):
                    masks.step(pool, nc.gpsimd.memset(eps[:, 0:1], RMS_EPS))
                    masks.step(pool, nc.gpsimd.memset(eps[:, 1:2], GN_EPS))
                    masks.step(pool, nc.gpsimd.memset(ident[:], 1.0))
                    masks.step(pool, nc.gpsimd.affine_select(ident[:], ident[:], [[-1, P]], ALU.is_equal, 0.0, 0, 1))

            def make_masks(block):
                @block.gpsimd
                def _(pool):
                    def keep(ap, pattern, base, cm):
                        masks.step(pool, nc.gpsimd.affine_select(ap, ap, pattern, ALU.is_ge, 0.0, base, cm))
                    for ap in (ones[:], blk4[:], tri[:], stri[:], tr64[:, :, :], tr4[:, :, :], bm4[:, :, :]):
                        masks.step(pool, nc.gpsimd.memset(ap, 1.0))
                    for ap in (lvl[:, :, :], head64[:], pr[:, :, 0:1], pg[:, :, 0:CW - 1]):
                        masks.step(pool, nc.gpsimd.memset(ap, 0.0))
                    keep(tri[:], [[1, P]], 0, -1)
                    keep(stri[:], [[1, P]], -1, -1)
                    for m in (tr64, tr4):
                        keep(m[:, 0, :], [[1, P]], -1, -1)
                        keep(m[:, 1, :], [[1, P]], 0, -1)
                    keep(tr64[:, :, 64:], [[0, 2], [0, 64]], -64, 1)
                    for j in range(2):
                        v = tr4[:, j, :].rearrange("p (b t) -> p b t", t=TS)
                        keep(v, [[-TS, P // TS], [0, TS]], 0, 1)
                    v = blk4[:].rearrange("p (b t) -> p b t", t=TS)
                    keep(v, [[-TS, P // TS], [0, TS]], 0, 1)
                    keep(v, [[TS, P // TS], [0, TS]], TS - 1, -1)
                    keep(bm4[:, :, :], [[-32, 4], [-4, NB]], 0, 1)
                    keep(bm4[:, :, :], [[32, 4], [4, NB]], 3, -1)
                    for j in range(2):
                        masks.step(pool, nc.gpsimd.memset(head64[64 * j:64 * j + 64, 64 * j:64 * j + 64], 1.0))
                    for lv in range(7):
                        B = 1 << lv
                        v = lvl[:, lv, :].rearrange("p (j h b) -> p j h b", h=2, b=B)[:, :, 1, :]
                        masks.step(pool, nc.gpsimd.memset(v, 1.0))
                        keep(v, [[-2 * B, P // (2 * B)], [0, B]], 0, 1)
                        keep(v, [[2 * B, P // (2 * B)], [0, B]], B - 1, -1)
                    zero_dead(nc, ld)

            with nc.Block() as block:
                first(block)
            norm_stage("mix", x, TILES, 0, hT, h_tm)

            prj, evac_v, evac_a = sem("prj"), sem("evac_v"), sem("evac_a")
            turned, turned_ok = sem("turned"), sem("turned_ok")
            ntile = -(-P_TOT // P)

            def dest(i):
                if i < R_TILES:
                    v = pr[:, i, 1 + TP:].rearrange("p (b u) -> p b u", u=1 + TS)
                    return pr[:, i, 1:1 + TP], v[:, :, 1:]
                if i < Z0:
                    v = pg[:, i - R_TILES, CW - 1 + TP:].rearrange("p (b u) -> p b u", u=CW - 1 + TS)
                    return pg[:, i - R_TILES, CW - 1:CW - 1 + TP], v[:, :, CW - 1:]
                if i < Z0 + HG:
                    return zt[:, i - Z0, 0:TP], zt[:, i - Z0, TP:].rearrange("p (b u) -> p b u", u=TS)
                return ba[:, 0:TP], ba[:, TP:].rearrange("p (b u) -> p b u", u=TS)

            with nc.Block() as block:
                make_masks(block)

                @block.sync
                def _(sp):
                    for g in range(NG, ngroups):
                        sp.wait_ge(prj, (g - NG + 1) * wide // P)
                        load_w(sp, g)

                def move(eng, copy, i, done):
                    eng.wait_ge(prj, i + 1)
                    n = min(P, P_TOT - i * P)
                    big, small = dest(i)
                    copy(big, ps[:n, i % 4, 0:TP])
                    copy(small, ps[:n, i % 4, TP:T].rearrange("p (b u) -> p b u", u=TS)).then_inc(done, 1)

                @block.vector
                def _(dve):
                    for i in range(0, ntile, 2):
                        move(dve, nc.vector.tensor_copy, i, evac_v)
                    dve.wait_ge(turned, 1)
                    nc.vector.tensor_copy(vec[:, :], ps[:, 4, 0:V_ROWS]).then_inc(turned_ok, 1)
                    dve.wait_ge(turned, 2)
                    nc.vector.tensor_copy(
                        pr[:, :, 1 + TP:].rearrange("p i (b u) -> p i b u", u=1 + TS)[:, :, :, 0],
                        ps[:, 5, 0:R_TILES * NB].rearrange("p (i b) -> p i b", b=NB)).then_inc(turned_ok, 1)
                    dve.wait_ge(turned, 3)
                    for j in range(CW - 1):
                        nc.vector.tensor_copy(
                            pg[:, :, CW - 1 + TP:].rearrange("p i (b u) -> p i b u", u=CW - 1 + TS)[:, :, :, j],
                            ps[:, 6, 0:C_TILES * NB * 3].rearrange("p (i b j) -> p i b j", b=NB, j=3)[:, :, :, j])
                    dve.wait_ge(masks.sem, masks.n)
                    nc.vector.tensor_reduce(bmask[:], bm4[:, :, :].rearrange("p m b -> p b m"), AXX, ALU.add)

                @block.scalar
                def _(act):
                    rows = [("mu_shift", V_MU, 14), ("a0", V_A0, 4), ("k_k", V_KK, 4), ("k_a", V_KA, 4),
                            ("r_k", V_RK, 4), ("lnx_w", V_LW, 4), ("lnx_b", V_LB, 4), ("conv_w", V_CW, 48),
                            ("gdn_norm_w", V_GN, 1)]
                    for name, r0, n in rows:
                        src = a[name][0]
                        src = (src.rearrange("h n -> (h n)") if name == "r_k" else
                               src.rearrange("w n -> (w n)") if name == "conv_w" else src)
                        act.dma_start(vrow[r0:r0 + n, :], src.rearrange("(r p) -> r p", p=P)).then_inc(vec_in, 16)
                    act.dma_start(shr[:, :], a["state_rwkv_shift"][0]).then_inc(vec_in, 16)
                    act.dma_start(cvr[:, :], a["state_gdn_conv"][0].rearrange("b j n -> (b j) n")).then_inc(vec_in, 16)
                    act.dma_start(w2x[0:64, :], a["w2_decay"][0]).then_inc(tail_in, 16)
                    act.dma_start(w2x[64:65, :], a["w0"]).then_inc(tail_in, 16)
                    act.dma_start(a2[64:P, :], a["a2_iclr"][0]).then_inc(tail_in, 16)
                    act.dma_start(g2[:, :], a["g2_gate"][0]).then_inc(tail_in, 16)
                    act.dma_start(dtb[:, 0, :], a["dt_bias"][0].partition_broadcast(P)).then_inc(tail_in, 16)
                    act.dma_start(dtb[:, 1, :], a["a_log"][0].partition_broadcast(P)).then_inc(tail_in, 16)
                    for i in range(1, ntile, 2):
                        move(act, nc.scalar.copy, i, evac_a)
                    act.wait_ge(tail_in, 96)

                @block.tensor
                def _(pe):
                    for i in range(ntile):
                        g, n = i * P // wide, min(P, P_TOT - i * P)
                        if i * P % wide == 0:
                            pe.wait_ge(w_in[g % NG], 16 * (g // NG + 1))
                        if i >= 4:
                            pe.wait_ge(evac_a if i % 2 else evac_v, (i - 4) // 2 + 1)
                        o = i * P % wide
                        for c in range(KC):
                            ins = nc.tensor.matmul(ps[:n, i % 4, 0:T], wst[:, g % NG, c, o:o + n], hT[:, c, :],
                                                   start=(c == 0), stop=(c == KC - 1))
                        ins.then_inc(prj, 1)
                    pe.wait_ge(vec_in, 16 * 11)
                    nc.tensor.transpose(ps[:, 4, 0:V_ROWS], vrow[:, :], ident[:V_ROWS, :V_ROWS]).then_inc(turned, 1)
                    for i in range(R_TILES):
                        ins = nc.tensor.transpose(ps[:, 5, i * NB:(i + 1) * NB], shr[:, i * P:(i + 1) * P],
                                                  ident[:NB, :NB])
                    ins.then_inc(turned, 1)
                    for i in range(C_TILES):
                        ins = nc.tensor.transpose(ps[:, 6, i * 24:(i + 1) * 24], cvr[:, i * P:(i + 1) * P],
                                                  ident[:24, :24])
                    ins.then_inc(turned, 1)


        rk = ExitStack()
        with rk:
            def sb_(n, shape):
                return sb(rk, n, shape)
            gate = sb_("gate", [P, PAIRS, T])
            bv = sb_("bv", [P, PAIRS, T])
            plast = sb_("plast", [P, PAIRS, NCR + NB])
            be_e = sb_("be_e", [P, NCR * PAIRS, P])
            ka_e = sb_("ka_e", [P, NCR * PAIRS, P])
            ar_e = sb_("ar_e", [P, NCR * PAIRS, 2, P])
            be_s = sb_("be_s", [P, 2, 2, 2 * NS])
            ka_s = sb_("ka_s", [P, 2, 2, 2 * NS])
            ar_s = sb_("ar_s", [P, 2, 2, 2, 2 * NS])
            v_c = sb_("v_c", [P, 18, NR])
            qk = sb_("qk", [P, 2, HG, T])
            gv = sb_("gv", [P, HG, T])
            sc = sb_("sc", [P, 12, 9])
            glb = sb_("glb", [P, HG * NB])
            m = Tiles()
            m.pr, m.vec, m.w2x, m.a2, m.g2, m.tr64, m.tr4, m.head64 = pr, vec, w2x, a2, g2, tr64, tr4, head64
            m.gate, m.bv, m.plast, m.be_e, m.ka_e, m.ar_e, m.be_s, m.ka_s = gate, bv, plast, be_e, ka_e, ar_e, be_s, ka_s
            m.ar_s, m.v_c, m.pg, m.zt, m.ba, m.dtb, m.tri, m.stri = ar_s, v_c, pg, zt, ba, dtb, tri, stri
            m.lvl, m.blk4, m.bm4, m.bmask, m.qk, m.gv, m.sc, m.glb = lvl, blk4, bm4, bmask, qk, gv, sc, glb
            m.yT = yT
            rwkv_elementwise(nc, a, out, sb, ps, ident, eps, m)
            m.y_r = sb(rk, "y_r", [P, 18, NR])
            m.y_g = sb(rk, "y_g", [P, 9, DG])
            with ExitStack() as states:
                sem = semaphores(nc, states, "st")
                m.states_in, m.cleared = sem("in"), sem("cleared")
                m.sst = sb(states, "sst", [P, HG, NB, DG], side="right")
                m.stage_t = m.pr[:, :, :].rearrange("p i w -> p (i w)")[:, 0:PAIRS * NB * P].rearrange(
                    "p (q b k) -> p q b k", q=PAIRS, b=NB)
                gdn_elementwise(nc, a, sb, ps, ident, ones, eps, m)
                sample_step(nc, a, out, sb, ps, ident, ones, m)
            prompt_chunks(nc, out, sb, ps, ident, ones, m)
            ahead.start()
            read_out(nc, sb, ps, ident, eps, m, ahead)
        ahead.memory()
        project_add(nc, sb, ps, ident, x, yT, ahead.wa, ahead.out_in, "out", ahead.load_memory)


S_BE, S_G, S_GC, S_NEG, S_EG, S_KT, S_GL, S_X, S_Y, S_U, S_DT, S_AL = range(12)


def rwkv_elementwise(nc, a, out, sb, ps, ident, eps, m):
    with ExitStack() as st:
        sem = semaphores(nc, st, "rw")
        xm = sb(st, "xm", [P, R_TILES, T])
        thx = sb(st, "thx", [65, T])
        sg = sb(st, "sg", [P, T])
        wl = sb(st, "wl", [P, 3, HR * NR])
        pc = sb(st, "pc", [P, PAIRS, T])
        px = sb(st, "px", [P, PAIRS, T])
        pi = sb(st, "pi", [P, PAIRS, T])
        av = sb(st, "av", [P, PAIRS, T])
        kk = sb(st, "kk", [P, PAIRS, T])
        tmp = sb(st, "tmp", [P, PAIRS, T])
        rkc = sb(st, "rkc", [P, PAIRS])
        v_e = sb(st, "v_e", [P, 4, P])
        pr, vec = m.pr, m.vec
        xr, xk, xv = (xm[:, 4 * j:4 * j + 4, :] for j in range(3))
        d, z = Count(sem("dve_chain")), Count(sem("zeroed"))
        lo_ready, th_ready, z_done, wl_ready, cs_done = (sem(n) for n in ("lo", "th", "z", "wl", "cs"))
        a_done, g_done, gate_ok, sq_ready, ss_done, root = (sem(n) for n in ("a", "g", "gate", "sq", "ss", "root"))
        a_ready, rkk, bonus, p_ready, ones_row, z_t = (sem(n) for n in ("a_ready", "rkk", "bonus", "p", "ones", "z_t"))
        kk_done, k_ok = sem("kk"), sem("k")
        a_t, sg_t, bonus_used = (sem(n) for n in ("a_t", "sg_t", "bonus_used"))
        pairs = range(PAIRS)

        def products(ops, which):
            for name, j, f0, f1 in which:
                for h in range(2):
                    r, o, es = (slice(w * h, w * h + w) for w in (64, CR, NS))
                    big, small = {"ar": (m.ar_e[r, :, j, o], m.ar_s[r, :, j, :, es]),
                                  "be": (m.be_e[r, :, o], m.be_s[r, :, :, es]),
                                  "ka": (m.ka_e[r, :, o], m.ka_s[r, :, :, es])}[name]
                    for p in pairs:
                        ops.tensor_tensor(big[:, p::PAIRS], f0[r, p, 0:TP].rearrange("p (c t) -> p c t", t=CR),
                                          f1[r, p, 0:TP].rearrange("p (c t) -> p c t", t=CR), ALU.mult)
                    ops.tensor_tensor(small, f0[r, :, TP:].rearrange("p (i j) t -> p i j t", i=2),
                                      f1[r, :, TP:].rearrange("p (i j) t -> p i j t", i=2), ALU.mult)

        with nc.Block() as block:
            @block.gpsimd
            def _(pool):
                nc.gpsimd.memset(thx[64:65, :], 1.0).then_inc(ones_row, 1)
                pool.wait_ge(ones_row, 1)
                for ap in (m.be_e[:, :, :], m.ka_e[:, :, :], m.ar_e[:, :, :, :], m.be_s[:, :, :, :],
                           m.ka_s[:, :, :, :], m.ar_s[:, :, :, :, :]):
                    z.step(pool, nc.gpsimd.memset(ap, 0.0))
                pool.wait_ge(p_ready, 3 * 4 + 3)
                pool.wait_ge(k_ok, 1)
                products(nc.gpsimd, (("ka", 0, xk, pi),))

            @block.vector
            def _(dve):
                prs = pr[:, :, 1 + TP:].rearrange("p i (b u) -> p i b u", u=1 + TS)
                xms = xm[:, :, TP:].rearrange("p i (b u) -> p i b u", u=TS)
                for i0, i1 in ((12, 14), (0, 12)):
                    nc.vector.tensor_tensor(xm[:, i0:i1, 0:TP], pr[:, i0:i1, 0:TP], pr[:, i0:i1, 1:1 + TP], ALU.subtract)
                    d.step(dve, nc.vector.tensor_tensor(xms[:, i0:i1], prs[:, i0:i1, :, 0:TS], prs[:, i0:i1, :, 1:],
                                                        ALU.subtract))
                    for i in range(i0, i1):
                        mu = vec[:, V_MU + i:V_MU + i + 1]
                        nc.vector.scalar_tensor_tensor(xm[:, i, 0:TP], xm[:, i, 0:TP], mu, pr[:, i, 1:1 + TP],
                                                       ALU.mult, ALU.add)
                        ins = nc.vector.scalar_tensor_tensor(xms[:, i], xms[:, i], mu, prs[:, i, :, 1:],
                                                             ALU.mult, ALU.add)
                        if i == 13:
                            ins.then_inc(lo_ready, 1)
                d.step(dve, nc.vector.tensor_scalar(rkc[:, :], vec[:, V_A0:V_A0 + 4], 0.5, None, ALU.mult))
                for p in pairs:
                    ins = nc.vector.tensor_scalar(kk[:, p, :], xk[:, p, :], vec[:, V_KK + p:V_KK + p + 1], None,
                                                  ALU.mult)
                d.step(dve, ins)
                nc.vector.tensor_tensor(tmp[:, :, :], kk[:, :, :], kk[:, :, :], ALU.mult).then_inc(sq_ready, 1)
                dve.wait_ge(th_ready, 2)
                nc.vector.tensor_scalar(sg[:, :], sg[:, :], 0.5, 0.5, ALU.mult, ALU.add).then_inc(sg_t, 1)
                for i, (t0, n) in enumerate(TILES):
                    dve.wait_ge(z_t, i + 1)
                    nc.vector.tensor_scalar(wl[:n, i, :], wl[:n, i, :], -EXP_M05 / 2, -EXP_M05 / 2,
                                            ALU.mult, ALU.add).then_inc(wl_ready, 1)
                dve.wait_ge(a_t, 4)
                d.step(dve, nc.vector.tensor_scalar(av[:, :, :], av[:, :, :], 0.5, 0.5, ALU.mult, ALU.add))
                dve.wait_ge(root, 4)
                d.step(dve, nc.vector.reciprocal(pi[:, :, :], pi[:, :, :]))
                nc.vector.tensor_tensor(kk[:, :, :], kk[:, :, :], pi[:, :, :], ALU.mult).then_inc(kk_done, 1)
                dve.wait_ge(kk_done, 1)
                for p in pairs:
                    ins = nc.vector.tensor_scalar(tmp[:, p, :], av[:, p, :], 1.0, vec[:, V_KA + p:V_KA + p + 1],
                                                  ALU.subtract, ALU.mult)
                d.step(dve, ins)
                d.step(dve, nc.vector.scalar_tensor_tensor(xk, tmp[:, :, :], 1.0, xk, ALU.add, ALU.mult))
                for p in pairs:
                    nc.vector.scalar_tensor_tensor(tmp[:, p, :], xr[:, p, :], vec[:, V_RK + p:V_RK + p + 1],
                                                   xk[:, p, :], ALU.mult, ALU.mult).then_inc(rkk, 1)
                nc.vector.tensor_tensor(av[:, :, :], kk[:, :, :], av[:, :, :], ALU.mult).then_inc(k_ok, 1)
                dve.wait_ge(k_ok, 1)
                for p in pairs:
                    dve.wait_ge(bonus, p + 1)
                    nc.vector.tensor_tensor(m.bv[:, p, :], ps[:, 4 + p, 0:T], xv[:, p, :], ALU.mult).then_inc(
                        bonus_used, 1)
                dve.wait_ge(p_ready, 3 * 4 + 3)
                dve.wait_ge(z.sem, 6)
                products(nc.vector, (("ar", 0, px, kk), ("be", 0, av, pi), ("ar", 1, pc, xr)))
                nc.vector.tensor_copy(m.plast[:, :, 0:NCR], pc[:, :, CR - 1:TP:CR])
                nc.vector.tensor_copy(m.plast[:, :, NCR:], pc[:, :, TP + TS - 1::TS])

            @block.scalar
            def _(act):
                act.wait_ge(lo_ready, 1)
                nc.scalar.activation(thx[0:64, :], xm[0:64, 12, :], ACT.Tanh).then_inc(th_ready, 1)
                nc.scalar.activation(sg[:, :], xm[:, 13, :], ACT.Tanh, scale=0.5).then_inc(th_ready, 1)
                for i, (t0, n) in enumerate(TILES):
                    act.wait_ge(z_done, i + 1)
                    nc.scalar.activation(wl[:n, i, :], ps[:n, i, :], ACT.Tanh, scale=0.5).then_inc(z_t, 1)
                act.wait_ge(sq_ready, 1)
                for p in pairs:
                    act.wait_ge(a_done, p + 1)
                    nc.scalar.activation(av[:, p, :], ps[:, 4 + p, 0:T], ACT.Tanh, bias=rkc[:, p:p + 1],
                                         scale=0.5).then_inc(a_t, 1)
                for p in pairs:
                    act.wait_ge(g_done, p + 1)
                    nc.scalar.copy(m.gate[:, p, :], ps[:, p, 0:T]).then_inc(gate_ok, 1)
                for p in pairs:
                    act.wait_ge(ss_done, p + 1)
                    nc.scalar.activation(pi[:, p, :], ps[:, 4 + p, 0:T], ACT.Sqrt, bias=eps[:, 0:1]).then_inc(root, 1)
                act.wait_ge(kk_done, 1)
                for p in pairs:
                    act.wait_ge(cs_done, p + 1)
                    v = ps[:, p, :].rearrange("p (i j t) -> p i j t", i=2, j=2)
                    for dst, j, s in ((px, 0, 1.0), (pc, 1, 1.0), (pi, 1, -1.0)):
                        nc.scalar.activation(dst[:, p, 0:TP].rearrange("p (i t) -> p i t", i=2), v[:, :, j, :],
                                             ACT.Exp, scale=s).then_inc(p_ready, 1)
                act.wait_ge(cs_done, 5)
                v = ps[:, 4, 0:256].rearrange("p (q j t) -> p q j t", q=4, j=2)
                for dst, j, s in ((px, 0, 1.0), (pc, 1, 1.0), (pi, 1, -1.0)):
                    nc.scalar.activation(dst[:, :, TP:], v[:, :, j, :], ACT.Exp, scale=s).then_inc(p_ready, 1)

            @block.tensor
            def _(pe):
                pe.wait_ge(ones_row, 1)
                pe.wait_ge(th_ready, 1)
                for i, (t0, n) in enumerate(TILES):
                    nc.tensor.matmul(ps[:n, i, :], thx[:, t0:t0 + n], m.w2x[:, :], start=True,
                                     stop=True).then_inc(z_done, 1)
                for p in pairs:
                    nc.tensor.matmul(ps[:, 4 + p, 0:T], m.a2[64:P, p * P:(p + 1) * P], xm[64:P, 12, :], start=True,
                                     stop=True).then_inc(a_done, 1)
                pe.wait_ge(sg_t, 1)
                pe.wait_ge(z_t, 3)
                for p in pairs:
                    nc.tensor.matmul(ps[:, p, 0:T], m.g2[:, p * P:(p + 1) * P], sg[:, :], start=True,
                                     stop=True).then_inc(g_done, 1)
                pe.wait_ge(sq_ready, 1)
                pe.wait_ge(a_t, 4)
                for p in pairs:
                    nc.tensor.matmul(ps[:, 4 + p, 0:T], m.head64[:], tmp[:, p, :], start=True,
                                     stop=True).then_inc(ss_done, 1)
                pe.wait_ge(wl_ready, 3)
                pe.wait_ge(gate_ok, 4)
                for p in pairs:
                    for i in range(2):
                        ins = nc.tensor.matmul(ps[:, p, 256 * i:256 * i + 256], wl[:, i, p * P:(p + 1) * P],
                                               m.tr64[:, :, :], start=True, stop=True)
                    ins.then_inc(cs_done, 1)
                for p in pairs:
                    pe.wait_ge(rkk, p + 1)
                    pe.wait_ge(root, 4)
                    nc.tensor.matmul(ps[:, 4 + p, 0:T], m.head64[:], tmp[:, p, :], start=True,
                                     stop=True).then_inc(bonus, 1)
                pe.wait_ge(bonus_used, 1)
                for p in pairs:
                    ins = nc.tensor.matmul(ps[:, 4, 64 * p:64 * p + 64], wl[:NS, 2, p * P:(p + 1) * P],
                                           m.tr4[:NS, :, 0:NS], start=True, stop=True)
                ins.then_inc(cs_done, 1)

        NJ = CW - 1
        v_s = sb(st, "v_s", [P, 2, 2, 2 * NS])
        last = sb(st, "last", [P, R_TILES, 1 + NB])
        lastc = sb(st, "lastc", [P, C_TILES, (1 + NB) * NJ])
        row = sb(st, "row", [1 + NB, R_PROJ])
        rowc = sb(st, "rowc", [(1 + NB) * NJ, CONV])
        turned, kept, spread, zeroed = sem("turned"), sem("kept"), sem("spread"), sem("zeroed2")
        picked, rows_t, moved, stored = sem("picked"), sem("rows_t"), sem("moved"), sem("stored")
        with nc.Block() as block:
            @block.gpsimd
            def _(pool):
                nc.gpsimd.memset(v_e[:, :, :], 0.0).then_inc(zeroed, 1)
                pool.wait_ge(zeroed, 1)
                nc.gpsimd.memset(v_s[:, :, :, :], 0.0).then_inc(zeroed, 1)

            @block.scalar
            def _(act):
                act.wait_ge(zeroed, 2)
                for h in range(2):
                    r = slice(64 * h, 64 * h + 64)
                    ins = nc.scalar.copy(v_s[r, :, :, NS * h:NS * h + NS],
                                         xv[r, :, TP:].rearrange("p (i j) t -> p i j t", i=2))
                ins.then_inc(spread, 1)
                for c in range(NCR):
                    if c:
                        act.wait_ge(turned, c + 1)
                    for h in range(2):
                        r = slice(64 * h, 64 * h + 64)
                        ins = nc.scalar.copy(v_e[r, :, CR * h:CR * h + CR], xv[r, :, c * CR:c * CR + CR])
                    ins.then_inc(spread, 1)
                    if c == 0:
                        act.wait_ge(rows_t, 1)
                        for i in range(4):
                            n = min(512, R_PROJ - 512 * i)
                            ins = nc.scalar.copy(row[:, 512 * i:512 * i + n], ps[:1 + NB, 3 + i, 0:n])
                        ins.then_inc(moved, 1)
                    if c == 1:
                        act.wait_ge(rows_t, 2)
                        for i in range(3):
                            ins = nc.scalar.copy(rowc[:, 512 * i:512 * i + 512], ps[:(1 + NB) * NJ, 3 + i, :])
                        ins.then_inc(moved, 1)

            @block.sync
            def _(sp):
                sp.wait_ge(moved, 1)
                sp.dma_start(out[3][0], row[0:1, :]).then_inc(stored, 16)
                sp.dma_start(out[9][0], row[1:1 + NB, :]).then_inc(stored, 16)
                sp.wait_ge(moved, 2)
                sp.dma_start(out[5][0, 0], rowc[0:NJ, :]).then_inc(stored, 16)
                sp.dma_start(out[11][0].rearrange("b j n -> (b j) n"), rowc[NJ:, :]).then_inc(stored, 16)
                sp.wait_ge(stored, 64)

            @block.tensor
            def _(pe):
                pe.wait_ge(spread, 1)
                for p in pairs:
                    r = slice(64 * (p % 2), 64 * (p % 2) + 64)
                    ins = nc.tensor.matmul(ps[r, 2, (p // 2) * P:(p // 2) * P + P], v_s[:, p // 2, p % 2, :], ident[:],
                                           start=True, stop=True)
                ins.then_inc(turned, 1)
                pe.wait_ge(picked, 1)
                for i in range(R_TILES):
                    ins = nc.tensor.transpose(ps[:1 + NB, 3 + i // 4, P * (i % 4):P * (i % 4) + P], last[:, i, :],
                                              ident[:])
                ins.then_inc(rows_t, 1)
                for c in range(NCR):
                    pe.wait_ge(spread, c + 2)
                    if c >= 2:
                        pe.wait_ge(kept, c)
                    for p in pairs:
                        ins = nc.tensor.transpose(ps[:, c % 2, p * P:(p + 1) * P], v_e[:, p, :], ident[:])
                    ins.then_inc(turned, 1)
                    if c == 0:
                        pe.wait_ge(picked, 2)
                        pe.wait_ge(moved, 1)
                        for i in range(C_TILES):
                            ins = nc.tensor.transpose(
                                ps[:(1 + NB) * NJ, 3 + i // 4, P * (i % 4):P * (i % 4) + P], lastc[:, i, :], ident[:])
                        ins.then_inc(rows_t, 1)

            @block.vector
            def _(dve):
                pg = m.pg
                nc.vector.tensor_copy(last[:, :, 0:1], pr[:, :, TP:TP + 1])
                nc.vector.tensor_copy(last[:, :, 1:], pr[:, :, 1 + TP + TS::1 + TS]).then_inc(picked, 1)
                nc.vector.tensor_copy(lastc[:, :, 0:NJ], pg[:, :, TP:TP + NJ])
                nc.vector.tensor_copy(lastc[:, :, NJ:].rearrange("p i (b j) -> p i b j", j=NJ),
                                      pg[:, :, NJ + TP:].rearrange("p i (b u) -> p i b u", u=NJ + TS)[:, :, :, TS:]
                                      ).then_inc(picked, 1)
                dve.wait_ge(turned, 1)
                for q in range(4):
                    r, h = slice(NS * q, NS * q + NS), q % 2
                    ins = nc.vector.tensor_copy(m.v_c[r, 16:18, :], ps[r, 2, 0:256].rearrange(
                        "p (i v) -> p i v", i=2)[:, :, NR * h:NR * h + NR])
                ins.then_inc(kept, 1)
                for c in range(NCR):
                    dve.wait_ge(turned, c + 2)
                    for h in range(2):
                        r = slice(64 * h, 64 * h + 64)
                        ins = nc.vector.tensor_copy(
                            m.v_c[r, 4 * c:4 * c + 4, :],
                            ps[r, c % 2, :].rearrange("p (q v) -> p q v", q=4)[:, :, NR * h:NR * h + NR])
                    ins.then_inc(kept, 1)


def gdn_elementwise(nc, a, sb, ps, ident, ones, eps, m):
    with ExitStack() as st:
        sem = semaphores(nc, st, "gd")
        cv = sb(st, "cv", [P, C_TILES, T])
        th = sb(st, "th", [P, C_TILES, T])
        cwh = sb(st, "cwh", [P, 48])
        gm = sb(st, "gm", [P, HG * NB])
        nrm = sb(st, "nrm", [8, T])
        col8 = sb(st, "col8", [P, 8, 8])
        row8 = sb(st, "row8", [8, 8, P])
        inv_ok, spread, sqd = sem("inv_ok"), sem("spread"), sem("sqd")
        d, g = Count(sem("dve")), Count(sem("pool"))
        conv_v, conv_p, cw_ok, th_v, sq, ss, root, zh, zth = (
            sem(n) for n in ("conv_v", "conv_p", "cw", "th", "sq", "ss", "root", "zh", "zth"))
        bt, bt_ok, x_ok, ex, ln, gs, gc, sc_t, gm_ok, egc = (
            sem(n) for n in ("bt", "bt_ok", "x", "ex", "ln", "g", "gc", "sc_t", "gm", "egc"))
        sc, vec = m.sc, m.vec
        gv_ok = sem("gv_ok")
        NV = 10

        pgs = m.pg[:, :, CW - 1 + TP:].rearrange("p i (b u) -> p i b u", u=CW - 1 + TS)

        def convolve(eng, ops, i0, i1, chain, done, fused, taps=range(CW)):
            for j in taps:
                for i in range(i0, i1):
                    w = cwh[:, 12 * j + i:12 * j + i + 1]
                    to = cv if fused or j == 0 else th
                    ts = to[:, i, TP:].rearrange("p (b u) -> p b u", u=TS)
                    for dst, src in ((to[:, i, 0:TP], m.pg[:, i, j:j + TP]), (ts, pgs[:, i, :, j:j + TS])):
                        if j == 0 or not fused:
                            ins = ops.tensor_scalar(dst, src, w, None, ALU.mult)
                        else:
                            ins = ops.scalar_tensor_tensor(dst, src, w, dst, ALU.mult, ALU.add)
                if j and not fused:
                    chain.step(eng, ins)
                    ins = ops.tensor_tensor(cv[:, i0:i1, :], cv[:, i0:i1, :], th[:, i0:i1, :], ALU.add)
                if j < CW - 1:
                    chain.step(eng, ins)
                else:
                    ins.then_inc(done, 1)

        with nc.Block() as block:
            @block.vector
            def _(dve):
                nc.vector.tensor_scalar(cwh[:, :], vec[:, V_CW:V_CW + 48], 0.5, None, ALU.mult).then_inc(cw_ok, 1)
                nc.vector.memset(col8[:, :, :], 0.0)
                nc.vector.tensor_copy(row8[:, :, :], over(ident[:8, :8], P, 2))
                d.step(dve, nc.vector.memset(sc[:, :, :], 0.0))
                nc.vector.memset(col8[:, :, :].rearrange("p i j -> p (i j)")[:, 0::9], 1.0)
                for j, row in ((0, S_DT), (1, S_AL)):
                    for i in range(2):
                        nc.vector.tensor_copy(sc[:, row, 4 * i:4 * i + 4], m.dtb[:, j, :])
                    for h in range(HG):
                        r = slice(NS * h, NS * h + NS)
                        ins = nc.vector.tensor_copy(sc[r, row, 8:9], m.dtb[r, j, h:h + 1])
                dve.wait_ge(bt, 1)
                for j, row in ((0, S_BE), (1, S_X)):
                    nc.vector.tensor_copy(sc[:, row, 0:8].rearrange("p (i h) -> p i h", i=2),
                                          ps[:, 0, 0:16].rearrange("p (i j h) -> p i j h", i=2, j=2)[:, :, j, :])
                    for h in range(HG):
                        r = slice(NS * h, NS * h + NS)
                        ins = nc.vector.tensor_copy(sc[r, row, 8:9], ps[r, 0, 16 + 4 * j + h:17 + 4 * j + h])
                d.step(dve, ins)
                d.step(dve, nc.vector.tensor_tensor(sc[:, S_X, :], sc[:, S_X, :], sc[:, S_DT, :], ALU.add))
                d.step(dve, nc.vector.tensor_scalar(sc[:, S_Y, :], sc[:, S_X, :], -1.0, None, ALU.mult))
                nc.vector.tensor_tensor(sc[:, S_Y, :], sc[:, S_X, :], sc[:, S_Y, :], ALU.max).then_inc(x_ok, 1)
                dve.wait_ge(cw_ok, 1)
                convolve(dve, nc.vector, 0, NV, d, conv_v, True, (0,))
                dve.wait_ge(ln, 1)
                d.step(dve, nc.vector.tensor_scalar(sc[:, S_X, :], sc[:, S_X, :], 0.0, None, ALU.max))
                d.step(dve, nc.vector.tensor_tensor(sc[:, S_X, :], sc[:, S_X, :], sc[:, S_U, :], ALU.add))
                nc.vector.tensor_scalar(sc[:, S_BE, :], sc[:, S_BE, :], 0.5, 0.5, ALU.mult, ALU.add)
                d.step(dve, nc.vector.scalar_tensor_tensor(sc[:, S_G, :], sc[:, S_X, :], -1.0, sc[:, S_AL, :],
                                                           ALU.mult, ALU.mult))
                nc.vector.tensor_scalar(gm[:, :], m.bm4[:, :, :].rearrange("p m b -> p (m b)"), sc[:, S_G, 8:9], None,
                                        ALU.mult).then_inc(gs, 1)
                convolve(dve, nc.vector, 0, NV, d, conv_v, True, (1, 2))
                dve.wait_ge(gc, 1)
                nc.vector.tensor_copy(sc[:, S_GC, :], ps[:, 1, 0:9])
                nc.vector.tensor_copy(m.glb[:, :], ps[:, 1, 32:64])
                d.step(dve, nc.vector.tensor_copy(sc[:, S_GL, :], ps[:, 1, 16:25]))
                nc.vector.tensor_tensor(sc[:, S_KT, :], sc[:, S_GL, :], sc[:, S_GC, :], ALU.subtract).then_inc(gm_ok, 1)
                convolve(dve, nc.vector, 0, NV, d, conv_v, True, (3,))
                dve.wait_ge(egc, 2)
                nc.vector.tensor_scalar(sc[:, S_NEG, :], sc[:, S_EG, :], -1.0, None, ALU.mult)
                for i in range(2):
                    dve.wait_ge(th_v, i + 1)
                    nc.vector.scalar_tensor_tensor(cv[:, 4 * i:4 * i + 4, :], th[:, 4 * i:4 * i + 4, :], 1.0,
                                                   cv[:, 4 * i:4 * i + 4, :], ALU.add, ALU.mult).then_inc(sq, 1)
                dve.wait_ge(th_v, 3)
                nc.vector.scalar_tensor_tensor(m.gv[:, :, :], th[:, 8:12, :], 1.0, cv[:, 8:12, :], ALU.add,
                                               ALU.mult).then_inc(gv_ok, 1)
                dve.wait_ge(root, 1)
                nc.vector.reciprocal(nrm[:, :], nrm[:, :]).then_inc(inv_ok, 1)
                dve.wait_ge(spread, 1)
                nc.vector.scalar_tensor_tensor(m.qk[:, 1, :, :], cv[:, 0:4, :], DG ** -0.5, ps[:, 0:4, 0:T], ALU.mult,
                                               ALU.mult)
                dve.wait_ge(spread, 2)
                nc.vector.tensor_tensor(m.qk[:, 0, :, :], cv[:, 4:8, :], ps[:, 4:8, 0:T], ALU.mult)
                dve.wait_ge(zth, 1)
                nc.vector.scalar_tensor_tensor(m.zt[:, :, :], cv[:, 8:12, :], 1.0, m.zt[:, :, :], ALU.add, ALU.mult)

            @block.sync
            def _(sp):
                for h in range(HG):
                    sp.dma_start(m.sst[:, h], a["state_gdn"][0, :, h].rearrange("b k v -> k b v")).then_inc(m.states_in, 16)
                sp.wait_ge(m.cleared, 1)
                for p in range(PAIRS):
                    for h in range(2):
                        r = slice(64 * h, 64 * h + 64)
                        sp.dma_start(m.stage_t[r, p, :, r],
                                     a["state_rwkv"][0, :, 2 * p + h].rearrange("b v k -> v b k")).then_inc(m.states_in, 16)

            @block.gpsimd
            def _(pool):
                pool.wait_ge(cw_ok, 1)
                convolve(pool, nc.gpsimd, NV, C_TILES, g, conv_p, False)
                nc.gpsimd.tensor_scalar(m.zt[:, :, :], m.zt[:, :, :], 0.5, None, ALU.mult).then_inc(zh, 1)
                nc.gpsimd.memset(m.stage_t, 0.0).then_inc(m.cleared, 1)
                zero_dead(nc, st)

            @block.scalar
            def _(act):
                act.wait_ge(x_ok, 1)
                nc.scalar.activation(sc[:, S_BE, :], sc[:, S_BE, :], ACT.Tanh, scale=0.5)
                nc.scalar.activation(sc[:, S_AL, :], sc[:, S_AL, :], ACT.Exp)
                nc.scalar.activation(sc[:, S_U, :], sc[:, S_Y, :], ACT.Exp, scale=-1.0).then_inc(ex, 1)
                act.wait_ge(ex, 1)
                nc.scalar.activation(sc[:, S_U, :], sc[:, S_U, :], ACT.Ln, bias=1.0).then_inc(ln, 1)
                act.wait_ge(gm_ok, 1)
                nc.scalar.activation(sc[:, S_EG, :], sc[:, S_GC, :], ACT.Exp).then_inc(egc, 1)
                nc.scalar.activation(sc[:, S_KT, :], sc[:, S_KT, :], ACT.Exp)
                nc.scalar.activation(sc[:, S_GL, :], sc[:, S_GL, :], ACT.Exp)
                nc.scalar.activation(m.glb[:, :], m.glb[:, :], ACT.Exp).then_inc(egc, 1)
                act.wait_ge(conv_v, 1)
                for i in range(2):
                    nc.scalar.activation(th[:, 4 * i:4 * i + 4, :], cv[:, 4 * i:4 * i + 4, :], ACT.Tanh).then_inc(
                        th_v, 1)
                act.wait_ge(conv_p, 1)
                nc.scalar.activation(th[:, 8:12, :], cv[:, 8:12, :], ACT.Tanh).then_inc(th_v, 1)
                for i in range(2):
                    act.wait_ge(sq, i + 1)
                    nc.scalar.activation(th[:, 4 * i:4 * i + 4, :], cv[:, 4 * i:4 * i + 4, :], ACT.Square).then_inc(
                        sqd, 1)
                act.wait_ge(zh, 1)
                act.wait_ge(ss, 1)
                nc.scalar.activation(nrm[:, :], ps[:8, 0, 0:T], ACT.Sqrt, bias=eps[:8, 0:1]).then_inc(root, 1)
                act.wait_ge(gv_ok, 1)
                nc.scalar.activation(cv[:, 8:12, :], m.zt[:, :, :], ACT.Tanh).then_inc(zth, 1)

            @block.tensor
            def _(pe):
                for i in range(2):
                    nc.tensor.transpose(ps[:, 0, 8 * i:8 * i + 8], m.ba[:, P * i:P * i + P], ident[:8, :8])
                for h in range(HG):
                    ins = nc.tensor.matmul(ps[NS * h:NS * h + NS, 0, 16:24], m.ba[:, TP:T], ident[:8, :8],
                                           start=True, stop=True, tile_position=(0, NS * h))
                ins.then_inc(bt, 1)
                pe.wait_ge(gs, 1)
                nc.tensor.matmul(ps[:, 1, 0:8], m.tri[:], sc[:, S_G, 0:8], start=True, stop=True)
                nc.tensor.matmul(ps[:, 1, 8:9], m.tr4[:, 1, :], sc[:, S_G, 8:9], start=True, stop=True)
                nc.tensor.matmul(ps[:, 1, 16:24], ones[:], sc[:, S_G, 0:8], start=True, stop=True)
                nc.tensor.matmul(ps[:, 1, 24:25], m.blk4[:], sc[:, S_G, 8:9], start=True, stop=True)
                nc.tensor.matmul(ps[:, 1, 32:64], ones[:], gm[:, :], start=True, stop=True).then_inc(gc, 1)
                pe.wait_ge(egc, 2)
                for i in range(8):
                    pe.wait_ge(sqd, i // 4 + 1)
                    ins = nc.tensor.matmul(ps[:8, 0, 0:T], col8[:, i, :], th[:, i, :], start=(i == 0), stop=(i == 7))
                ins.then_inc(ss, 1)
                pe.wait_ge(inv_ok, 1)
                for i in range(8):
                    ins = nc.tensor.matmul(ps[:, i, 0:T], row8[:, i, :], nrm[:, :], start=True, stop=True)
                    if i % 4 == 3:
                        ins.then_inc(spread, 1)


def over(ap, n, at=1):
    v = ap.unsqueeze(at)
    shape = list(v.shape)
    shape[at] = n
    return v.broadcast_to(shape)


def invert(nc, sb, ps, ident, m, name, groups):
    with ExitStack() as st:
        sem = semaphores(nc, st, name)
        ng = len(groups)
        ct = [sb(st, f"{name}_ct{g}", [P, n, P]) for g, (_, _, n, _) in enumerate(groups)]
        tt = [sb(st, f"{name}_t{g}", [P, n, P]) for g, (_, _, n, _) in enumerate(groups)]
        xt = [sb(st, f"{name}_x{g}", [P, n, P]) for g, (_, _, n, _) in enumerate(groups)]
        init, c_ok = Count(sem("init")), sem("c_ok")
        t_done, t_ok = [sem(f"t_done{g}") for g in range(ng)], [sem(f"t_ok{g}") for g in range(ng)]
        x_done, x_ok = [sem(f"x_done{g}") for g in range(ng)], [sem(f"x_ok{g}") for g in range(ng)]
        z_done, z_ok = [sem(f"z_done{g}") for g in range(ng)], [sem(f"z_ok{g}") for g in range(ng)]
        steps = [(lv, g) for lv in range(1, max(q[3] for q in groups)) for g in range(ng) if lv < groups[g][3]]
        levels = sorted({lv for lv, _ in steps})
        order = [(kind, lv, g) for lv in levels for kind in "TXZ" for l2, g in steps if l2 == lv]
        emptied = {"T": t_ok, "X": x_ok, "Z": z_ok}
        bank = {q: i % 8 for i, q in enumerate(order)}

        def out_of(q):
            n = groups[q[2]][2]
            return ps[:, bank[q], 0:n * P].rearrange("p (u t) -> p u t", u=n)

        with nc.Block() as block:
            @block.gpsimd
            def _(pool):
                done = 0
                for lv, g in steps:
                    at, _, n, _ = groups[g]
                    if lv > 1:
                        pool.wait_ge(x_done[g], lv - 1)
                    if done:
                        pool.wait_ge(c_ok, done)
                    nc.gpsimd.tensor_tensor(ct[g][:, :, :], at, over(m.lvl[:, lv, :], n), ALU.mult).then_inc(c_ok, 1)
                    done += 1

            @block.vector
            def _(dve):
                for at, ttr, n, _ in groups:
                    ins = nc.vector.tensor_tensor(ttr, at, over(m.lvl[:, 0, :], n), ALU.mult)
                init.step(dve, ins)
                for at, ttr, n, _ in groups:
                    init.inc(nc.vector.tensor_tensor(ttr, over(ident[:], n), ttr, ALU.subtract))
                dve.wait_ge(init.sem, 1 + ng)
                for lv, g in steps:
                    dve.wait_ge(z_done[g], lv)
                    ttr = groups[g][1]
                    nc.vector.tensor_tensor(ttr, ttr, out_of(("Z", lv, g)), ALU.subtract).then_inc(z_ok[g], 1)

            @block.scalar
            def _(act):
                for kind, lv, g in order:
                    if kind == "T":
                        act.wait_ge(t_done[g], lv)
                        nc.scalar.copy(tt[g][:, :, :], out_of((kind, lv, g))).then_inc(t_ok[g], 1)
                    if kind == "X":
                        act.wait_ge(x_done[g], lv)
                        nc.scalar.copy(xt[g][:, :, :], out_of((kind, lv, g))).then_inc(x_ok[g], 1)

            @block.tensor
            def _(pe):
                for i, (kind, lv, g) in enumerate(order):
                    if i >= 8:
                        k8, l8, g8 = order[i - 8]
                        pe.wait_ge(emptied[k8][g8], l8)
                    _, ttr, n, _ = groups[g]
                    if kind == "T":
                        pe.wait_ge(init.sem, 2 + g)
                        if lv > 1:
                            pe.wait_ge(z_ok[g], lv - 1)
                    elif kind == "X":
                        pe.wait_ge(t_ok[g], lv)
                        pe.wait_ge(c_ok, steps.index((lv, g)) + 1)
                    else:
                        pe.wait_ge(x_ok[g], lv)
                    dst = out_of((kind, lv, g))
                    for u in range(n):
                        if kind == "T":
                            ins = nc.tensor.transpose(dst[:, u, :], ttr[:, u, :], ident[:])
                        elif kind == "X":
                            ins = nc.tensor.matmul(dst[:, u, :], ct[g][:, u, :], tt[g][:, u, :], start=True, stop=True)
                        else:
                            ins = nc.tensor.matmul(dst[:, u, :], xt[g][:, u, :], ttr[:, u, :], start=True, stop=True)
                    ins.then_inc({"T": t_done, "X": x_done, "Z": z_done}[kind][g], 1)


def sample_step(nc, a, out, sb, ps, ident, ones, m):
    with ExitStack() as st:
        sem = semaphores(nc, st, "sa")
        stage_t, sst = m.stage_t, m.sst
        mst = sb(st, "mst", [P, PAIRS, NB, NR])
        mb = sb(st, "s_mb", [P, 2, 2, P])
        mk = sb(st, "s_mk", [P, 2, 2, P])
        gmx = sb(st, "s_gm", [P, 2, P])
        dt = sb(st, "s_dt", [P, P])
        dtm = sb(st, "s_dtm", [P, 2, P])
        gb = sb(st, "s_gb", [P, P])
        tmt = sb(st, "s_tmt", [P, 2, 2, P])
        kv = sb(st, "s_kv", [P, 2, P])
        tinv = sb(st, "s_tinv", [P, 3, P])
        ati = sb(st, "s_ati", [P, 3, P])
        qs_, ks_ = m.qk[:, 1, :, TP:], m.qk[:, 0, :, TP:]
        gb_ok, mm, ev, dd, de = (sem(n) for n in ("gb", "mm", "ev", "dd", "de"))
        dch = Count(sem("dve"))
        ks_c = sb(st, "s_ksc", [P, 2, P])
        gvs = sb(st, "s_gvs", [P, P])
        with nc.Block() as block:
            @block.gpsimd
            def _(pool):
                nc.gpsimd.tensor_scalar(gb[:, :], ones[:], m.sc[:, S_G, 8:9], None, ALU.mult).then_inc(gb_ok, 1)

            @block.tensor
            def _(pe):
                for q, w in ((0, m.be_s), (1, m.ka_s)):
                    for p2 in range(2):
                        for pp in range(2):
                            r = slice(64 * pp, 64 * pp + 64)
                            ins = nc.tensor.matmul(ps[r, 2 * q + p2, 0:256], w[:, p2, pp, :],
                                                   m.ar_s[:, p2].rearrange("p j q t -> p (j q t)"), start=True, stop=True)
                            nc.tensor.matmul(ps[r, 6, 256 * q + P * p2:256 * q + P * p2 + P], w[:, p2, pp, :],
                                             ident[:], start=True, stop=True)
                        ins.then_inc(mm, 1)
                pe.wait_ge(gb_ok, 1)
                nc.tensor.matmul(ps[:, 4, 0:P], gb[:, :], m.tr4[:, 1, :], start=True, stop=True).then_inc(mm, 1)
                pe.wait_ge(ev, 1)
                nc.tensor.matmul(ps[:, 5, 0:256], ks_c[:, 0, :], ks_c[:, :, :].rearrange("p j t -> p (j t)"),
                                 start=True, stop=True).then_inc(mm, 1)
                nc.tensor.transpose(ps[:, 7, 0:P], ks_c[:, 0, :], ident[:])
                nc.tensor.transpose(ps[:, 7, P:2 * P], gvs[:, :], ident[:]).then_inc(mm, 1)

            @block.vector
            def _(dve):
                nc.vector.tensor_copy(gvs[:, :].rearrange("p (h t) -> p h t", h=HG), m.gv[:, :, TP:])
                nc.vector.tensor_copy(ks_c[:, :, :].rearrange("p j (h t) -> p j h t", h=HG),
                                      m.qk[:, :, :, TP:]).then_inc(ev, 1)
                for i in range(4):
                    dve.wait_ge(mm, i + 1)
                    dst = (mb, mk)[i // 2]
                    nc.vector.tensor_tensor(dst[:, i % 2, :, :].rearrange("p j t -> p (j t)"), ps[:, i, 0:256],
                                            m.tr4[:, :, :].rearrange("p j t -> p (j t)"), ALU.mult)
                dve.wait_ge(mm, 5)
                nc.vector.tensor_scalar(dt[:, :], ps[:, 4, 0:P], m.sc[:, S_GC, 8:9], 0.0, ALU.subtract,
                                        ALU.min).then_inc(dd, 1)
                dve.wait_ge(de, 1)
                nc.vector.scalar_tensor_tensor(dtm[:, 0, :], dt[:, :], m.sc[:, S_BE, 8:9], m.tr4[:, 0, :], ALU.mult,
                                               ALU.mult)
                dch.step(dve, nc.vector.tensor_tensor(dtm[:, 1, :], dt[:, :], m.tr4[:, 1, :], ALU.mult))
                dve.wait_ge(mm, 7)
                dch.step(dve, nc.vector.tensor_tensor(gmx[:, :, :].rearrange("p j t -> p (j t)"), ps[:, 5, 0:256],
                                                      dtm[:, :, :].rearrange("p j t -> p (j t)"), ALU.mult))
                nc.vector.tensor_copy(ati[:, 0, :], gmx[:, 0, :])
                nc.vector.tensor_copy(ati[:, 1:3, :], mb[:, :, 0, :])
                nc.vector.tensor_scalar(kv[:, 0, :], ps[:, 7, 0:P], m.sc[:, S_KT, 8:9], None, ALU.mult)
                nc.vector.tensor_copy(kv[:, 1, :], ps[:, 7, P:2 * P])
                nc.vector.tensor_copy(tmt[:, :, :, :].rearrange("p q i k -> p (q i k)"), ps[:, 6, :])

            @block.scalar
            def _(act):
                act.wait_ge(dd, 1)
                nc.scalar.activation(dt[:, :], dt[:, :], ACT.Exp).then_inc(de, 1)

        turned = sem("turned")

        def turn_states(block):
            def gather(eng, copy, odd):
                for q in range(8):
                    if q % 2 == odd:
                        eng.wait_ge(turned, q + 1)
                        for h in range(2):
                            r = slice(64 * h, 64 * h + 64)
                            ins = copy(mst[r, q // 2, 4 * odd:4 * odd + 4, :],
                                       ps[r, q, :].rearrange("p (b k) -> p b k", b=4)[:, :, r])

            @block.tensor
            def _(pe):
                pe.wait_ge(m.states_in, 16 * 12)
                for q in range(8):
                    for b in range(4):
                        ins = nc.tensor.transpose(ps[:, q, P * b:P * b + P], stage_t[:, q // 2, 4 * (q % 2) + b, :],
                                                  ident[:])
                    ins.then_inc(turned, 1)

            @block.vector
            def _(dve):
                gather(dve, nc.vector.tensor_copy, 0)

            @block.scalar
            def _(act):
                gather(act, nc.scalar.copy, 1)

        with nc.Block() as block:
            turn_states(block)
        invert(nc, sb, ps, ident, m, "si", [(ati[:, :, :], tinv[:, :, :], 3, 2)])

        zt = sb(st, "s_z", [P, 2, NB, NR])
        zg = sb(st, "s_zg", [P, NB, DG])
        zs = sb(st, "s_zs", [P, 2, 2, NR])
        zgs = sb(st, "s_zgs", [P, 2, DG])
        rr = sb(st, "s_r", [P, 2, NR])
        un = sb(st, "s_un", [P, 2, NR])
        vm = sb(st, "s_vm", [P, 2, NB, NR])
        um, ugm = zt, zg
        r0 = sb(st, "s_r0", [P, DG])
        ug = sb(st, "s_ug", [P, DG])
        mm, ev = sem("mm2"), Count(sem("ev2"))
        vc = m.v_c[:, 16:18, :]
        with nc.Block() as block:
            @block.tensor
            def _(pe):
                for j in range(2):
                    for p2 in range(2):
                        for pp in range(2):
                            r = slice(64 * pp, 64 * pp + 64)
                            ins = nc.tensor.matmul(ps[r, 2 * j + p2, :], m.ar_s[:, p2, j, pp, :],
                                                   mst[:, 2 * p2 + pp].rearrange("p b v -> p (b v)"),
                                                   start=True, stop=True)
                        ins.then_inc(mm, 1)
                for j in range(2):
                    for half in range(2):
                        for h in range(HG):
                            r = slice(NS * h, NS * h + NS)
                            ins = nc.tensor.matmul(ps[r, 4 + 2 * j + half, :], ks_c[:, j, r],
                                                   sst[:, h, 4 * half:4 * half + 4, :].rearrange("p b v -> p (b v)"),
                                                   start=True, stop=True, tile_position=(0, NS * h))
                        ins.then_inc(mm, 1)

            @block.vector
            def _(dve):
                bm = over(m.bmask[:, :], NR, 2)
                for j in range(2):
                    for p2 in range(2):
                        dve.wait_ge(mm, 2 * j + p2 + 1)
                        ins = nc.vector.tensor_tensor(zt[:, p2], ps[:, 2 * j + p2, :].rearrange("p (b v) -> p b v", b=NB),
                                                      bm, ALU.mult)
                    ev.step(dve, ins)
                    ev.step(dve, nc.vector.tensor_reduce(zs[:, j], zt[:, :, :, :].rearrange("p q b v -> p q v b"), AXX,
                                                         ALU.add))
                bm = over(m.bmask[:, :], DG, 2)
                for j in range(2):
                    dve.wait_ge(mm, 4 + 2 * j + 2)
                    for half in range(2):
                        b4 = slice(4 * half, 4 * half + 4)
                        ins = nc.vector.tensor_tensor(zg[:, b4], ps[:, 4 + 2 * j + half, :].rearrange(
                            "p (b v) -> p b v", b=4), over(m.bmask[:, b4], DG, 2), ALU.mult)
                    ev.step(dve, ins)
                    ev.step(dve, nc.vector.tensor_reduce(zgs[:, j], zg[:, :, :].rearrange("p b v -> p v b"), AXX,
                                                         ALU.add))
                nc.vector.tensor_tensor(vm[:, :, :, :], over(vc, NB, 2), over(over(m.bmask[:, :], NR, 2), 2), ALU.mult)
                nc.vector.scalar_tensor_tensor(r0[:, :], zgs[:, 0, :], m.sc[:, S_NEG, 8:9], kv[:, 1, :], ALU.mult,
                                               ALU.add)

        mm, ev = sem("mm3"), sem("ev3")
        with nc.Block() as block:
            @block.tensor
            def _(pe):
                for p2 in range(2):
                    ins = nc.tensor.matmul(ps[:, 0, 64 * p2:64 * p2 + 64], mk[:, p2, 0, :], vc[:, p2, :], start=True,
                                           stop=True)
                ins.then_inc(mm, 1)
                nc.tensor.matmul(ps[:, 1, 0:DG], tinv[:, 0, :], r0[:, :], start=True, stop=True).then_inc(mm, 1)
                pe.wait_ge(ev, 1)
                for p2 in range(2):
                    ins = nc.tensor.matmul(ps[:, 2, 64 * p2:64 * p2 + 64], tinv[:, 1 + p2, :], rr[:, p2, :], start=True,
                                           stop=True)
                ins.then_inc(mm, 1)
                pe.wait_ge(ev, 2)
                nc.tensor.matmul(ps[:, 3, 0:DG], gmx[:, 1, :], ug[:, :], start=True, stop=True).then_inc(mm, 1)
                pe.wait_ge(ev, 3)
                for p2 in range(2):
                    nc.tensor.matmul(ps[:, 4, 64 * p2:64 * p2 + 64], mk[:, p2, 1, :], vc[:, p2, :], start=True,
                                     stop=False)
                    ins = nc.tensor.matmul(ps[:, 4, 64 * p2:64 * p2 + 64], mb[:, p2, 1, :], un[:, p2, :], start=False,
                                           stop=True)
                ins.then_inc(mm, 1)

            @block.vector
            def _(dve):
                dve.wait_ge(mm, 1)
                nc.vector.tensor_tensor(rr[:, :, :].rearrange("p q v -> p (q v)"), ps[:, 0, 0:P],
                                        zs[:, 0].rearrange("p q v -> p (q v)"), ALU.add).then_inc(ev, 1)
                dve.wait_ge(mm, 2)
                nc.vector.tensor_scalar(ug[:, :], ps[:, 1, 0:DG], m.sc[:, S_BE, 8:9], None, ALU.mult).then_inc(ev, 1)
                dve.wait_ge(mm, 3)
                nc.vector.tensor_scalar(un[:, :, :].rearrange("p q v -> p (q v)"), ps[:, 2, 0:P], -1.0, None,
                                        ALU.mult).then_inc(ev, 1)
                dve.wait_ge(mm, 4)
                nc.vector.scalar_tensor_tensor(m.y_g[:, 8, :], zgs[:, 1, :], m.sc[:, S_EG, 8:9], ps[:, 3, 0:DG],
                                               ALU.mult, ALU.add)
                nc.vector.tensor_tensor(ugm[:, :, :], over(ug[:, :], NB), over(m.bmask[:, :], DG, 2), ALU.mult)
                dve.wait_ge(ev, 3)
                nc.vector.tensor_tensor(um[:, :, :, :], over(un[:, :, :], NB, 2), over(over(m.bmask[:, :], NR, 2), 2),
                                        ALU.mult)
                dve.wait_ge(mm, 5)
                nc.vector.tensor_tensor(m.y_r[:, 16:18, :].rearrange("p q v -> p (q v)"), ps[:, 4, 0:P],
                                        zs[:, 1].rearrange("p q v -> p (q v)"), ALU.add)

        mm, ev, ev2, stored = sem("mm4"), Count(sem("ev4")), sem("ev5"), sem("stored")
        with nc.Block() as block:
            @block.tensor
            def _(pe):
                for p in range(PAIRS):
                    p2, r = p // 2, slice(64 * (p % 2), 64 * (p % 2) + 64)
                    nc.tensor.matmul(ps[:, p, :], tmt[r, 1, p2, :], vm[r, p2].rearrange("p b v -> p (b v)"), start=True,
                                     stop=False)
                    nc.tensor.matmul(ps[:, p, :], tmt[r, 0, p2, :], um[r, p2].rearrange("p b v -> p (b v)"),
                                     start=False, stop=True).then_inc(mm, 1)
                for h in range(HG):
                    r = slice(NS * h, NS * h + NS)
                    if h >= 2:
                        pe.wait_ge(ev2, h - 1)
                    for half in range(2):
                        ins = nc.tensor.matmul(ps[:, 4 + 2 * (h % 2) + half, :], kv[r, 0, :],
                                               ugm[r, 4 * half:4 * half + 4, :].rearrange("p b v -> p (b v)"),
                                               start=True, stop=True, tile_position=(NS * h, 0))
                    ins.then_inc(mm, 1)

            @block.vector
            def _(dve):
                for h in range(HG):
                    ins = nc.vector.tensor_tensor(sst[:, h], sst[:, h], over(m.glb[:, NB * h:NB * h + NB], DG, 2),
                                                  ALU.mult)
                for p in range(PAIRS):
                    dve.wait_ge(mm, p + 1)
                    ins = nc.vector.tensor_tensor(mst[:, p].rearrange("p b v -> p (b v)"), ps[:, p, :],
                                                  mst[:, p].rearrange("p b v -> p (b v)"), ALU.add)
                ev.step(dve, ins)
                ev.step(dve, nc.vector.tensor_tensor(mst[:, :, :, :], mst[:, :, :, :],
                                                     over(m.plast[:, :, NCR:], NR, 3), ALU.mult))
                for h in range(2):
                    r = slice(64 * h, 64 * h + 64)
                    ins = nc.vector.tensor_copy(stage_t[r, :, :, r], mst[r, :, :, :])
                for h in range(HG):
                    dve.wait_ge(mm, 5 + h)
                    for half in range(2):
                        v = sst[:, h, 4 * half:4 * half + 4, :].rearrange("p b v -> p (b v)")
                        ins = nc.vector.tensor_tensor(v, ps[:, 4 + 2 * (h % 2) + half, :], v, ALU.add)
                    ins.then_inc(ev2, 1)

            @block.sync
            def _(sp):
                for h in range(HG):
                    sp.wait_ge(ev2, h + 1)
                    sp.dma_start(out[10][0, :, h].rearrange("b k v -> k b v"), sst[:, h]).then_inc(stored, 16)
        turned = sem("turned2")
        with nc.Block() as block:
            turn_states(block)
        with nc.Block() as block:
            @block.sync
            def _(sp):
                for p in range(PAIRS):
                    sp.dma_start(out[8][0].rearrange("b h v k -> (h v) b k")[P * p:P * p + P], mst[:, p]).then_inc(
                        stored, 16)
                sp.wait_ge(stored, 16 * 8)


def prompt_chunks(nc, out, sb, ps, ident, ones, m):
    with ExitStack() as st:
        sem = semaphores(nc, st, "pc")
        NU, NG = NCR * PAIRS, 2 * HG
        mb = m.pr[:, :, :].rearrange("p i w -> p (i w)")[:, 0:NU * 2 * P].rearrange(
            "p (u j t) -> p u j t", u=NU, j=2)
        tinv = m.pg[:, :, :].rearrange("p i w -> p (i w)")[:, 0:(NU + NG) * P].rearrange(
            "p (u t) -> p u t", u=NU + NG)
        mk = sb(st, "mk", [P, NU, 2, P])
        gmx = sb(st, "gmx", [P, NG, 2, P])
        kt = sb(st, "kt", [P, NG, P])
        vt = sb(st, "vt", [P, NG, P])
        be_tm = mb[:, :, 0, :]

        with ExitStack() as s1:
            gb = sb(s1, "gb", [P, NG, P])
            dt = sb(s1, "dt", [P, NG, P])
            dtm = sb(s1, "dtm", [P, NG, 2, P])
            gb_ok, pe_done, dd, de, dch = sem("gb"), sem("pe"), sem("dd"), sem("de"), Count(sem("dch"))
            v_done, a_done = sem("v_done"), sem("a_done")
            order = ([("row", 0), ("row", 1), ("kt", 0), ("kt", 1), ("vt", 0), ("vt", 1)]
                     + [("mb", c, h) for c in range(2) for h in range(2)] + [("gm", i, h) for i in range(2)
                                                                             for h in range(2)]
                     + [("mk", c, h) for c in range(2) for h in range(2)]
                     + [(w, c, h) for w in ("mb", "mk") for c in range(2, NCR) for h in range(2)])
            by_act = [q for q in order if q[0] in ("kt", "vt")]
            by_dve = [q for q in order if q not in by_act]
            bank = {q: i % 8 for i, q in enumerate(order)}
            with nc.Block() as block:
                @block.gpsimd
                def _(pool):
                    for u in range(NG):
                        if u:
                            pool.wait_ge(gb_ok, u)
                        nc.gpsimd.tensor_scalar(gb[:, u, :], ones[:], m.sc[:, S_G, u:u + 1], None,
                                                ALU.mult).then_inc(gb_ok, 1)

                @block.tensor
                def _(pe):
                    for i, q in enumerate(order):
                        if i >= 8:
                            old = order[i - 8]
                            if old in by_act:
                                pe.wait_ge(a_done, by_act.index(old) + 1)
                            else:
                                pe.wait_ge(v_done, by_dve.index(old) + 1)
                        b = bank[q]
                        if q[0] == "row":
                            for h in range(HG):
                                pe.wait_ge(gb_ok, 4 * q[1] + h + 1)
                                ins = nc.tensor.matmul(ps[:, b, P * h:P * h + P], gb[:, 4 * q[1] + h, :], m.tri[:],
                                                       start=True, stop=True)
                        elif q[0] in ("kt", "vt"):
                            src = m.qk[:, 0] if q[0] == "kt" else m.gv
                            for h in range(HG):
                                ins = nc.tensor.transpose(ps[:, b, P * h:P * h + P], src[:, h, P * q[1]:P * q[1] + P],
                                                          ident[:])
                        elif q[0] == "gm":
                            t = slice(P * q[1], P * q[1] + P)
                            for j in range(2):
                                h = 2 * q[2] + j
                                ins = nc.tensor.matmul(ps[:, b, 256 * j:256 * j + 256].rearrange(
                                    "p (j t) -> p j t", j=2), m.qk[:, 0, h, t], m.qk[:, :, h, t], start=True, stop=True)
                        else:
                            w = m.be_e if q[0] == "mb" else m.ka_e
                            for j in range(2):
                                u = PAIRS * q[1] + 2 * q[2] + j
                                ins = nc.tensor.matmul(ps[:, b, 256 * j:256 * j + 256], w[:, u, :],
                                                       m.ar_e[:, u].rearrange("p j t -> p (j t)"), start=True, stop=True)
                        ins.then_inc(pe_done, 1)

                @block.vector
                def _(dve):
                    for q in by_dve:
                        dve.wait_ge(pe_done, order.index(q) + 1)
                        b = ps[:, bank[q], :]
                        if q[0] == "row":
                            for h in range(HG):
                                u = 4 * q[1] + h
                                ins = nc.vector.tensor_scalar(dt[:, u, :], b[:, P * h:P * h + P],
                                                              m.sc[:, S_GC, u:u + 1], 0.0, ALU.subtract, ALU.min)
                            ins.then_inc(v_done, 1)
                        elif q[0] == "gm":
                            if q[1:] == (0, 0):
                                dve.wait_ge(de, 2)
                                for u in range(NG):
                                    nc.vector.scalar_tensor_tensor(dtm[:, u, 0, :], dt[:, u, :],
                                                                   m.sc[:, S_BE, u:u + 1], m.stri[:], ALU.mult, ALU.mult)
                                dch.step(dve, nc.vector.tensor_tensor(dtm[:, :, 1, :], dt[:, :, :],
                                                                      over(m.tri[:], NG), ALU.mult))
                            u = 4 * q[1] + 2 * q[2]
                            nc.vector.tensor_tensor(gmx[:, u:u + 2].rearrange("p u j t -> p (u j t)"), b,
                                                    dtm[:, u:u + 2].rearrange("p u j t -> p (u j t)"),
                                                    ALU.mult).then_inc(v_done, 1)
                        else:
                            u = PAIRS * q[1] + 2 * q[2]
                            dst = mb if q[0] == "mb" else mk
                            nc.vector.tensor_tensor(dst[:, u:u + 2], b.rearrange("p (u j t) -> p u j t", u=2, j=2),
                                                    over(m.tr64[:, :, :], 2), ALU.mult).then_inc(v_done, 1)

                @block.scalar
                def _(act):
                    for q in by_act:
                        act.wait_ge(pe_done, order.index(q) + 1)
                        b = ps[:, bank[q], :]
                        for h in range(HG):
                            u = 4 * q[1] + h
                            if q[0] == "kt":
                                ins = nc.scalar.activation(kt[:, u, :], b[:, P * h:P * h + P], ACT.Copy,
                                                           scale=m.sc[:, S_KT, u:u + 1])
                            else:
                                ins = nc.scalar.copy(vt[:, u, :], b[:, P * h:P * h + P])
                        ins.then_inc(a_done, 1)
                    act.wait_ge(v_done, 2)
                    for i in range(2):
                        nc.scalar.activation(dt[:, 4 * i:4 * i + 4], dt[:, 4 * i:4 * i + 4], ACT.Exp).then_inc(de, 1)

        for i in range(2):
            invert(nc, sb, ps, ident, m, f"pi{i}",
                   [(mb[:, 8 * i + 4 * c:8 * i + 4 * c + 4, 0, :], tinv[:, 8 * i + 4 * c:8 * i + 4 * c + 4, :], 4, 6)
                    for c in range(2)]
                   + [(gmx[:, 4 * i:4 * i + 4, 0, :], tinv[:, NU + 4 * i:NU + 4 * i + 4, :], 4, 7)])

        ka_tm = sb(st, "ka_tm", [P, NU, P])
        turned = sem("turned")
        with nc.Block() as block:
            @block.tensor
            def _(pe):
                for q in range(8):
                    for j in range(4):
                        src = (m.be_e, m.ka_e)[q % 2]
                        ins = nc.tensor.transpose(ps[:, q, P * j:P * j + P], src[:, 4 * (q // 2) + j, :], ident[:])
                    ins.then_inc(turned, 1)

            def gather(eng, copy, odd, dst):
                for q in range(odd, 8, 2):
                    eng.wait_ge(turned, q + 1)
                    u = 4 * (q // 2)
                    copy(dst[:, u:u + 4, :], ps[:, q, :].rearrange("p (u k) -> p u k", u=4))

            @block.vector
            def _(dve):
                gather(dve, nc.vector.tensor_copy, 0, be_tm)

            @block.scalar
            def _(act):
                gather(act, nc.scalar.copy, 1, ka_tm)

        ms = sb(st, "ms", [P, 2, PAIRS, NR])
        ss = sb(st, "ss", [P, HG, DG])
        rr = sb(st, "rr", [P, PAIRS, NR])
        un = sb(st, "un", [P, PAIRS, NR])
        r0 = sb(st, "r0", [P, HG, DG])
        ug = sb(st, "ug", [P, HG, DG])
        qs = sb(st, "qs", [P, HG, DG])
        r_done, u_done, y_done, m_done = (sem(n) for n in ("r_done", "u_done", "y_done", "m_done"))
        r_ok, u_ok, y_ok, m_ok = (sem(n) for n in ("r_ok", "u_ok", "y_ok", "m_ok"))
        ks_done, w_done, o_done, s_done = (sem(n) for n in ("ks_done", "w_done", "o_done", "s_done"))
        r0_ok, qs_ok, ug_ok, o_ok, s_ok = (sem(n) for n in ("r0_ok", "qs_ok", "ug_ok", "o_ok", "s_ok"))
        mch = Count(sem("mch"))

        with nc.Block() as block:
            @block.tensor
            def _(pe):
                def each(w, sem_):
                    for j in range(HG):
                        prods = w(j)
                        for k, (dst, lhs, rhs) in enumerate(prods):
                            ins = nc.tensor.matmul(dst, lhs, rhs, start=(k == 0), stop=(k == len(prods) - 1))
                    ins.then_inc(sem_, 1)

                for c in range(NCR):
                    i, u0 = c // 2, PAIRS * c
                    cols = [slice(NR * p, NR * p + NR) for p in range(PAIRS)]
                    if c:
                        pe.wait_ge(m_ok, c)
                    each(lambda p: ([(ps[:, 0, cols[p]], m.ar_e[:, u0 + p, 0, :], ms[:, c % 2, p, :])] if c else []) + [
                        (ps[:, 0, cols[p]], mk[:, u0 + p, 0, :], m.v_c[:, u0 + p, :])], r_done)
                    if c == 2:
                        pe.wait_ge(s_ok, 1)
                        for j, b in ((0, 4), (1, 5)):
                            for h in range(HG):
                                ins = nc.tensor.matmul(ps[:, b, P * h:P * h + P], m.qk[:, j, h, P:2 * P], ss[:, h, :],
                                                       start=True, stop=True)
                            ins.then_inc(ks_done, 1)
                    if c % 2:
                        pe.wait_ge(ug_ok, i + 1)
                        if i:
                            pe.wait_ge(o_ok, 1)
                        each(lambda h: [(ps[:, 7, P * h:P * h + P], gmx[:, 4 * i + h, 1, :], ug[:, h, :])], o_done)
                    pe.wait_ge(r_ok, c + 1)
                    each(lambda p: [(ps[:, 1, cols[p]], tinv[:, u0 + p, :], rr[:, p, :])], u_done)
                    if c % 2 == 0:
                        if i:
                            pe.wait_ge(r0_ok, 1)
                        src = r0 if i else vt
                        each(lambda h: [(ps[:, 6, P * h:P * h + P], tinv[:, NU + 4 * i + h, :], src[:, h, :])],
                             w_done)
                    else:
                        if i:
                            pe.wait_ge(r0_ok, 1)
                        each(lambda h: [(ps[:, 4, P * h:P * h + P], kt[:, 4 * i + h, :], ug[:, h, :])], s_done)
                    pe.wait_ge(u_ok, c + 1)
                    if c:
                        pe.wait_ge(y_ok, c)
                    each(lambda p: [(ps[:, 3, cols[p]], ka_tm[:, u0 + p, :], m.v_c[:, u0 + p, :]),
                                       (ps[:, 3, cols[p]], be_tm[:, u0 + p, :], un[:, p, :])], m_done)
                    each(lambda p: ([(ps[:, 2, cols[p]], m.ar_e[:, u0 + p, 1, :], ms[:, c % 2, p, :])] if c else []) + [
                        (ps[:, 2, cols[p]], mk[:, u0 + p, 1, :], m.v_c[:, u0 + p, :]),
                        (ps[:, 2, cols[p]], mb[:, u0 + p, 1, :], un[:, p, :])], y_done)

            def flat(ap):
                return ap.rearrange("p q v -> p (q v)")

            @block.gpsimd
            def _(pool):
                zero_dead(nc, st)

            @block.scalar
            def _(act):
                for c in range(NCR):
                    i = c // 2
                    act.wait_ge(r_done, c + 1)
                    nc.scalar.copy(flat(rr[:, :, :]), ps[:, 0, 0:256]).then_inc(r_ok, 1)
                    if c == 2:
                        act.wait_ge(ks_done, 2)
                        for h in range(HG):
                            ins = nc.scalar.activation(qs[:, h, :], ps[:, 5, P * h:P * h + P], ACT.Copy,
                                                       scale=m.sc[:, S_EG, 4 + h:5 + h])
                        ins.then_inc(qs_ok, 1)
                    if c == 1:
                        act.wait_ge(o_done, 1)
                        nc.scalar.copy(flat(m.y_g[:, 0:4, :]), ps[:, 7, :]).then_inc(o_ok, 1)
                    act.wait_ge(y_done, c + 1)
                    nc.scalar.copy(flat(m.y_r[:, PAIRS * c:PAIRS * c + PAIRS, :]), ps[:, 2, 0:256]).then_inc(y_ok, 1)

            @block.vector
            def _(dve):
                for c in range(NCR):
                    i = c // 2
                    if c == 2:
                        dve.wait_ge(ks_done, 1)
                        for h in range(HG):
                            ins = nc.vector.scalar_tensor_tensor(r0[:, h, :], ps[:, 4, P * h:P * h + P],
                                                                 m.sc[:, S_NEG, 4 + h:5 + h], vt[:, 4 + h, :], ALU.mult,
                                                                 ALU.add)
                        ins.then_inc(r0_ok, 1)
                    dve.wait_ge(u_done, c + 1)
                    nc.vector.tensor_scalar(flat(un[:, :, :]), ps[:, 1, 0:256], -1.0, None, ALU.mult).then_inc(u_ok, 1)
                    if c % 2 == 0:
                        dve.wait_ge(w_done, i + 1)
                        for h in range(HG):
                            ins = nc.vector.tensor_scalar(ug[:, h, :], ps[:, 6, P * h:P * h + P],
                                                          m.sc[:, S_BE, 4 * i + h:4 * i + h + 1], None, ALU.mult)
                        ins.then_inc(ug_ok, 1)
                    dve.wait_ge(m_done, c + 1)
                    new = ms[:, (c + 1) % 2]
                    if c == 0:
                        mch.step(dve, nc.vector.tensor_copy(flat(new), ps[:, 3, 0:256]))
                    else:
                        mch.step(dve, nc.vector.tensor_tensor(flat(new), ps[:, 3, 0:256], flat(ms[:, c % 2]), ALU.add))
                    nc.vector.tensor_tensor(new, new, over(m.plast[:, :, c], NR, 2),
                                            ALU.mult).then_inc(m_ok, 1)
                    if c % 2:
                        dve.wait_ge(s_done, i + 1)
                        if i == 0:
                            nc.vector.tensor_copy(flat(ss[:, :, :]), ps[:, 4, :]).then_inc(s_ok, 1)
                        else:
                            for h in range(HG):
                                nc.vector.scalar_tensor_tensor(ss[:, h, :], ss[:, h, :], m.sc[:, S_GL, 4 + h:5 + h],
                                                               ps[:, 4, P * h:P * h + P], ALU.mult, ALU.add)
                            dve.wait_ge(o_done, 2)
                            dve.wait_ge(qs_ok, 1)
                            nc.vector.tensor_tensor(flat(m.y_g[:, 4:8, :]), ps[:, 7, :], flat(qs[:, :, :]), ALU.add)

        spread, turned, kept, stored, zeroed = (sem(n) for n in ("spread", "turned2", "kept", "stored", "zeroed"))
        with nc.Block() as block:
            @block.vector
            def _(dve):
                dve.wait_ge(zeroed, 1)
                for h in range(2):
                    r = slice(64 * h, 64 * h + 64)
                    ins = nc.vector.tensor_copy(r0[r, :, r], ms[r, NCR % 2, :, :])
                ins.then_inc(spread, 1)
                dve.wait_ge(turned, 1)
                for h in range(2):
                    r = slice(64 * h, 64 * h + 64)
                    ins = nc.vector.tensor_copy(rr[r, :, :], ps[r, 0, :].rearrange("p (q k) -> p q k", q=4)[:, :, r])
                ins.then_inc(kept, 1)

            @block.gpsimd
            def _(pool):
                nc.gpsimd.memset(r0[:, :, :], 0.0).then_inc(zeroed, 1)

            @block.tensor
            def _(pe):
                pe.wait_ge(spread, 1)
                for p in range(PAIRS):
                    ins = nc.tensor.transpose(ps[:, 0, P * p:P * p + P], r0[:, p, :], ident[:])
                ins.then_inc(turned, 1)

            @block.sync
            def _(sp):
                sp.dma_start(out[4][0, 0].rearrange("h k v -> k h v"), ss[:, :, :]).then_inc(stored, 16)
                sp.wait_ge(kept, 1)
                sp.dma_start(out[2][0, 0].rearrange("(q h) v k -> (h v) q k", h=2), rr[:, :, :]).then_inc(stored, 16)
                sp.wait_ge(stored, 32)


def read_out(nc, sb, ps, ident, eps, m, ahead):
    with ExitStack() as st:
        sem = semaphores(nc, st, "ro")
        y, g = m.y_r, m.y_g
        ye = sb(st, "ye", [P, 18, P])
        sq = sb(st, "sq", [P, 18 * NR])
        mom = sb(st, "mom", [P, 4, 18])
        zeroed, v_ok, root, spread, turned, kept = (sem(n) for n in ("zeroed", "var", "root", "spread", "turned", "kept"))
        d = Count(sem("dve"))
        gok = sem("g_ready")
        sqr = sq[:, :].rearrange("p (u v) -> p u v", v=NR)
        sqg = sq[:, :].rearrange("p (u v) -> p u v", v=DG)
        with nc.Block() as block:
            @block.sync
            def _(sp):
                ahead.halves(sp, ahead.wa, "w_out", ahead.out_in)

            @block.gpsimd
            def _(pool):
                nc.gpsimd.memset(ye[:, :, :], 0.0).then_inc(zeroed, 1)

            @block.scalar
            def _(act):
                act.wait_ge(v_ok, 1)
                nc.scalar.activation(mom[:, 2, :], mom[:, 1, :], ACT.Sqrt, bias=eps[:, 1:2], scale=1.0 / NR).then_inc(
                    root, 1)
                act.wait_ge(v_ok, 2)
                nc.scalar.activation(mom[:, 3, 0:9], mom[:, 3, 0:9], ACT.Sqrt, bias=eps[:, 0:1],
                                     scale=1.0 / DG).then_inc(root, 1)

            @block.vector
            def _(dve):
                d.step(dve, nc.vector.tensor_reduce(mom[:, 0, :], y[:, :, :], AXX, ALU.add))
                d.step(dve, nc.vector.tensor_scalar(mom[:, 0, :], mom[:, 0, :], 1.0 / NR, None, ALU.mult))
                d.step(dve, nc.vector.tensor_tensor(y[:, :, :], y[:, :, :], over(mom[:, 0, :], NR, 2), ALU.subtract))
                d.step(dve, nc.vector.tensor_tensor(sqr, y[:, :, :], y[:, :, :], ALU.mult))
                nc.vector.tensor_reduce(mom[:, 1, :], sqr, AXX, ALU.add).then_inc(v_ok, 1)
                dve.wait_ge(v_ok, 1)
                d.step(dve, nc.vector.tensor_tensor(sqg, g[:, :, :], g[:, :, :], ALU.mult))
                nc.vector.tensor_reduce(mom[:, 3, 0:9], sqg, AXX, ALU.add).then_inc(v_ok, 1)
                dve.wait_ge(root, 1)
                d.step(dve, nc.vector.reciprocal(mom[:, 2, :], mom[:, 2, :]))
                dve.wait_ge(zeroed, 1)
                for h in range(2):
                    r = slice(64 * h, 64 * h + 64)
                    nc.vector.tensor_tensor(ye[r, 0:16, r], y[r, 0:16, :], over(mom[r, 2, 0:16], NR, 2), ALU.mult)
                for q in range(4):
                    r, h = slice(NS * q, NS * q + NS), q % 2
                    ins = nc.vector.tensor_tensor(ye[r, 16:18, 64 * h:64 * h + 64], y[r, 16:18, :],
                                                  over(mom[r, 2, 16:18], NR, 2), ALU.mult)
                ins.then_inc(spread, 1)
                dve.wait_ge(root, 2)
                d.step(dve, nc.vector.reciprocal(mom[:, 3, 0:9], mom[:, 3, 0:9]))
                nc.vector.tensor_tensor(g[:, :, :], g[:, :, :], over(mom[:, 3, 0:9], DG, 2), ALU.mult).then_inc(gok, 1)
                yT = m.yT
                for c in range(NCR):
                    dve.wait_ge(turned, c + 1)
                    for h in range(2):
                        r = slice(64 * h, 64 * h + 64)
                        nc.vector.tensor_copy(yT[r, 0:4, CR * c:CR * c + CR],
                                              ps[r, c, :].rearrange("p (q t) -> p q t", q=4)[:, :, r])
                dve.wait_ge(turned, 5)
                for h in range(2):
                    r = slice(64 * h, 64 * h + 64)
                    ins = nc.vector.tensor_copy(yT[r, 0:4, TP:],
                                                ps[r, 4, 0:256].rearrange("p (q t) -> p q t", q=4)[
                                                    :, :, NS * h:NS * h + NS])
                d.step(dve, ins)
                for p in range(PAIRS):
                    ins = nc.vector.tensor_scalar(yT[:, p, :], yT[:, p, :], m.vec[:, V_LW + p:V_LW + p + 1],
                                                  m.vec[:, V_LB + p:V_LB + p + 1], ALU.mult, ALU.add)
                d.step(dve, ins)
                d.step(dve, nc.vector.tensor_tensor(yT[:, 0:4, :], yT[:, 0:4, :], m.bv[:, :, :], ALU.add))
                nc.vector.tensor_tensor(yT[:, 0:4, :], yT[:, 0:4, :], m.gate[:, :, :], ALU.mult)
                gw = m.vec[:, V_GN:V_GN + 1]
                for i in range(2):
                    dve.wait_ge(turned, 6 + i)
                    nc.vector.tensor_scalar(yT[:, 4:8, P * i:P * i + P], ps[:, 5 + i, :].rearrange(
                        "p (h t) -> p h t", h=HG), gw, None, ALU.mult)
                dve.wait_ge(turned, 8)
                d.step(dve, nc.vector.tensor_scalar(yT[:, 4:8, TP:], ps[:, 7, 0:P].rearrange("p (h t) -> p h t", h=HG),
                                                    gw, None, ALU.mult))
                nc.vector.tensor_tensor(yT[:, 4:8, :], yT[:, 4:8, :], m.zt[:, :, :], ALU.mult)

            @block.tensor
            def _(pe):
                pe.wait_ge(spread, 1)
                for c in range(NCR):
                    for p in range(PAIRS):
                        ins = nc.tensor.transpose(ps[:, c, P * p:P * p + P], ye[:, PAIRS * c + p, :], ident[:])
                    ins.then_inc(turned, 1)
                for p2 in range(2):
                    ins = nc.tensor.transpose(ps[:, 4, P * p2:P * p2 + P], ye[:, 16 + p2, :], ident[:])
                ins.then_inc(turned, 1)
                pe.wait_ge(gok, 1)
                for i in range(2):
                    for h in range(HG):
                        ins = nc.tensor.transpose(ps[:, 5 + i, P * h:P * h + P], g[:, 4 * i + h, :], ident[:])
                    ins.then_inc(turned, 1)
                nc.tensor.transpose(ps[:, 7, 0:P], g[:, 8, :], ident[:]).then_inc(turned, 1)


def project_add(nc, sb, ps, ident, x, yT, wt, w_in, name, load):
    with ExitStack() as st:
        sem = semaphores(nc, st, name)
        summed, part_ok = sem("summed"), sem("part_ok")
        part = sb(st, f"{name}_p", [P, DX])
        tiles = [(i, half) for half in range(2) for i in range(2)]
        with nc.Block() as block:
            @block.sync
            def _(sp):
                load(sp)

            @block.tensor
            def _(pe):
                def prompt(k):
                    i, half = tiles[k]
                    pe.wait_ge(w_in[half], 16)
                    for c in range(KC):
                        ins = nc.tensor.matmul(ps[:, k, :], yT[:, c, P * i:P * i + P],
                                               wt[:, c, 512 * half:512 * half + 512], start=(c == 0),
                                               stop=(c == KC - 1))
                    ins.then_inc(summed, 1)

                for k in range(3):
                    prompt(k)
                for c in range(KC):
                    for j in range(4):
                        ins = nc.tensor.matmul(ps[NS * j:NS * j + NS, 4, 0:DX], yT[:, c, TP:T],
                                               wt[:, c, DX * j:DX * j + DX], start=(c == 0), stop=(c == KC - 1),
                                               tile_position=(0, NS * j))
                ins.then_inc(summed, 1)
                prompt(3)
                pe.wait_ge(part_ok, 1)
                for j in range(4):
                    ins = nc.tensor.matmul(ps[:NS, 5 + j // 2, DX * (j % 2):DX * (j % 2) + DX],
                                           ident[:, NS * j:NS * j + NS], part[:, :], start=True, stop=True)
                ins.then_inc(summed, 1)

            @block.scalar
            def _(act):
                act.wait_ge(summed, 4)
                nc.scalar.copy(part[:, :], ps[:, 4, 0:DX]).then_inc(part_ok, 1)

            @block.vector
            def _(dve):
                for k, (i, half) in enumerate(tiles):
                    dve.wait_ge(summed, k + 1 + (k == 3))
                    v = x[:, i, 512 * half:512 * half + 512]
                    nc.vector.tensor_tensor(v, v, ps[:, k, :], ALU.add)
                dve.wait_ge(summed, 6)
                v = x[:NS, 2, :].rearrange("p (h d) -> p h d", h=2)
                nc.vector.tensor_tensor(v, v, ps[:NS, 5:7, :], ALU.add)


def attention(nc, a, out, ahead, sb, ps, ident, ones, x, g8, stat, eps, norm_stage):
    with ExitStack() as st:
        sem = semaphores(nc, st, "at")
        h_tm = sb(st, "ah_tm", [P, 3, D])
        hT = sb(st, "ahT", [P, KC, T])
        memx, wk, wv, wq = ahead.memx, ahead.wb, ahead.wc, ahead.wa
        kT = sb(st, "kT", [P, KC, NM])
        qT = sb(st, "qT", [P, KC, T])
        oT = sb(st, "oT", [P, KC, T])
        k_tm = h_tm
        with nc.Block() as block:
            @block.sync
            def _(sp):
                ahead.whole(sp, wq, "wq_x", ahead.wq_in)
                sp.wait_ge(ahead.mem_in, 16)
        norm_stage("mem", memx, TILES[:2], 2, hT, h_tm)

        with ahead.wv:
            summed, v_ok, a_ok, turned, stored = (
                sem(n) for n in ("kv_sum", "v_ok", "a_ok", "k_turned", "kv_stored"))
            parts = [(w, i, half) for w in range(2) for i in range(2) for half in range(2)]
            with nc.Block() as block:
                @block.sync
                def _(sp):
                    sp.wait_ge(v_ok, 4)
                    ahead.halves(sp, ahead.wb, "wo_x", ahead.wo_in)
                    sp.dma_start(out[6][0, 0].rearrange("(i p) h d -> p i (h d)", p=P), k_tm[:, 0:2, :]).then_inc(
                        stored, 16)
                    sp.wait_ge(a_ok, 4)
                    sp.dma_start(out[7][0, 0].rearrange("(i p) h d -> p i (h d)", p=P), memx[:, :, :]).then_inc(
                        stored, 16)
                    sp.wait_ge(stored, 32)

                @block.tensor
                def _(pe):
                    for k, (w, i, half) in enumerate(parts):
                        pe.wait_ge((ahead.wk_in, ahead.wv_in)[w], 16)
                        for c in range(KC):
                            ins = nc.tensor.matmul(ps[:, k, :], hT[:, c, P * i:P * i + P],
                                                   (wk, wv)[w][:, c, 512 * half:512 * half + 512], start=(c == 0),
                                                   stop=(c == KC - 1))
                        ins.then_inc(summed, 1)
                    for q in range(4):
                        pe.wait_ge(v_ok, 4)
                        for j in range(2):
                            for i in range(2):
                                n = 2 * q + j
                                ins = nc.tensor.transpose(ps[:, q, 256 * j + P * i:256 * j + P * i + P],
                                                          k_tm[:, i, P * n:P * n + P], ident[:])
                        ins.then_inc(turned, 1)

                @block.vector
                def _(dve):
                    for k in range(4):
                        _, i, half = parts[k]
                        dve.wait_ge(summed, k + 1)
                        nc.vector.tensor_copy(k_tm[:, i, 512 * half:512 * half + 512], ps[:, k, :]).then_inc(v_ok, 1)
                    for q in range(4):
                        dve.wait_ge(turned, q + 1)
                        nc.vector.tensor_copy(kT[:, 2 * q:2 * q + 2, :].rearrange("p n m -> p (n m)"), ps[:, q, :])

                @block.scalar
                def _(act):
                    for k in range(4, 8):
                        _, i, half = parts[k]
                        act.wait_ge(summed, k + 1)
                        nc.scalar.copy(memx[:, i, 512 * half:512 * half + 512], ps[:, k, :]).then_inc(a_ok, 1)

        norm_stage("cross", x, TILES, 1, hT, h_tm)

        cache = Cache(nc, a, sb, st)
        with ExitStack() as s1:
            sem = semaphores(nc, s1, "q")
            summed = sem("q_sum")
            with nc.Block() as block:
                @block.gpsimd
                def _(pool):
                    zero_dead(nc, st)

                @block.sync
                def _(sp):
                    cache.first(sp)

                @block.tensor
                def _(pe):
                    pe.wait_ge(ahead.wq_in, 16)
                    for n in range(KC):
                        for c in range(KC):
                            ins = nc.tensor.matmul(ps[:, n, 0:T], wq[:, c, P * n:P * n + P], hT[:, c, :],
                                                   start=(c == 0), stop=(c == KC - 1))
                        ins.then_inc(summed, 1)

                @block.scalar
                def _(act):
                    for n in range(KC):
                        act.wait_ge(summed, n + 1)
                        nc.scalar.mul(qT[:, n, :], ps[:, n, 0:T], DX ** -0.5)
        prompt_attention(nc, sb, ps, ident, qT, kT, memx, oT)
        sample_attention(nc, sb, ps, ident, qT, oT, cache)
        project_add(nc, sb, ps, ident, x, oT, ahead.wb, ahead.wo_in, "wo", lambda sp: load_w1(sp, a, ahead, 0))
    ahead.temp.close()


def prompt_attention(nc, sb, ps, ident, qT, kT, v, oT):
    with ExitStack() as st:
        sem = semaphores(nc, st, "pa")
        pr = sb(st, "probs", [P, 8, NM])
        pT = sb(st, "probsT", [P, HX, 2, TP])
        mx = sb(st, "pa_mx", [P, 3, 8])
        s_done, mx_ok, e_ok, n_ok, turned, t_ok, o_done, d = (
            sem(n) for n in ("scores", "max", "exp", "norm", "turned", "t_ok", "o_done", "chain"))
        ch = Count(d)
        with nc.Block() as block:
            @block.tensor
            def _(pe):
                for u in range(8):
                    h, i = u // 2, u % 2
                    for dc in range(2):
                        ins = nc.tensor.matmul(ps[:, h, NM * i:NM * i + NM], qT[:, 2 * h + dc, P * i:P * i + P],
                                               kT[:, 2 * h + dc, :], start=(dc == 0), stop=(dc == 1))
                    if i:
                        ins.then_inc(s_done, 1)
                for h in range(HX):
                    pe.wait_ge(n_ok, h + 1)
                    for mt in range(2):
                        for i in range(2):
                            ins = nc.tensor.transpose(ps[:, 4 + h, NM * mt + P * i:NM * mt + P * i + P],
                                                      pr[:, 2 * h + i, P * mt:P * mt + P], ident[:])
                    ins.then_inc(turned, 1)
                for h in range(HX):
                    pe.wait_ge(t_ok, h + 1)
                    for dc in range(2):
                        for mt in range(2):
                            c0 = DX * h + P * dc
                            ins = nc.tensor.matmul(ps[:, h, TP * dc:TP * dc + TP], v[:, mt, c0:c0 + P], pT[:, h, mt, :],
                                                   start=(mt == 0), stop=(mt == 1))
                    ins.then_inc(o_done, 1)

            @block.vector
            def _(dve):
                for h in range(HX):
                    dve.wait_ge(s_done, h + 1)
                    nc.vector.tensor_reduce(mx[:, 0, 2 * h:2 * h + 2], ps[:, h, :].rearrange("p (i m) -> p i m", i=2),
                                            AXX, ALU.max, negate=True).then_inc(mx_ok, 1)
                for h in range(HX):
                    dve.wait_ge(e_ok, 2 * h + 2)
                    ch.step(dve, nc.vector.reciprocal(mx[:, 2, 2 * h:2 * h + 2], mx[:, 1, 2 * h:2 * h + 2]))
                    nc.vector.tensor_tensor(pr[:, 2 * h:2 * h + 2, :], pr[:, 2 * h:2 * h + 2, :],
                                            over(mx[:, 2, 2 * h:2 * h + 2], NM, 2), ALU.mult).then_inc(n_ok, 1)
                for h in range(HX):
                    dve.wait_ge(turned, h + 1)
                    nc.vector.tensor_copy(pT[:, h].rearrange("p m t -> p (m t)"), ps[:, 4 + h, :]).then_inc(t_ok, 1)

            @block.scalar
            def _(act):
                for u in range(8):
                    act.wait_ge(mx_ok, u // 2 + 1)
                    nc.scalar.activation(pr[:, u, :], ps[:, u // 2, NM * (u % 2):NM * (u % 2) + NM], ACT.Exp,
                                         bias=mx[:, 0, u:u + 1], accum_out=mx[:, 1, u:u + 1]).then_inc(e_ok, 1)
                for h in range(HX):
                    act.wait_ge(o_done, h + 1)
                    nc.scalar.copy(oT[:, 2 * h:2 * h + 2, 0:TP], ps[:, h, :].rearrange("p (c t) -> p c t", c=2))


class Cache:
    NK, NV = 2, 5

    def __init__(self, nc, a, sb, st):
        sem = semaphores(nc, st, "ca")
        self.kb = sb(st, "kb", [P, self.NK, 2, D])
        vb = sb(st, "vb", [P, self.NV - self.NK, 2, D])
        self.v = [vb[:, j] for j in range(self.NV - self.NK)] + [self.kb[:, j] for j in range(self.NK)]
        self.k_in = [sem(f"k_in{j}") for j in range(self.NK)]
        self.v_in = [sem(f"v_in{j}") for j in range(self.NV)]
        self.kd = a["cache_mem_k"][0].rearrange("b (i p) h d -> b p i (h d)", p=P)
        self.vd = a["cache_mem_v"][0].rearrange("b (i p) h d -> b p i (h d)", p=P)

    def load_k(self, sp, b):
        sp.dma_start(self.kb[:, b % self.NK], self.kd[b]).then_inc(self.k_in[b % self.NK], 16)

    def load_v(self, sp, b):
        sp.dma_start(self.v[b % self.NV], self.vd[b]).then_inc(self.v_in[b % self.NV], 16)

    def first(self, sp):
        for b in range(self.NK):
            self.load_k(sp, b)
        for b in range(self.NV - self.NK):
            self.load_v(sp, b)


def sample_attention(nc, sb, ps, ident, qT, oT, cache):
    with ExitStack() as st:
        sem = semaphores(nc, st, "sx")
        NK, NV, kb, k_in, v_in = cache.NK, cache.NV, cache.kb, cache.k_in, cache.v_in
        kbT = sb(st, "kbT", [P, 2, KC, NM])
        qm = sb(st, "qm", [P, KC, NB, NS])
        pm = sb(st, "pm", [P, 2, NB, P])
        pr = sb(st, "s_probs", [P, NM])
        os_ = sb(st, "s_o", [P, NM])
        mx = sb(st, "sx_mx", [P, 3])
        zeroed, q_ok, turned, kt_v, kt_a, s_done, mx_ok, e_ok, p_ok, pt_done, pm_ok, o_done, o_ok, ot_done = (
            sem(n) for n in ("zeroed", "q_ok", "turned", "kt_v", "kt_a", "s_done", "mx_ok", "e_ok", "p_ok", "pt_done",
                             "pm_ok", "o_done", "o_ok", "ot_done"))
        ch = Count(sem("chain"))
        with nc.Block() as block:
            @block.gpsimd
            def _(pool):
                nc.gpsimd.memset(qm[:, :, :, :], 0.0).then_inc(zeroed, 1)
                pool.wait_ge(zeroed, 1)
                nc.gpsimd.memset(pm[:, :, :, :], 0.0).then_inc(zeroed, 1)

            @block.sync
            def _(sp):
                for b in range(NK, NB):
                    sp.wait_ge(turned, 4 * (b - NK + 1))
                    cache.load_k(sp, b)
                for b in range(NV - NK, NV):
                    sp.wait_ge(turned, 4 * (NB - NV + b + 1))
                    cache.load_v(sp, b)
                for b in range(NV, NB):
                    sp.wait_ge(o_done, b - NV + 1)
                    cache.load_v(sp, b)

            @block.tensor
            def _(pe):
                def scores(b):
                    pe.wait_ge(kt_v, 2 * b + 2)
                    pe.wait_ge(kt_a, 2 * b + 2)
                    for dc in range(2):
                        for h in range(HX):
                            n, r = 2 * h + dc, slice(NS * h, NS * h + NS)
                            ins = nc.tensor.matmul(ps[r, 0, 0:NM], qm[:, n, b, :], kbT[:, b % 2, n, :],
                                                   start=(b == 0 and dc == 0), stop=(b == NB - 1 and dc == 1),
                                                   tile_position=(0, NS * h))
                    ins.then_inc(s_done, 1)

                for b in range(NB):
                    pe.wait_ge(k_in[b % NK], 16 * (b // NK + 1))
                    for q in range(4):
                        if b:
                            pe.wait_ge((kt_v, kt_a)[q % 2], 2 * (b - 1) + q // 2 + 1)
                        for j in range(2):
                            for i in range(2):
                                n = 2 * q + j
                                ins = nc.tensor.transpose(ps[:, 4 + q, NM * j + P * i:NM * j + P * i + P],
                                                          kb[:, b % NK, i, P * n:P * n + P], ident[:])
                        ins.then_inc(turned, 1)
                    if b:
                        if b == 1:
                            pe.wait_ge(q_ok, 1)
                        scores(b - 1)
                scores(NB - 1)
                pe.wait_ge(p_ok, 1)
                for mt in range(2):
                    ins = nc.tensor.transpose(ps[:, 1, P * mt:P * mt + P], pr[:, P * mt:P * mt + P], ident[:])
                ins.then_inc(pt_done, 1)
                pe.wait_ge(pm_ok, 1)
                for b in range(NB):
                    pe.wait_ge(v_in[b % NV], 16 * (b // NV + 1))
                    for mt in range(2):
                        for h in range(HX):
                            r = slice(NS * h, NS * h + NS)
                            ins = nc.tensor.matmul(ps[r, 2, 0:DX], pm[:, mt, b, r], cache.v[b % NV][:, mt, DX * h:DX * h + DX],
                                                   start=(b == 0 and mt == 0), stop=(b == NB - 1 and mt == 1),
                                                   tile_position=(0, NS * h))
                    ins.then_inc(o_done, 1)
                pe.wait_ge(o_ok, 1)
                for dc in range(2):
                    ins = nc.tensor.transpose(ps[:, 3, P * dc:P * dc + P], os_[:, P * dc:P * dc + P], ident[:])
                ins.then_inc(ot_done, 1)

            def take(eng, copy, b, odd, done):
                for q in range(odd, 4, 2):
                    eng.wait_ge(turned, 4 * b + q + 1)
                    if b >= 2:
                        eng.wait_ge(s_done, b - 1)
                    copy(kbT[:, b % 2, 2 * q:2 * q + 2, :].rearrange("p n m -> p (n m)"), ps[:, 4 + q, :]).then_inc(
                        done, 1)

            @block.vector
            def _(dve):
                dve.wait_ge(zeroed, 2)
                for b in range(NB):
                    ins = nc.vector.tensor_copy(qm[:, :, b, TS * b:TS * b + TS], qT[:, :, TP + TS * b:TP + TS * b + TS])
                ins.then_inc(q_ok, 1)
                for b in range(NB):
                    take(dve, nc.vector.tensor_copy, b, 0, kt_v)
                dve.wait_ge(s_done, NB)
                nc.vector.tensor_reduce(mx[:, 0:1], ps[:, 0, 0:NM], AXX, ALU.max, negate=True).then_inc(mx_ok, 1)
                dve.wait_ge(e_ok, 1)
                ch.step(dve, nc.vector.reciprocal(mx[:, 2:3], mx[:, 1:2]))
                nc.vector.tensor_scalar(pr[:, :], pr[:, :], mx[:, 2:3], None, ALU.mult).then_inc(p_ok, 1)
                dve.wait_ge(pt_done, 1)
                for b in range(NB):
                    ins = nc.vector.tensor_copy(
                        pm[:, :, b, :].rearrange("p m (h t) -> p m h t", h=HX)[:, :, :, TS * b:TS * b + TS],
                        ps[:, 1, 0:256].rearrange("p (m h t) -> p m h t", m=2, h=HX)[:, :, :, TS * b:TS * b + TS])
                ins.then_inc(pm_ok, 1)
                dve.wait_ge(ot_done, 1)
                for dc in range(2):
                    nc.vector.tensor_copy(oT[:, dc::2, TP:], ps[:, 3, P * dc:P * dc + P].rearrange(
                        "p (h t) -> p h t", h=HX))

            @block.scalar
            def _(act):
                for b in range(NB):
                    take(act, nc.scalar.copy, b, 1, kt_a)
                act.wait_ge(mx_ok, 1)
                nc.scalar.activation(pr[:, :], ps[:, 0, 0:NM], ACT.Exp, bias=mx[:, 0:1], accum_out=mx[:, 1:2]).then_inc(
                    e_ok, 1)
                act.wait_ge(o_done, NB)
                nc.scalar.copy(os_[:, :], ps[:, 2, 0:DX]).then_inc(o_ok, 1)


CAP = 64
HK = 4
NQ = P
LIST = 2 * NE


def w1_view(a):
    return a["w1_e"][0].rearrange("e (h p c) n -> h p e c n", h=2, c=HK)


def load_w1(sp, a, ahead, h):
    w = (ahead.wa, ahead.wb)[h]
    sp.dma_start(w[:, :, :].rearrange("p (c g) n -> p c (g n)", g=2).unsqueeze(1),
                 w1_view(a)[h][:, 0:1]).then_inc(ahead.w1_in[h], 16)


def experts(nc, a, out, ahead, sb, ps, ident, ones, x, g8, stat, eps, norm_stage):
    with ExitStack() as st:
        sem = semaphores(nc, st, "mo")
        wc, wd = (sb(st, n, [P, HK, 2 * D], side="right") for n in ("wc1", "wd1"))
        w2 = sb(st, "w2", [P, 2, HK, D], side="right")
        w1 = [[w[:, :, :].rearrange("p (c g) n -> p c (g n)", g=2) for w in (ahead.wa, ahead.wb)],
              [w[:, :, :] for w in (wc, wd)]]
        w1_in = [ahead.w1_in, [sem(f"w1_in1{h}") for h in range(2)]]
        w2_in = [sem(f"w2_in{h}") for h in range(2)]
        h_tm = sb(st, "eh_tm", [P, 3, D])
        code = sb(st, "code", [P, 3, NE])
        gate = sb(st, "gate_e", [P, 3, NE])
        tab = sb(st, "tab", [1, LIST + 2], I32)
        base = sb(st, "base", [P, LIST])
        iota = sb(st, "iota", [P, CAP])
        gfx = sb(st, "gfx", [P, 2, HK])
        pick = sb(st, "pick", [4, 4, CAP])
        w1_d, w2_d = w1_view(a), a["w2_e"][0].rearrange("e (h p c) n -> h p e c n", h=2, c=HK)

        def load_first(sp):
            load_w1(sp, a, ahead, 1)
            for h in range(2):
                sp.dma_start(w2[:, h].unsqueeze(1), w2_d[h][:, 0:1]).then_inc(w2_in[h], 16)
            for h in range(2):
                sp.dma_start(w1[1][h].unsqueeze(1), w1_d[h][:, 1:2]).then_inc(w1_in[1][h], 16)

        route(nc, a, st, sb, ps, ident, ones, x, g8, stat, eps, norm_stage, h_tm, code, gate, tab, base, iota, gfx,
              pick, load_first)

        b1 = sb(st, "b1", [4, 2, 512])
        sel = sb(st, "sel", [P, 3, CAP])
        gsel = sb(st, "gsel", [P, 3, 2, CAP])
        gT = sb(st, "gT", [P, 3, P])
        off = sb(st, "off", [P, 2, 3])
        xe = sb(st, "xe", [P, 512])
        xeT = sb(st, "xeT", [P, 2, HK, CAP])
        hg = sb(st, "hg", [P, 512])
        hl = sb(st, "hl", [P, 512])
        th = sb(st, "e_th", [P, 512])
        y = sb(st, "y", [P, 512])
        b1_in = [sem(f"b1_in{s}") for s in range(2)]
        w1_half, w2_half = sem("w1_half"), sem("w2_half")
        w1_done, cmb_done, gath_done, xt_done, gt_done, at_done, w2_done = (
            sem(n) for n in ("w1_done", "cmb_done", "gath_done", "xt_done", "gt_done", "at_done", "w2_done"))
        th_ok, xe_ok, at_ok, y_ok = (sem(n) for n in ("th_ok", "xe_ok", "at_ok", "y_ok"))
        hg_ok, act_ok, add_ok, sel_ok, xT_ok, g_ok, gt_ok, chain = (
            sem(n) for n in ("hg_ok", "act_ok", "add_ok", "sel_ok", "xT_ok", "g_ok", "gt_ok", "chain"))
        b1_d = a["b1_e"][0].rearrange("e (r n) -> r e n", n=512)
    
        def count_of(eng):
            return eng.value_load(tab[0:1, LIST + 1:LIST + 2], min_val=NE // 2, max_val=LIST // 2 - 1)

        with nc.Block() as block:
            @block.sync
            def _(sp):
                def load_b1(e, s):
                    sp.dma_start(b1[:, s].unsqueeze(1), b1_d[:, e]).then_inc(b1_in[s], 16)

                def expert(k):
                    return bass.ds(sp.value_load(tab[0:1, bass.ds(k, 1)], min_val=0, max_val=NE - 1), 1)

                def load_w2(k):
                    e = expert(k)
                    for h in range(2):
                        sp.wait_ge((w2_half, w2_done)[h], k)
                        sp.dma_start(w2[:, h].unsqueeze(1), w2_d[h][:, e]).then_inc(w2_in[h], 16)

                more = sp.value_load(tab[0:1, LIST:LIST + 1], min_val=NE // 2 - 1, max_val=LIST // 2 - 2)
                for s in range(2):
                    load_b1(slice(s, s + 1), s)
                with sp.Fori(0, more) as i:
                    for s in range(2):
                        k = 2 * i + s
                        e = expert(k + 2)
                        for h in range(2):
                            sp.wait_ge((w1_half, w1_done)[h], k + 1)
                            sp.dma_start(w1[s][h].unsqueeze(1), w1_d[h][:, e]).then_inc(w1_in[s][h], 16)
                            if h == 0:
                                load_b1(e, s)
                        load_w2(k + 1)
                load_w2(2 * more + 1)

            @block.gpsimd
            def _(pool):
                nc.gpsimd.memset(y[:, :], 0.0).then_inc(y_ok, 1)
                nc.gpsimd.memset(gT[:, 0:2, :], 0.0).then_inc(gt_ok, 1)
                zero_dead(nc, st)

            @block.tensor
            def _(pe):
                def gather():
                    for half in range(2):
                        for i, (t0, n) in enumerate(TILES):
                            ins = nc.tensor.matmul(ps[CAP * half:CAP * half + CAP, 3, :], sel[:n, i, :],
                                                   h_tm[:n, i, 512 * half:512 * half + 512], start=(i == 0),
                                                   stop=(i == 2))
                    ins.then_inc(gath_done, 1)

                def turn_x():
                    for c in range(HK):
                        ins = nc.tensor.transpose(ps[:, 4, P * c:P * c + P], xe[:, c::HK], ident[:])
                    ins.then_inc(xt_done, 1)

                def combine(i):
                    b = 0 if i == 2 else 6
                    for half in range(2):
                        r = slice(CAP * half, CAP * half + CAP)
                        ins = nc.tensor.matmul(ps[:, b + half, :], gT[r, i, :], y[r, :], start=True, stop=True)
                    ins.then_inc(cmb_done, 1)

                pairs = count_of(pe)
                pe.wait_ge(sel_ok, 1)
                gather()
                pe.wait_ge(xe_ok, 1)
                turn_x()
                with pe.Fori(0, pairs) as j:
                    for s in range(2):
                        k = 2 * j + s
                        pe.wait_ge(xT_ok, k + 1)
                        pe.wait_ge(add_ok, 3 * k + 1)
                        pe.wait_ge(b1_in[s], 16 * j + 16)
                        for half in range(2):
                            for g in range(2):
                                ins = nc.tensor.matmul(ps[CAP * half:CAP * half + CAP, g, :], pick[:, 2 * g + half, :],
                                                       b1[:, s, :], start=True, stop=False)
                        for h in range(2):
                            pe.wait_ge(w1_in[s][h], 16 * j + 16)
                            for c in range(HK):
                                for g in range(2):
                                    for half in range(2):
                                        c0 = D * g + 512 * half
                                        ins = nc.tensor.matmul(ps[CAP * half:CAP * half + CAP, g, :], xeT[:, h, c, :],
                                                               w1[s][h][:, c, c0:c0 + 512], start=False,
                                                               stop=(h == 1 and c == HK - 1))
                            if h == 0:
                                ins.then_inc(w1_half, 1)
                        ins.then_inc(w1_done, 1)
                        pe.wait_ge(y_ok, k + 1)
                        pe.wait_ge(gt_ok, k + 1)
                        combine(0)
                        pe.wait_ge(sel_ok, k + 2)
                        gather()
                        pe.wait_ge(add_ok, 3 * k + 2)
                        combine(1)
                        pe.wait_ge(xe_ok, k + 2)
                        turn_x()
                        pe.wait_ge(act_ok, k + 1)
                        for c in range(HK):
                            ins = nc.tensor.transpose(ps[:, 5, P * c:P * c + P], hl[:, c::HK], ident[:])
                        ins.then_inc(at_done, 1)
                        combine(2)
                        pe.wait_ge(g_ok, k + 1)
                        for i, (t0, n) in enumerate(TILES):
                            ins = nc.tensor.transpose(ps[:, 3, t0:t0 + n], gsel[:n, i].rearrange("p r t -> p (r t)"),
                                                      ident[:n, :n])
                        ins.then_inc(gt_done, 1)
                        pe.wait_ge(at_ok, k + 1)
                        actT = th[:, :].rearrange("p (c h t) -> p c h t", c=HK, h=2)
                        for h in range(2):
                            pe.wait_ge(w2_in[h], 16 * k + 16)
                            for c in range(HK):
                                for half in range(2):
                                    ins = nc.tensor.matmul(ps[CAP * half:CAP * half + CAP, 2, :], actT[:, c, h, :],
                                                           w2[:, h, c, 512 * half:512 * half + 512],
                                                           start=(h == 0 and c == 0), stop=(h == 1 and c == HK - 1))
                            if h == 0:
                                ins.then_inc(w2_half, 1)
                        ins.then_inc(w2_done, 1)
                pe.wait_ge(y_ok, 2 * pairs + 1)
                pe.wait_ge(gt_ok, 2 * pairs + 1)
                for i in range(3):
                    pe.wait_ge(add_ok, 6 * pairs + i + 1)
                    combine(i)

            @block.scalar
            def _(act):
                def take_x():
                    nc.scalar.copy(xe[:, :], ps[:, 3, :]).then_inc(xe_ok, 1)

                pairs = count_of(act)
                act.wait_ge(gath_done, 1)
                take_x()
                with act.Fori(0, pairs) as j:
                    for s in range(2):
                        k = 2 * j + s
                        act.wait_ge(hg_ok, k + 1)
                        nc.scalar.activation(th[:, :], hg[:, :], ACT.Tanh, scale=ALPHA / 2).then_inc(th_ok, 1)
                        act.wait_ge(gath_done, k + 2)
                        take_x()
                        act.wait_ge(at_done, k + 1)
                        nc.scalar.copy(th[:, :], ps[:, 5, :]).then_inc(at_ok, 1)
                        act.wait_ge(w2_done, k + 1)
                        nc.scalar.activation(y[:, :], ps[:, 2, :], ACT.Copy, scale=0.5).then_inc(y_ok, 1)

            @block.vector
            def _(dve):
                ch = Count(chain)

                def add(i):
                    n = TILES[i][1]
                    v = x[:n, i, :].rearrange("p (h d) -> p h d", h=2)
                    b = 0 if i == 2 else 6
                    nc.vector.tensor_tensor(v, v, ps[:n, b:b + 2, :], ALU.add).then_inc(add_ok, 1)

                def turned_x():
                    nc.vector.tensor_tensor(xeT[:, :, :, :].rearrange("p h c t -> p c h t"),
                                            ps[:, 4, :].rearrange("p (c h t) -> p c h t", c=HK, h=2),
                                            over(gfx[:, :, :].rearrange("p h c -> p c h"), CAP, 3),
                                            ALU.mult).then_inc(xT_ok, 1)

                def offset(w, e, k, steps):
                    nc.vector.tensor_scalar(off[:, w, :], code[:, :, e].rearrange("p i o -> p (i o)"), base[:, k], None,
                                            ALU.subtract).then_inc(chain, 1)
                    dve.wait_ge(chain, steps)

                def select(w=1):
                    for i, (_, n) in enumerate(TILES):
                        ins = nc.vector.tensor_scalar(sel[:n, i, :], iota[:n, :], off[:n, w, i:i + 1], None, ALU.is_equal)
                    ins.then_inc(sel_ok, 1)

                def weigh(e):
                    for i, (_, n) in enumerate(TILES):
                        ins = nc.vector.tensor_scalar(gsel[:n, i], over(iota[:n, :], 2), off[:n, 0, i:i + 1],
                                                      gate[:n, i, e], ALU.is_equal, ALU.mult)
                    ins.then_inc(g_ok, 1)

                pairs = count_of(dve)
                nc.vector.memset(gT[:, 2, :], 0.0).then_inc(add_ok, 1)
                offset(0, slice(0, 1), slice(0, 1), 1)
                select(0)
                weigh(slice(0, 1))
                dve.wait_ge(gath_done, 1)
                offset(1, slice(1, 2), slice(1, 2), 2)
                select()
                dve.wait_ge(xt_done, 1)
                turned_x()
                with dve.Fori(0, pairs) as j:
                    for s in range(2):
                        k = 2 * j + s
                        dve.wait_ge(w1_done, k + 1)
                        nc.vector.tensor_scalar(hg[:, :], ps[:, 0, :], LIMIT, None, ALU.min).then_inc(hg_ok, 1)
                        nc.vector.tensor_scalar(hl[:, :], ps[:, 1, :], LIMIT, -LIMIT, ALU.min, ALU.max)
                        dve.wait_ge(cmb_done, 3 * k + 1)
                        add(0)
                        dve.wait_ge(th_ok, k + 1)
                        nc.vector.scalar_tensor_tensor(hg[:, :], th[:, :], 1.0, hg[:, :], ALU.add, ALU.mult).then_inc(
                            chain, 1)
                        dve.wait_ge(chain, 3 * k + 3)
                        nc.vector.scalar_tensor_tensor(hl[:, :], hl[:, :], 1.0, hg[:, :], ALU.add, ALU.mult).then_inc(
                            act_ok, 1)
                        dve.wait_ge(cmb_done, 3 * k + 2)
                        add(1)
                        dve.wait_ge(xt_done, k + 2)
                        turned_x()
                        dve.wait_ge(cmb_done, 3 * k + 3)
                        add(2)
                        dve.wait_ge(gt_done, k + 1)
                        nc.vector.tensor_copy(gT[:, :, :].rearrange("p i t -> p (i t)")[:, 0:T], ps[:, 3, 0:T]).then_inc(gt_ok, 1)
                        e1 = bass.ds(dve.value_load(tab[0:1, bass.ds(k + 1, 1)], min_val=0, max_val=NE - 1), 1)
                        offset(0, e1, bass.ds(k + 1, 1), 3 * k + 4)
                        weigh(e1)
                        e2 = bass.ds(dve.value_load(tab[0:1, bass.ds(k + 2, 1)], min_val=0, max_val=NE - 1), 1)
                        offset(1, e2, bass.ds(k + 2, 1), 3 * k + 5)
                        select()
                for i in range(3):
                    dve.wait_ge(cmb_done, 6 * pairs + i + 1)
                    add(i)
    final_norm(nc, a, out, sb, ps, x, stat, eps)


def route(nc, a, outer, sb, ps, ident, ones, x, g8, stat, eps, norm_stage, h_tm, code, gate, tab, base, iota, gfx,
          pick, load_first):
    with ExitStack() as st:
        sem = semaphores(nc, st, "rt")
        hT = sb(st, "ehT", [P, KC, T])
        rw = sb(st, "rw", [P, KC, NE])
        rb = sb(st, "rb", [P, NE])
        b2 = sb(st, "b2", [NE, D])
        lg = sb(st, "lg", [P, 3, NE])
        mask = sb(st, "mask", [P, 3, NE])
        onei = sb(st, "onei", [P, NE])
        top = sb(st, "top", [P, 3, 8])
        idx = sb(st, "idx", [P, 3, 8], mybir.dt.uint32)
        idf = sb(st, "idf", [P, 3, 8])
        sm = sb(st, "sm", [P, 3, 2])
        stri = sb(st, "estri", [P, P])
        gateT = sb(st, "gateT", [NE, T])
        mrep = sb(st, "mrep", [P, 3, 4, NE])
        q = sb(st, "q", [P, 8])
        hit = sb(st, "hit", [P, 3, NE])
        Q_E, Q_OFF, Q_OVER, Q_POS = range(4)
        loaded, made, summed, moved, ex, turned = (sem(n) for n in ("in", "made", "sum", "moved", "exp", "turned"))
        pool_c, d = Count(sem("pool")), Count(sem("dve"))
        with nc.Block() as block:
            @block.sync
            def _(sp):
                sp.dma_start(rw[:, :, :], a["router_w"][0].rearrange("(p c) e -> p c e", c=KC)).then_inc(loaded, 16)
                sp.dma_start(rb[:, :], a["router_b"][0].partition_broadcast(P)).then_inc(loaded, 16)
                sp.dma_start(b2[:, :], a["b2_e"][0]).then_inc(loaded, 16)
                sp.dma_start(gfx[:, :, :], a["norm_ffn"][0].rearrange("(h p c) -> p h c", h=2, c=HK)).then_inc(loaded, 16)
                load_first(sp)
                sp.wait_ge(loaded, 64)

            @block.gpsimd
            def _(pool):
                def step(ins):
                    pool_c.step(pool, ins)
                step(nc.gpsimd.iota(iota[:, :], [[1, CAP]], 0, 0, allow_small_or_imprecise_dtypes=True))
                step(nc.gpsimd.memset(stri[:, :], 1.0))
                step(nc.gpsimd.affine_select(stri[:], stri[:], [[1, P]], ALU.is_ge, 0.0, -1, -1))
                step(nc.gpsimd.memset(pick[:, :, :], 1.0))
                step(nc.gpsimd.affine_select(pick[:, :, :], pick[:, :, :], [[-1, 4], [0, CAP]], ALU.is_equal, 0.0, 0, 1))
                step(nc.gpsimd.iota(hit[:, 0, 0:4], [[-NE, 4]], 0, 1, allow_small_or_imprecise_dtypes=True))

        norm_stage("ffn", x, TILES, 3, hT, h_tm)
        with nc.Block() as block:
            @block.tensor
            def _(pe):
                for i, (t0, n) in enumerate(TILES):
                    for c in range(KC):
                        ins = nc.tensor.matmul(ps[:n, i, 0:NE], hT[:, c, t0:t0 + n], rw[:, c, :], start=(c == 0),
                                               stop=(c == KC - 1))
                    ins.then_inc(summed, 1)
                pe.wait_ge(made, 1)
                for i, (t0, n) in enumerate(TILES):
                    for j in range(i + 1):
                        m = TILES[j][1]
                        lhs = ones[:m, :n] if j < i else stri[:n, :n]
                        ins = nc.tensor.matmul(ps[:n, 3 + i, 0:NE], lhs, mask[:m, j, :], start=(j == 0), stop=(j == i))
                for j in range(3):
                    m = TILES[j][1]
                    ins = nc.tensor.matmul(ps[:, 6, 0:1], mrep[:m, j].rearrange("p b e -> p (b e)"), ones[:m, 0:1],
                                           start=(j == 0), stop=(j == 2))
                for j, (t0, n) in enumerate(TILES):
                    ins = nc.tensor.transpose(ps[:NE, 7, t0:t0 + n], gate[:n, j, :], ident[:n, :n])
                ins.then_inc(turned, 1)
                pe.wait_ge(made, 2)
                nc.tensor.matmul(ps[:, 0, 0:1], stri[:], q[:, Q_OVER:Q_OVER + 1], start=True, stop=True)
                nc.tensor.matmul(ps[:, 0, 1:2], ones[:], q[:, Q_OVER:Q_OVER + 1], start=True, stop=True).then_inc(
                    turned, 1)
                pe.wait_ge(made, 3)
                nc.tensor.matmul(ps[:, 1, 0:2 * NE], ones[:], hit[:, 1:3, :].rearrange("p j m -> p (j m)"), start=True,
                                 stop=True).then_inc(turned, 1)
                for i, (t0, n) in enumerate(TILES):
                    for half in range(2):
                        ins = nc.tensor.matmul(ps[:n, 2 + 2 * i + half, :], gateT[:, t0:t0 + n],
                                               b2[:, 512 * half:512 * half + 512], start=True, stop=True)
                    ins.then_inc(turned, 1)

            @block.scalar
            def _(act):
                for i, (_, n) in enumerate(TILES):
                    act.wait_ge(moved, i + 1)
                    nc.scalar.activation(top[:n, i, 4:8], top[:n, i, 0:4], ACT.Exp, bias=sm[:n, i, 0:1],
                                         accum_out=sm[:n, i, 1:2]).then_inc(ex, 1)

            @block.vector
            def _(dve):
                d.step(dve, nc.vector.tensor_scalar(hit[:, 1, 0:4], hit[:, 0, 0:4], 0.0, None, ALU.is_ge))
                d.step(dve, nc.vector.tensor_reduce(q[:, Q_OFF:Q_OFF + 1], hit[:, 1, 0:4], AXX, ALU.add))
                d.step(dve, nc.vector.scalar_tensor_tensor(q[:, Q_E:Q_E + 1], q[:, Q_OFF:Q_OFF + 1], -float(NE),
                                                           hit[:, 0, 0:1], ALU.mult, ALU.add))
                d.step(dve, nc.vector.tensor_scalar(q[:, Q_E:Q_E + 1], q[:, Q_E:Q_E + 1], float(NE), None, ALU.add))
                nc.vector.tensor_scalar(q[:, Q_OFF:Q_OFF + 1], q[:, Q_OFF:Q_OFF + 1], float(CAP), None, ALU.mult)
                for i, (_, n) in enumerate(TILES):
                    dve.wait_ge(summed, i + 1)
                    d.step(dve, nc.vector.tensor_tensor(lg[:n, i, :], ps[:n, i, 0:NE], rb[:n, :], ALU.add))
                    d.step(dve, nc.vector.max(top[:n, i, :], lg[:n, i, :]))
                    d.step(dve, nc.vector.max_index(idx[:n, i, :], top[:n, i, :], lg[:n, i, :]))
                    nc.vector.tensor_copy(idf[:n, i, :], idx[:n, i, :])
                    nc.vector.tensor_scalar(sm[:n, i, 0:1], top[:n, i, 0:1], -1.0, None, ALU.mult).then_inc(moved, 1)
                dve.wait_ge(moved, 3)
                for i, (_, n) in enumerate(TILES):
                    dve.wait_ge(ex, i + 1)
                    d.step(dve, nc.vector.reciprocal(sm[:n, i, 1:2], sm[:n, i, 1:2]))
                    d.step(dve, nc.vector.tensor_scalar(top[:n, i, 4:8], top[:n, i, 4:8], sm[:n, i, 1:2], None,
                                                        ALU.mult))
                    for j in range(TOPK):
                        one = mask[:n, i, :] if j == 0 else onei[:n, :]
                        d.step(dve, nc.vector.tensor_scalar(one, iota[:n, 0:NE], idf[:n, i, j:j + 1], None,
                                                            ALU.is_equal))
                        g = top[:n, i, 4 + j:5 + j]
                        if j == 0:
                            ins = nc.vector.tensor_scalar(gate[:n, i, :], one, g, None, ALU.mult)
                        else:
                            nc.vector.tensor_tensor(mask[:n, i, :], mask[:n, i, :], one, ALU.add)
                            ins = nc.vector.scalar_tensor_tensor(gate[:n, i, :], one, g, gate[:n, i, :], ALU.mult,
                                                                 ALU.add)
                        d.step(dve, ins)
                    ins = nc.vector.tensor_copy(mrep[:n, i], over(mask[:n, i, :], 4))
                ins.then_inc(made, 1)
                dve.wait_ge(turned, 1)
                d.step(dve, nc.vector.memset(code[:, :, :], -1.0))
                for i, (_, n) in enumerate(TILES):
                    ins = nc.vector.scalar_tensor_tensor(code[:n, i, :], ps[:n, 3 + i, 0:NE], 1.0, mask[:n, i, :],
                                                         ALU.add, ALU.mult)
                d.step(dve, ins)
                for i, (_, n) in enumerate(TILES):
                    nc.vector.tensor_scalar(code[:n, i, :], code[:n, i, :], 1.0, None, ALU.subtract)
                nc.vector.tensor_copy(gateT[:, :], ps[:NE, 7, 0:T])
                nc.vector.tensor_tensor(q[:, Q_OVER:Q_OVER + 1], ps[:, 6, 0:1], q[:, Q_OFF:Q_OFF + 1],
                                        ALU.is_gt).then_inc(made, 1)
                dve.wait_ge(turned, 2)
                nc.vector.tensor_copy(q[:, Q_POS:Q_POS + 2], ps[:, 0, 0:2])
                d.step(dve, nc.vector.tensor_scalar(q[:, 6:7], q[:, Q_OVER:Q_OVER + 1], -1.0, -1000.0, ALU.add,
                                                    ALU.mult))
                d.step(dve, nc.vector.tensor_tensor(q[:, Q_POS:Q_POS + 1], q[:, Q_POS:Q_POS + 1], q[:, 6:7], ALU.add))
                d.step(dve, nc.vector.tensor_scalar(hit[:, 0, :], iota[:, 0:NE], q[:, Q_POS:Q_POS + 1], None,
                                                    ALU.is_equal))
                nc.vector.tensor_scalar(q[:, 5:6], q[:, Q_OFF:Q_OFF + 1], 5.0 * CAP, None, ALU.subtract)
                nc.vector.tensor_scalar(hit[:, 1, :], hit[:, 0, :], q[:, Q_E:Q_E + 1], None, ALU.mult)
                d.step(dve, nc.vector.memset(base[:, 0:NE], 0.0))
                nc.vector.tensor_scalar(hit[:, 2, :], hit[:, 0, :], q[:, 5:6], None, ALU.mult).then_inc(made, 1)
                d.step(dve, nc.vector.tensor_scalar(q[:, 7:8], q[:, Q_POS + 1:Q_POS + 2], 0.5, NE / 2 + 0.25, ALU.mult,
                                                    ALU.add))
                nc.vector.tensor_copy(tab[0:1, LIST + 1:LIST + 2], q[0:1, 7:8])
                nc.vector.tensor_scalar(tab[0:1, LIST:LIST + 1], q[0:1, 7:8], 1.0, None, ALU.subtract)
                dve.wait_ge(turned, 3)
                nc.vector.tensor_copy(tab[0:1, 0:NE], iota[0:1, 0:NE])
                nc.vector.tensor_copy(tab[0:1, NE:LIST], ps[0:1, 1, 0:NE])
                nc.vector.tensor_scalar(base[:, NE:LIST], ps[:, 1, NE:2 * NE], 5.0 * CAP, None, ALU.add)
                for i, (_, n) in enumerate(TILES):
                    dve.wait_ge(turned, 4 + i)
                    v = x[:n, i, :].rearrange("p (h d) -> p h d", h=2)
                    nc.vector.tensor_tensor(v, v, ps[:n, 2 + 2 * i:4 + 2 * i, :], ALU.add)


def final_norm(nc, a, out, sb, ps, x, stat, eps):
    with ExitStack() as st:
        sem = semaphores(nc, st, "fn")
        gf = sb(st, "gf", [P, D])
        y = sb(st, "fy", [P, 3, D])
        loaded, sq, root, done, stored = (sem(n) for n in ("in", "sq", "root", "done", "stored"))
        d = Count(sem("dve"))
        with nc.Block() as block:
            @block.sync
            def _(sp):
                sp.dma_start(gf[:, :], a["final_norm"].partition_broadcast(P)).then_inc(loaded, 16)
                for i in range(2):
                    sp.wait_ge(done, i + 1)
                    sp.dma_start(out[0][0].rearrange("(i p) d -> i p d", p=P)[i], y[:, i, :]).then_inc(stored, 16)
                sp.wait_ge(done, 3)
                sp.dma_start(out[1].rearrange("b t d -> (b t) d"), y[:NS, 2, :]).then_inc(stored, 16)
                sp.wait_ge(stored, 48)

            @block.scalar
            def _(act):
                for i, (_, n) in enumerate(TILES):
                    nc.scalar.activation(y[:n, i, :], x[:n, i, :], ACT.Square, accum_out=stat[:n, i, 0:1]).then_inc(
                        sq, 1)
                for i, (_, n) in enumerate(TILES):
                    act.wait_ge(sq, i + 1)
                    nc.scalar.activation(stat[:n, i, 1:2], stat[:n, i, 0:1], ACT.Sqrt, bias=eps[:n, 0:1],
                                         scale=1.0 / D).then_inc(root, 1)

            @block.vector
            def _(dve):
                dve.wait_ge(loaded, 16)
                for i, (_, n) in enumerate(TILES):
                    dve.wait_ge(root, i + 1)
                    d.step(dve, nc.vector.reciprocal(stat[:n, i, 2:3], stat[:n, i, 1:2]))
                    nc.vector.scalar_tensor_tensor(y[:n, i, :], x[:n, i, :], stat[:n, i, 2:3], gf[:n, :], ALU.mult,
                                                   ALU.mult).then_inc(done, 1)


_INS = ['x_prompt', 'x_sample', 'mem_prompt', 'state_rwkv', 'state_rwkv_shift', 'state_gdn', 'state_gdn_conv',
        'cache_mem_k', 'cache_mem_v', 'norm_mix', 'w_in', 'mu_shift', 'w0', 'w2_decay', 'a0', 'a2_iclr', 'g2_gate',
        'k_k', 'k_a', 'r_k', 'lnx_w', 'lnx_b', 'conv_w', 'a_log', 'dt_bias', 'gdn_norm_w', 'w_out',
        'norm_cross', 'norm_mem', 'wq_x', 'wk_x', 'wv_x', 'wo_x',
        'norm_ffn', 'router_w', 'router_b', 'w1_e', 'b1_e', 'w2_e', 'b2_e', 'final_norm']
_OUTS = [(1, TP, D), (NB, TS, D),
         (1, 1, HR, NR, NR), (1, 1, R_PROJ), (1, 1, HG, DG, DG), (1, 1, CW - 1, CONV),
         (1, 1, NM, HX, DX), (1, 1, NM, HX, DX),
         (1, NB, HR, NR, NR), (1, NB, R_PROJ), (1, NB, HG, DG, DG), (1, NB, CW - 1, CONV)]


def kernel(**inputs):
    import numpy as _np
    import concourse.bacc as _bacc
    from concourse import mybir as _mybir
    from concourse.bass_utils import run_bass_kernel_spmd as _run

    nc = _bacc.Bacc("TRN2", target_bir_lowering=False, num_devices=1)
    arrays, ins, outs = {}, {}, []
    for name in _INS:
        arr = _np.ascontiguousarray(inputs[name])
        arrays[f"in_{name}_dram"] = arr
        ins[name] = nc.dram_tensor(f"in_{name}_dram", arr.shape, _mybir.dt.from_np(arr.dtype),
                                   kind="ExternalInput").ap()
    for i, shape in enumerate(_OUTS):
        outs.append(nc.dram_tensor(f"out_{i}_dram", shape, _mybir.dt.float32, kind="ExternalOutput").ap())
    build(nc, ins, outs)
    r = _run(nc, [arrays], core_ids=[0])
    return tuple(r.results[0][f"out_{i}_dram"] for i in range(len(_OUTS)))
```
